# Optimizing a Trainium2 kernel written in Bass

```python
import jax
import jax.numpy as jnp
from jax import lax
import numpy as np

D_MODEL = 1024
BATCH = 1
SEQ = 512
DEPTH = 2

GRID_W = 64
CTX_LEN = 256
HEAD_DIM = 64
ROPE_THETA = 10000.0
Q_BLOCK = 128
EPS = 1e-6

GLA_HEADS = 4
GLA_DK = 32
GLA_DV = 64
GLA_WIDTH = GLA_HEADS * GLA_DV
GLA_GATE_RANK = 16
GLA_GATE_NORM = 16.0
GLA_CHUNK = 64

MLA_HEADS = 6
MLA_NOPE = 64
MLA_ROPE = 32
MLA_V = 64
MLA_Q_LORA = 256
MLA_KV_LORA = 256
MLA_WIDTH = MLA_HEADS * MLA_V

GQA_HEADS = 6
GQA_KV_HEADS = 2
GQA_GROUP = GQA_HEADS // GQA_KV_HEADS
GQA_WIDTH = GQA_HEADS * HEAD_DIM

D_MIX = GLA_WIDTH + MLA_WIDTH + GQA_WIDTH
GLA_COLS = (GLA_HEADS * GLA_DK, GLA_HEADS * GLA_DK, GLA_WIDTH, GLA_WIDTH, 2 * GLA_GATE_RANK)
MLA_COLS = (MLA_Q_LORA, MLA_KV_LORA, MLA_ROPE, MLA_WIDTH)
GQA_COLS = (GQA_HEADS * HEAD_DIM, GQA_KV_HEADS * HEAD_DIM, GQA_KV_HEADS * HEAD_DIM, GQA_WIDTH)
IN_COLS = GLA_COLS + MLA_COLS + GQA_COLS
D_IN = sum(IN_COLS)

kernel_name = 'hybrid_gla_mla_gqa_diffusion_trunk'

def rms_norm(x, w):
    xf = x.astype(jnp.float32)
    y = xf * lax.rsqrt(jnp.mean(xf * xf, axis=-1, keepdims=True) + EPS)
    return (y * w.astype(jnp.float32)).astype(x.dtype)

def split_cols(u, sizes):
    idx = [int(i) for i in np.cumsum(sizes)[:-1]]
    return jnp.split(u, idx, axis=-1)

def rope_2d_tables(rows, d_rot):
    quarter = d_rot // 4
    row = jnp.repeat(jnp.arange(rows), GRID_W).astype(jnp.float32)
    col = jnp.tile(jnp.arange(GRID_W), rows).astype(jnp.float32)
    freqs = ROPE_THETA ** (-jnp.arange(quarter, dtype=jnp.float32) / quarter)
    ang = jnp.stack([row[:, None] * freqs, col[:, None] * freqs], axis=1)
    return jnp.cos(ang), jnp.sin(ang)

def apply_rope_2d(x, cos, sin):
    n, d = x.shape[1], x.shape[-1]
    q = d // 4
    xr = x.astype(jnp.float32).reshape(x.shape[:-1] + (2, 2, q))
    shape = (1, n) + (1,) * (x.ndim - 3) + (2, q)
    cos = cos.reshape(shape)
    sin = sin.reshape(shape)
    x1, x2 = xr[..., 0, :], xr[..., 1, :]
    out = jnp.stack([x1 * cos - x2 * sin, x2 * cos + x1 * sin], axis=-2)
    return out.reshape(x.shape).astype(x.dtype)

def attend(q, keys, vals, scale):
    s = jnp.einsum('bqhgd,bkhd->bhgqk', q, keys) * scale
    p = jax.nn.softmax(s.astype(jnp.float32), axis=-1).astype(vals.dtype)
    return jnp.einsum('bhgqk,bkhe->bqhge', p, vals)

def latent_attention(q, k, v, k_c, v_c, scale):
    keys = jnp.concatenate([k_c, k], axis=1)
    vals = jnp.concatenate([v_c, v], axis=1)
    b, n, hk, g, dq = q.shape
    nb = n // Q_BLOCK
    qb = jnp.moveaxis(q.reshape(b, nb, Q_BLOCK, hk, g, dq), 1, 0)
    o = lax.map(lambda qblk: attend(qblk, keys, vals, scale), qb)
    return jnp.moveaxis(o, 0, 1).reshape(b, n, hk, g, vals.shape[-1])

def gla_chunk_states(k, v, g, s0):
    bsz, t, h, dk = k.shape
    nc = t // GLA_CHUNK
    kc = k.reshape(bsz, nc, GLA_CHUNK, h, dk).astype(jnp.float32)
    vc = v.reshape(bsz, nc, GLA_CHUNK, h, v.shape[-1]).astype(jnp.float32)
    cum = jnp.cumsum(g.reshape(bsz, nc, GLA_CHUNK, h, dk), axis=2)
    last = cum[:, :, -1]
    ds = jnp.einsum('bnchk,bnchv->bnhkv', kc * jnp.exp(last[:, :, None] - cum), vc)

    def step(s, inp):
        decay, d = inp
        return jnp.exp(decay)[..., None] * s + d, s

    s_final, s_prev = lax.scan(step, s0, (jnp.moveaxis(last, 1, 0), jnp.moveaxis(ds, 1, 0)))
    return cum, jnp.moveaxis(s_prev, 0, 1), s_final

def gla_chunk_outputs(q, k, v, cum, s_prev):
    bsz, t, h, dk = q.shape
    dv = v.shape[-1]
    nc = t // GLA_CHUNK
    qc = q.reshape(bsz, nc, GLA_CHUNK, h, dk).astype(jnp.float32)
    kc = k.reshape(bsz, nc, GLA_CHUNK, h, dk).astype(jnp.float32)
    vc = v.reshape(bsz, nc, GLA_CHUNK, h, dv).astype(jnp.float32)
    q_dec = qc * jnp.exp(cum)
    k_inv = kc * jnp.exp(-cum)
    o_inter = jnp.einsum('bnchk,bnhkv->bnchv', q_dec, s_prev)
    a = jnp.einsum('bnihk,bnjhk->bnhij', q_dec, k_inv)
    mask = jnp.tril(jnp.ones((GLA_CHUNK, GLA_CHUNK), dtype=bool))
    a = jnp.where(mask, a, 0.0)
    o_intra = jnp.einsum('bnhij,bnjhv->bnihv', a, vc)
    return (o_inter + o_intra).reshape(bsz, t, h, dv).astype(v.dtype)

def gla_direction(lat, cx, want_ctx):
    q, k, v, g = lat
    qc, kc, vc, gc = cx
    s0 = jnp.zeros((kc.shape[0], GLA_HEADS, GLA_DK, GLA_DV), jnp.float32)
    cum_c, sp_c, sf_c = gla_chunk_states(kc, vc, gc, s0)
    cum, sp, _ = gla_chunk_states(k, v, g, sf_c)
    o = gla_chunk_outputs(q, k, v, cum, sp)
    oc = gla_chunk_outputs(qc, kc, vc, cum_c, sp_c) if want_ctx else None
    return o, oc

def gla_inputs(parts, w_a_f, b_a_f, w_a_b, b_a_b):
    q, k, v, _, a = parts
    bsz, t = q.shape[:2]
    hk = (bsz, t, GLA_HEADS, GLA_DK)
    q = q.reshape(hk) * GLA_DK ** -0.5
    k = k.reshape(hk)
    v = v.reshape(bsz, t, GLA_HEADS, GLA_DV)
    a_f, a_b = jnp.split(a, 2, axis=-1)
    g_f = (jax.nn.log_sigmoid((a_f @ w_a_f + b_a_f).astype(jnp.float32)) / GLA_GATE_NORM).reshape(hk)
    g_b = (jax.nn.log_sigmoid((a_b @ w_a_b + b_a_b).astype(jnp.float32)) / GLA_GATE_NORM).reshape(hk)
    return (q, k, v, g_f), (q, k, v, g_b)

def flip_t(ts):
    return tuple(jnp.flip(t, axis=1) for t in ts)

def gla_branch(parts, parts_c, w_a_f, b_a_f, w_a_b, b_a_b, norm_w, want_ctx):
    lat_f, lat_b = gla_inputs(parts, w_a_f, b_a_f, w_a_b, b_a_b)
    cx_f, cx_b = gla_inputs(parts_c, w_a_f, b_a_f, w_a_b, b_a_b)
    o_f, oc_f = gla_direction(lat_f, cx_f, want_ctx)
    o_b, oc_b = gla_direction(flip_t(lat_b), flip_t(cx_b), want_ctx)

    def finish(o_fwd, o_bwd, z):
        o = rms_norm(o_fwd + jnp.flip(o_bwd, axis=1), norm_w)
        return o.reshape(z.shape) * jax.nn.silu(z)

    y = finish(o_f, o_b, parts[3])
    yc = finish(oc_f, oc_b, parts_c[3]) if want_ctx else None
    return y, yc

def mla_project(parts, q_norm_w, w_uq, kv_norm_w, w_ukv, cos, sin, rotate):
    cq, ckv, kr, _ = parts
    bsz, t = cq.shape[:2]
    q = (rms_norm(cq, q_norm_w) @ w_uq).reshape(bsz, t, MLA_HEADS, MLA_NOPE + MLA_ROPE)
    kv = (rms_norm(ckv, kv_norm_w) @ w_ukv).reshape(bsz, t, MLA_HEADS, MLA_NOPE + MLA_V)
    q_nope, q_rope = q[..., :MLA_NOPE], q[..., MLA_NOPE:]
    k_nope, v = kv[..., :MLA_NOPE], kv[..., MLA_NOPE:]
    k_rope = kr[:, :, None, :]
    if rotate:
        q_rope = apply_rope_2d(q_rope, cos, sin)
        k_rope = apply_rope_2d(k_rope, cos, sin)
    q = jnp.concatenate([q_nope, q_rope], axis=-1)
    k = jnp.concatenate([k_nope, jnp.broadcast_to(k_rope, (bsz, t, MLA_HEADS, MLA_ROPE))], axis=-1)
    return q, k, v

def mla_branch(parts, parts_c, q_norm_w, w_uq, kv_norm_w, w_ukv, cos, sin, want_ctx):
    scale = (MLA_NOPE + MLA_ROPE) ** -0.5
    q, k, v = mla_project(parts, q_norm_w, w_uq, kv_norm_w, w_ukv, cos, sin, True)
    qc, kc, vc = mla_project(parts_c, q_norm_w, w_uq, kv_norm_w, w_ukv, None, None, False)
    z, zc = parts[3], parts_c[3]
    y = latent_attention(q[:, :, :, None], k, v, kc, vc, scale).reshape(z.shape) * jax.nn.silu(z)
    yc = attend(qc[:, :, :, None], kc, vc, scale).reshape(zc.shape) * jax.nn.silu(zc) if want_ctx else None
    return y, yc

def gqa_project(parts, q_norm_w, k_norm_w, cos, sin, rotate):
    q, k, v, _ = parts
    bsz, t = q.shape[:2]
    q = rms_norm(q.reshape(bsz, t, GQA_HEADS, HEAD_DIM), q_norm_w)
    k = rms_norm(k.reshape(bsz, t, GQA_KV_HEADS, HEAD_DIM), k_norm_w)
    v = v.reshape(bsz, t, GQA_KV_HEADS, HEAD_DIM)
    if rotate:
        q = apply_rope_2d(q, cos, sin)
        k = apply_rope_2d(k, cos, sin)
    return q.reshape(bsz, t, GQA_KV_HEADS, GQA_GROUP, HEAD_DIM), k, v

def gqa_branch(parts, parts_c, q_norm_w, k_norm_w, cos, sin, want_ctx):
    scale = HEAD_DIM ** -0.5
    q, k, v = gqa_project(parts, q_norm_w, k_norm_w, cos, sin, True)
    qc, kc, vc = gqa_project(parts_c, q_norm_w, k_norm_w, None, None, False)
    z, zc = parts[3], parts_c[3]
    y = latent_attention(q, k, v, kc, vc, scale).reshape(z.shape) * jax.nn.silu(z)
    yc = attend(qc, kc, vc, scale).reshape(zc.shape) * jax.nn.silu(zc) if want_ctx else None
    return y, yc

def setup_inputs(seed: int = 0) -> dict:
    key = jax.random.key(seed)
    ks = jax.random.split(key, 24)
    f32 = jnp.float32
    L = DEPTH

    def nrm(k, shape, s):
        return jax.random.normal(k, shape, f32) * s

    def gain(k, shape):
        return 1.0 + 0.02 * jax.random.normal(k, shape, f32)

    return {
        'x': nrm(ks[0], (BATCH, SEQ, D_MODEL), 1.0),
        'c': nrm(ks[1], (BATCH, D_MODEL), 1.0),
        'ctx': nrm(ks[2], (BATCH, CTX_LEN, D_MODEL), 1.0),
        'c_ctx': nrm(ks[3], (D_MODEL,), 1.0),
        'norm_w': gain(ks[4], (L, D_MODEL)),
        'w_mod': nrm(ks[5], (L, D_MODEL, 3 * D_MODEL), D_MODEL ** -0.5),
        'b_mod': nrm(ks[6], (L, 3 * D_MODEL), 0.01),
        'w_in': nrm(ks[7], (L, D_MODEL, D_IN), D_MODEL ** -0.5),
        'gla_w_a_fwd': nrm(ks[8], (L, GLA_GATE_RANK, GLA_HEADS * GLA_DK), GLA_GATE_RANK ** -0.5),
        'gla_b_a_fwd': nrm(ks[9], (L, GLA_HEADS * GLA_DK), 0.1),
        'gla_w_a_bwd': nrm(ks[10], (L, GLA_GATE_RANK, GLA_HEADS * GLA_DK), GLA_GATE_RANK ** -0.5),
        'gla_b_a_bwd': nrm(ks[11], (L, GLA_HEADS * GLA_DK), 0.1),
        'gla_norm_w': gain(ks[12], (L, GLA_DV)),
        'mla_q_norm_w': gain(ks[13], (L, MLA_Q_LORA)),
        'mla_w_uq': nrm(ks[14], (L, MLA_Q_LORA, MLA_HEADS * (MLA_NOPE + MLA_ROPE)), MLA_Q_LORA ** -0.5),
        'mla_kv_norm_w': gain(ks[15], (L, MLA_KV_LORA)),
        'mla_w_ukv': nrm(ks[16], (L, MLA_KV_LORA, MLA_HEADS * (MLA_NOPE + MLA_V)), MLA_KV_LORA ** -0.5),
        'gqa_q_norm_w': gain(ks[17], (L, HEAD_DIM)),
        'gqa_k_norm_w': gain(ks[18], (L, HEAD_DIM)),
        'w_out': nrm(ks[19], (L, D_MIX, D_MODEL), D_MIX ** -0.5),
        'final_norm_w': gain(ks[20], (D_MODEL,)),
    }

def reference(x, c, ctx, c_ctx, norm_w, w_mod, b_mod, w_in, gla_w_a_fwd, gla_b_a_fwd, gla_w_a_bwd,
              gla_b_a_bwd, gla_norm_w, mla_q_norm_w, mla_w_uq, mla_kv_norm_w, mla_w_ukv,
              gqa_q_norm_w, gqa_k_norm_w, w_out, final_norm_w):
    n = x.shape[1]
    rows = n // GRID_W
    cos_m, sin_m = rope_2d_tables(rows, MLA_ROPE)
    cos_g, sin_g = rope_2d_tables(rows, HEAD_DIM)
    n_a = len(GLA_COLS)
    n_b = n_a + len(MLA_COLS)
    for l in range(DEPTH):
        want_ctx = l < DEPTH - 1
        shift, scale, gate = jnp.split(jax.nn.silu(c) @ w_mod[l] + b_mod[l], 3, axis=-1)
        shift_c, scale_c, gate_c = jnp.split(jax.nn.silu(c_ctx) @ w_mod[l] + b_mod[l], 3, axis=-1)
        h = rms_norm(x, norm_w[l]) * (1.0 + scale[:, None, :]) + shift[:, None, :]
        hc = rms_norm(ctx, norm_w[l]) * (1.0 + scale_c) + shift_c
        u = split_cols(h @ w_in[l], IN_COLS)
        uc = split_cols(hc @ w_in[l], IN_COLS)
        y_a, yc_a = gla_branch(u[:n_a], uc[:n_a], gla_w_a_fwd[l], gla_b_a_fwd[l], gla_w_a_bwd[l],
                               gla_b_a_bwd[l], gla_norm_w[l], want_ctx)
        y_b, yc_b = mla_branch(u[n_a:n_b], uc[n_a:n_b], mla_q_norm_w[l], mla_w_uq[l], mla_kv_norm_w[l],
                               mla_w_ukv[l], cos_m, sin_m, want_ctx)
        y_c, yc_c = gqa_branch(u[n_b:], uc[n_b:], gqa_q_norm_w[l], gqa_k_norm_w[l], cos_g, sin_g, want_ctx)
        x = x + gate[:, None, :] * (jnp.concatenate([y_a, y_b, y_c], axis=-1) @ w_out[l])
        if want_ctx:
            ctx = ctx + gate_c * (jnp.concatenate([yc_a, yc_b, yc_c], axis=-1) @ w_out[l])
    return rms_norm(x, final_norm_w)


_drawn_inputs = setup_inputs


def setup_inputs(seed=0):
    import zlib

    import numpy as np

    out = dict(_drawn_inputs(seed))
    spreads = {}
    factors = {'norm_w': 4.242,
     'b_mod': 3.903,
     'gla_b_a_fwd': 3.726,
     'gla_b_a_bwd': 4.498,
     'gla_norm_w': 8.0,
     'mla_q_norm_w': 8.0,
     'mla_kv_norm_w': 8.0,
     'gqa_q_norm_w': 8.0,
     'gqa_k_norm_w': 8.0,
     'final_norm_w': 2.947}
    for name, (base, spread) in spreads.items():
        noise = np.random.default_rng([zlib.crc32(name.encode()), seed]).standard_normal(out[name].shape)
        drawn = base * np.exp(spread * noise) if base else spread * noise
        out[name] = jnp.asarray(drawn.astype(out[name].dtype))
    for name, factor in factors.items():
        out[name] = (out[name] * factor).astype(out[name].dtype)
    return out
```

```python
from contextlib import ExitStack

import numpy as np

import concourse.bass as bass
from concourse import mybir

ALU = mybir.AluOpType
ACT = mybir.ActivationFunctionType
F32 = mybir.dt.float32
F32R = mybir.dt.float32r
BF16 = mybir.dt.bfloat16
I32 = mybir.dt.int32
AX = mybir.AxisListType.X

P = 128
DEPTH = 2
D = 1024
KD = D // P
NC_TOK, NL_TOK = 256, 512
T = NC_TOK + NL_TOK
TILES = T // P
CTX, LAT = (0, NC_TOK), (NC_TOK, NL_TOK)
EPS = 1e-6
GLA_H, GLA_DK, GLA_DV, CHUNK, RANK = 4, 32, 64, 64, 16
NCHUNK = T // CHUNK
MLA_H, NOPE, ROPE, LORA = 6, 64, 32, 256
GQA_H, HD = 6, 64
MLA_SCALE = (NOPE + ROPE) ** -0.5
GQA_SCALE = HD ** -0.5

GLA_Q, GLA_K, GLA_V, GLA_Z, GLA_A = 0, 128, 256, 512, 768
MLA_CQ, MLA_CKV, MLA_KR, MLA_Z = 800, 1056, 1312, 1344
GQA_Q, GQA_K, GQA_V, GQA_Z = 1728, 2112, 2240, 2368

V_C, V_CC, V_NORM, V_BMOD, V_MQ, V_MKV, V_GBF, V_GBB, V_GN, V_QN, V_KN, V_ROWS = \
    0, 8, 16, 32, 80, 84, 88, 90, 92, 94, 96, 98

C_ID, C_BLK, C_PERM, C_SEL, C_MF, C_MB, C_COSG, C_SING, C_TABM, C_END = \
    0, 128, 256, 384, 640, 768, 896, 1408, 1920, 2432

SEQ = ["small", "cq0", "ga", "cq1", "ga2", "ckv0", "ckv1", "gq0", "ss0", "gq1", "ss1", "gq2", "gk",
       "gss0", "glaq", "gss1", "glak", "glamul", "gss2", "z0", "gss3", "tok", "z1", "rope0", "rope1",
       "z2", "rope2", "rope3", "z3", "z4", "kdT", "z5", "z6", "z7", "ds"]
IN_BLOCKS = [
    [(1, MLA_CQ, 384)],
    [(0, MLA_CKV + 128, 128), (1, GQA_Q, 384)],
    [(0, GQA_K, 128), (1, GLA_Q, 256), (3, GLA_Z, 128)],
    [(0, GLA_V, 256), (2, GQA_V, 128), (3, GLA_Z + 128, 128)],
    [(0, MLA_Z, 384), (3, GQA_Z, 128)],
    [(0, GQA_Z + 128, 256)],
]
SLOT = {"small": (0, 0), "cq0": (0, 1), "cq1": (0, 2), "ckv0": (0, 3), "ckv1": (1, 0), "gq0": (1, 1),
        "gq1": (1, 2), "gq2": (1, 3), "gk": (2, 0), "glaq": (2, 1), "glak": (2, 2), "z0": (2, 3),
        "tok": (3, 0), "z1": (3, 3), "z2": (4, 0), "z3": (4, 1), "z4": (4, 2), "z5": (4, 3),
        "z6": (5, 0), "z7": (5, 1)}
LAST_OF = ["ckv0", "gq2", "z0", "z1", "z5", "z7"]
RING = 6


def chunks_of(name, layer):
    query = name[0] == "z" or name in ("cq0", "cq1", "gq0", "gq1", "gq2", "glaq", "q")
    return [LAT] if layer == DEPTH - 1 and query else [CTX, LAT]


def out_tiles(layer):
    return list(range(2, TILES)) if layer == DEPTH - 1 else list(range(TILES))


def w_blocks():
    seq = [("mod", 0, b) for b in range(4)]
    for l in range(DEPTH):
        seq += [("in", l, b) for b in range(6)] + [("mod", l, 4), ("mod", l, 5)]
        if l + 1 < DEPTH:
            seq += [("mod", l + 1, b) for b in range(4)]
        seq += [("out", l, b) for b in range(2)]
    return seq


W_SEQ = w_blocks()
W_POS = {b: i for i, b in enumerate(W_SEQ)}


class Tally:

    def __init__(self, before=None):
        self.before = before
        self.sems, self.count, self.mark = {}, {}, {}
        self.order, self.freed = [], {}
        self.pv_order, self.pv_freed = [], {}

    def sem(self, stage):
        if stage not in self.sems:
            self.sems[stage] = self.ctx.enter_context(self.nc.semaphore(stage))
            self.count[stage] = 0
        return self.sems[stage]

    def up(self, stage, *step, by=1):
        s = self.sem(stage)
        self.count[stage] += by
        self.mark[(stage, step)] = self.count[stage]
        return s, by

    def dma(self, stage, *step):
        return self.up(stage, *step, by=16)

    def at(self, stage, *step):
        return self.sem(stage), self.before.mark[(stage, step)] if self.before else 1

    def let_go(self, group, stage, *step):
        self.freed.setdefault(group, []).append((stage, step))

    def bank(self, group):
        return self.before.order.index(group) % RING if self.before else 0


def build(nc, tally, a, out):
    up, dma, at, let_go = tally.up, tally.dma, tally.at, tally.let_go
    with ExitStack() as ctx:
        tally.ctx, tally.nc = ctx, nc

        def sb(name, shape, dt=F32):
            return ctx.enter_context(nc.sbuf_tensor(name, shape, dt))

        banks = [ctx.enter_context(nc.psum_tensor(f"bank{i}", [P, 512], F32)) for i in range(RING)]
        pv_banks = [ctx.enter_context(nc.psum_tensor(f"pv{i}", [P, 512], F32)) for i in range(2)]

        def ps(*group):
            return banks[tally.bank(group)]

        hA = sb("hA", [P, KD * T])
        hT = hA[:].rearrange("p (k t) -> p k t", k=KD)
        qh = [hA[:, i * T:(i + 1) * T] for i in range(2)]
        kh = [hA[:, (2 + i) * T:(3 + i) * T] for i in range(2)]
        prob = [hA[:, 3072 + 512 * i:3584 + 512 * i] for i in range(4)]
        rd, un = hA[:, 5120:5632], hA[:, 5632:6144]
        Ab = [hA[:, 3072 + 512 * d:3584 + 512 * d].rearrange("p (h t) -> p h t", h=4) for d in range(2)]
        qbd = [hA[:, 4096 + 512 * d:4608 + 512 * d].rearrange("p (h t) -> p h t", h=4) for d in range(2)]
        Sbd = [hA[:, 5120 + 512 * d:5632 + 512 * d].rearrange("p (c h v) -> p c h v", c=2, h=4)
               for d in range(2)]
        W = sb("W", [P, 2, KD, 512])
        XA = sb("XA", [P, TILES * D])
        X = XA[:].rearrange("p (t n) -> p t n", t=TILES)
        Ef = [XA[:, d * T:(d + 1) * T] for d in range(2)]
        ki = [XA[:, (2 + d) * T:(3 + d) * T] for d in range(2)]
        qd = [XA[:, (4 + d) * T:(5 + d) * T] for d in range(2)]
        kd = [XA[:, (6 + d) * T:(7 + d) * T] for d in range(2)]
        kdtok = [e.rearrange("p (t c) -> p t c", t=TILES) for e in Ef]
        St = [e.rearrange("p (n v) -> p n v", n=NCHUNK) for e in Ef]
        vm = XA[:, 0:3456].rearrange("p (t r c) -> p t r c", t=TILES, r=3)
        YA = sb("YA", [P, KD * T])
        xn = YA[:].rearrange("p (t n) -> p t n", t=TILES)
        Y = YA[:].rearrange("p (k t) -> p k t", k=KD)
        glaqk = sb("glaqk", [P, 2, T])
        small = sb("small", [P, T])
        cqkv = sb("cqkv", [P, 4, T])
        CQ = cqkv[:].rearrange("p f t -> p (f t)")
        gate = CQ[:, 0:2048].rearrange("p (s n) -> p s n", s=2)
        fnw = CQ[:, 2048:3072]
        gqk = sb("gqk", [P, 4, T])
        glav = sb("glav", [P, TILES, 256])
        vg = sb("vg", [P, TILES, 2, 192])
        wuq = sb("wuq", [P, 2, MLA_H, 128])
        wukv = sb("wukv", [P, 2, MLA_H, 128])
        wa = sb("wa", [32, 2, P])
        sq = sb("sq", [P, 2, 512])
        rs = sb("rs", [P, 512])
        tz = sb("tz", [P, 2, 512])
        rt = sb("rt", [P, 2, 512])
        cumA = sb("cumA", [P, 2 * T])
        cum = [cumA[:, d * T:(d + 1) * T] for d in range(2)]
        brow = cumA[:, 0:1024].rearrange("p (b n) -> p b n", b=2)
        modrow = cumA[:, 1024:1536]
        qr = sb("qr", [96, T], F32R)
        kr = sb("kr", [96, T], F32R)
        con = sb("con", [P, C_END])
        ident, blk, perm = con[:, C_ID:C_ID + P], con[:, C_BLK:C_BLK + P], con[:, C_PERM:C_PERM + P]
        sel = con[:, C_SEL:C_SEL + 256].rearrange("p (s n) -> p s n", s=2)
        mask = [con[:, c:c + P].bitcast(I32) for c in (C_MF, C_MB)]
        cosg, sing, tabm = (con[:, c:c + 512] for c in (C_COSG, C_SING, C_TABM))
        ones = sb("ones", [P, P])
        keep = sb("keep", [P, T], BF16)
        eps = sb("eps", [P, 1])
        vec = rt[0:V_ROWS, 0, 0:P]
        vt = sb("vt", [P, V_ROWS])
        vth = sb("vth", [P, V_ROWS])
        ct = sb("ct", [P, 2, 16])
        sc = sb("sc", [P, KD, 32])
        modc = sb("modc", [P, 16, 2])
        mA = sb("mA", [P, KD, 2])
        mB = sb("mB", [P, KD, 2])
        ssx = sb("ssx", [P, TILES])
        rx = sb("rx", [P, TILES])
        dec = sb("dec", [P, 2, NCHUNK])
        on = sq[:, 0, :].rearrange("p (b c) -> p b c", b=2)
        sqo = sq[:, 1, 0:256]
        ss4 = sb("ss4", [P, 4])
        mxp = sb("mxp", [P, TILES, 2])
        nmx = sb("nmx", [P, 2, TILES])
        x_dram = nc.dram_tensor("x_between_layers", [NL_TOK, D], F32, kind="Internal").ap()

        heads = list(range(MLA_H + GQA_H))

        def qbs(l):
            return ([(0, 256, 256)] if l < DEPTH - 1 else []) + [(256, 512, T)]

        def chunk_order(d):
            nctx = NC_TOK // CHUNK
            if d == 0:
                return list(range(NCHUNK))
            return list(range(nctx - 1, -1, -1)) + list(range(NCHUNK - 1, nctx - 1, -1))

        def lat_of(l):
            return slice(NC_TOK, T) if l == DEPTH - 1 else slice(0, T)

        def pv_index(l, h, q0):
            if l == 0:
                return 2 * h + (q0 > 0)
            return 24 + h

        def pv_owner(i):
            return (0, i // 2, (0, 256)[i % 2]) if i < 24 else (1, i - 24, 256)

        def prob_reader(l, slot):
            per = sum(nk // P for _, _, nk in qbs(l))
            h, u = divmod(slot, per)
            if u == per - 1:
                return "pv_filled", l, h, 256
            if l < DEPTH - 1 and u == 1:
                return "pv_filled", l, h, 0
            return "prob_used", l, slot

        block = ctx.enter_context(nc.Block())

        @block.sync
        def _(sp):
            def rows(r, n, src):
                sp.dma_start(vec[r:r + n, :], src).then_inc(*dma("vec_in"))
            rows(V_C, 8, a["c"][0, :].rearrange("(k p) -> k p", p=P))
            rows(V_CC, 8, a["c_ctx"].rearrange("(k p) -> k p", p=P))
            rows(V_NORM, 16, a["norm_w"].rearrange("l (k p) -> (l k) p", p=P))
            rows(V_BMOD, 48, a["b_mod"].rearrange("l (k p) -> (l k) p", p=P))
            rows(V_MQ, 4, a["mla_q_norm_w"].rearrange("l (k p) -> (l k) p", p=P))
            rows(V_MKV, 4, a["mla_kv_norm_w"].rearrange("l (k p) -> (l k) p", p=P))
            rows(V_GBF, 2, a["gla_b_a_fwd"])
            rows(V_GBB, 2, a["gla_b_a_bwd"])
            for r, name in ((V_GN, "gla_norm_w"), (V_QN, "gqa_q_norm_w"), (V_KN, "gqa_k_norm_w")):
                for half in range(2):
                    sp.dma_start(vec[r:r + 2, half * 64:half * 64 + 64], a[name]).then_inc(*dma("vec_in"))
            sp.dma_start(con[:], a["consts"]).then_inc(*dma("con_in"))

            def block_dma(i):
                kind, l, b = W_SEQ[i]
                if i >= 2:
                    sp.wait_ge(*at("filled", "block", i - 2))
                dst = W[:, i % 2]
                stage = f"w_half{i % 2}"
                if kind == "in":
                    src = a["w_in"][l].rearrange("(k p) n -> p k n", p=P)
                    for s, c, n in IN_BLOCKS[b]:
                        sp.dma_start(dst[:, :, s * P:s * P + n], src[:, :, c:c + n]).then_inc(*dma(stage, i))
                    if b == 0:
                        for o, c in ((0, GLA_A), (32, GLA_A), (64, MLA_KR)):
                            sp.dma_start(dst[:, :, o:o + 32], src[:, :, c:c + 32]).then_inc(*dma(stage, i))
                else:
                    src = a["w_mod" if kind == "mod" else "w_out"][l].rearrange("(k p) n -> p k n", p=P)
                    sp.dma_start(dst, src[:, :, 512 * b:512 * b + 512]).then_inc(*dma(stage, i))

            block_dma(0)
            for t in range(TILES):
                src = a["ctx"][0, t * P:(t + 1) * P, :] if t < 2 else a["x"][0, (t - 2) * P:(t - 1) * P, :]
                sp.dma_start(X[:, t, :], src).then_inc(*dma("x_in", 0))
            block_dma(1)
            for i in range(2, len(W_SEQ)):
                block_dma(i)

        @block.gpsimd
        def _(pool):
            pool.memset(ones[:], 1.0).then_inc(*up("pool_init"))
            pool.memset(eps[:], EPS).then_inc(*up("pool_init"))
            pool.memset(sc[:], 0.0).then_inc(*up("pool_init", "sc"))
            pool.memset(keep[:], 1.0).then_inc(*up("pool_init", "keep1"))
            pool.memset(vg[:, :, :, 64:128], 1.0).then_inc(*up("pool_init"))
            pool.memset(wa[:], 0.0).then_inc(*up("pool_init", "wa"))
            pool.wait_ge(*at("pool_init", "keep1"))
            pool.memset(keep[:, 0:T:CHUNK], 0.0).then_inc(*up("pool_init", "end"))
            for l in range(DEPTH):
                pool.wait_ge(*at("pool_init", "wa"))
                if l:
                    pool.wait_ge(*at("filled", "ga", l - 1, 1, LAT))
                    pool.wait_ge(*at("filled", "kp", l - 1, MLA_H - 1, LAT))
                    pool.wait_ge(*at("filled", "vp", l - 1, TILES - 1))
                pool.dma_start(wa[0:RANK, 0, :], a["gla_w_a_fwd"][l]).then_inc(*dma("wa_in", l))
                pool.dma_start(wa[RANK:2 * RANK, 1, :], a["gla_w_a_bwd"][l]).then_inc(*dma("wa_in", l))
                for f in range(2):
                    pool.dma_start(wuq[:, f, :, 0:96], a["mla_w_uq"][l, f * P:(f + 1) * P, :].rearrange(
                        "p (h c) -> p h c", h=MLA_H)).then_inc(*dma("wu_in", l))
                    pool.dma_start(wukv[:, f, :, :], a["mla_w_ukv"][l, f * P:(f + 1) * P, :].rearrange(
                        "p (h c) -> p h c", h=MLA_H)).then_inc(*dma("wu_in", l))
                i = W_POS[("in", l, 0)]
                pool.wait_ge(*at(f"w_half{i % 2}", i))
                for h in range(2):
                    w = W[:, i % 2, :, 0:P].rearrange("p k (g b s j) -> p k g b s j", g=4, b=2, s=2)
                    pool.tensor_copy(w[:, :, 3, :, 1 - h, :], w[:, :, 2, :, h, :]).then_inc(*up("swap_kr", l))
                pool.wait_ge(*at("wu_in", l))
                for h in range(2):
                    w = wuq[:].rearrange("p f h (g b s j) -> p (f h) g b s j", g=4, b=2, s=2)
                    pool.tensor_copy(w[:, :, 3, :, 1 - h, :], w[:, :, 2, :, h, :]).then_inc(*up("swap_q", l))

                pool.wait_ge(*at("filled", "F", l, "z7", LAT))
                pool.memset(hA[:, 3072:6144], 0.0).then_inc(*up("bd_zero", l))
                pool.wait_ge(*at("bd_zero", l))
                before = None
                for t in out_tiles(l):
                    tok = slice(t * P, (t + 1) * P)
                    for d in range(2):
                        pool.wait_ge(*at("gla_factors", l, d))
                        if before is not None:
                            pool.wait_ge(*at("filled", "A", l, before, d))
                        for h in range(GLA_H):
                            r = slice(32 * h, 32 * h + 32)
                            pool.tensor_copy(qbd[d][r, h, :], qd[d][r, tok]).then_inc(*up("qbd", l, t, d))
                    for d in range(2):
                        pool.wait_ge(*at("state", l, d))
                        if before is not None:
                            pool.wait_ge(*at("filled", "o", l, before))
                        for h in range(GLA_H):
                            r = slice(32 * h, 32 * h + 32)
                            pool.tensor_copy(Sbd[d][r, :, h, :], St[d][r, 2 * t:2 * t + 2, :])\
                                .then_inc(*up("Sbd", l, t, d))
                    before = t
                pool.wait_ge(*at("filled", "o", l, before))
                pool.memset(vm[:, :, :, 64:128], 1.0).then_inc(*up("vm_ones", l))
                pool.wait_ge(*at("kr_rope", l))
                pool.wait_ge(*at("vm_ones", l))
                for b in range(2):
                    if b:
                        pool.wait_ge(*at("kh_rope", l, 0))
                    pool.memset(kh[b][96:97, :], 1.0).then_inc(*up("kh_ones", l, b))
                    pool.wait_ge(*at("kh_ones", l, b))
                    pool.tensor_copy(kh[b][64:96, :], small[64:96, :]).then_inc(*up("kh_rope", l, b))
                for b in range(2):
                    pool.wait_ge(*at("filled", "sc", l, MLA_H - 2 + b, 256, TILES - 1))
                    pool.memset(qh[b][64:96, :], 0.0).then_inc(*up("gqa_zero", l, b))
                    pool.memset(kh[b][64:96, :], 0.0).then_inc(*up("gqa_zero", l, b))
                pool.wait_ge(*at("pv_filled", l, MLA_H - 1, 256))
                pool.wait_ge(*at("vm_ones", l))
                if l == 0:
                    for t in range(TILES):
                        src = a["ctx"][0, t * P:(t + 1) * P, :] if t < 2 else a["x"][0, (t - 2) * P:(t - 1) * P, :]
                        pool.dma_start(X[:, t, :], src).then_inc(*dma("x_back", l))
                else:
                    pool.wait_ge(*at("x_saved", l - 1))
                    for t in range(2, TILES):
                        pool.dma_start(X[:, t, :], x_dram[(t - 2) * P:(t - 1) * P, :]).then_inc(*dma("x_back", l))
                pool.wait_ge(*at("kd_exp", l, 1))
                pool.wait_ge(*at("gqa_zero", l, 1))
                pool.memset(brow, 0.0).then_inc(*up("brow_zero", l))
                pool.wait_ge(*at("brow_zero", l))
                for b in range(2):
                    for s in range(2):
                        pool.dma_start(brow[s:s + 1, b, :], a["b_mod"][l:l + 1, 2048 + 512 * b:2560 + 512 * b])\
                            .then_inc(*dma("brow_in", l))
                if l == DEPTH - 1:
                    pool.dma_start(fnw, a["final_norm_w"].partition_broadcast(P)).then_inc(*dma("fnw_in"))
                if l < DEPTH - 1:
                    for t in range(2, TILES):
                        pool.wait_ge(*at("resid", l, t, 1))
                        pool.dma_start(x_dram[(t - 2) * P:(t - 1) * P, :], X[:, t, :]).then_inc(*dma("x_saved", l))
            for t in range(2, TILES):
                pool.wait_ge(*at("final", t))
                pool.dma_start(out[0, (t - 2) * P:(t - 1) * P, :], xn[:, t, :]).then_inc(*dma("stored"))
            pool.wait_ge(*at("stored"))

        @block.scalar
        def _(act):
            act.wait_ge(*at("vec_turned"))
            act.activation(ct[:, 0, :], vt[:, 0:16], ACT.Tanh, scale=0.5).then_inc(*up("cond_tanh"))

            def mod_rows(l, b):
                act.wait_ge(*at("filled", "mod", l, b))
                if b < 4:
                    if (l, b) != (0, 0):
                        act.wait_ge(*at("filled", *(("modT", l, b - 1) if b else ("gate", l - 1, 1, 1))))
                    act.activation(modrow, ps("mod", l, b)[:], ACT.Copy).then_inc(*up("modrow", l, b))
                    let_go(("mod", l, b), "modrow", l, b)
                else:
                    for s in range(2):
                        act.wait_ge(*at("filled", "gate", l, b - 4, s))
                        act.activation(gate[:, s, 512 * (b - 4):512 * (b - 3)], ps("gate", l, b - 4, s)[:],
                                       ACT.Copy).then_inc(*up("gate_row", l, b - 4, s))
                        let_go(("gate", l, b - 4, s), "gate_row", l, b - 4, s)

            for b in range(4):
                mod_rows(0, b)

            def rms(stage, group, n, scale, *key):
                act.wait_ge(*at("filled", *group))
                act.activation(rs[:, 0:n], ps(*group)[:, 0:n], ACT.Ln, bias=eps[:, 0:1], scale=scale)\
                    .then_inc(*up(stage + "_ln", *key))
                let_go(group, stage + "_ln", *key)
                act.wait_ge(*at(stage + "_ln", *key))
                act.activation(rs[:, 0:n], rs[:, 0:n], ACT.Exp, scale=-0.5).then_inc(*up(stage + "_rstd", *key))

            def x_rstd(l, tiles):
                if l == 0:
                    act.wait_ge(*at("x_in", 0))
                    act.wait_ge(*at("pool_init", "end"))
                for t in tiles:
                    if 0 < l < DEPTH:
                        act.wait_ge(*at("resid", l - 1, t, 1))
                    elif l == DEPTH:
                        act.wait_ge(*at("resid", l - 1, t, 1))
                    if t > tiles[0]:
                        act.wait_ge(*at("x_sq", l, t - 1))
                    elif l:
                        act.wait_ge(*at("resid", l - 1, tiles[-1], 1))
                    act.activation(tz[:].rearrange("p a b -> p (a b)"), X[:, t, :], ACT.Square,
                                   accum_out=ssx[:, t:t + 1]).then_inc(*up("x_sq", l, t))
                act.wait_ge(*at("x_sq", l, tiles[-1]))
                act.activation(rx[:, tiles[0]:TILES], ssx[:, tiles[0]:TILES], ACT.Ln, bias=eps[:, 0:1],
                               scale=1.0 / D).then_inc(*up("x_ln", l))
                act.wait_ge(*at("x_ln", l))
                act.activation(rx[:, tiles[0]:TILES], rx[:, tiles[0]:TILES], ACT.Exp, scale=-0.5)\
                    .then_inc(*up("x_rstd", l))

            prev_norm = None
            for l in range(DEPTH):
                x_rstd(l, list(range(TILES)))
                act.wait_ge(*at("mod_cols", l))
                for k in range(KD):
                    act.wait_ge(*at("filled", "xT", l, k, 0))
                    act.activation(hT[:, k, 0:256], ps("xT", l, k, 0)[:, 0:256], ACT.Identity,
                                   bias=mB[:, k, 1:2], scale=mA[:, k, 1:2]).then_inc(*up("hT_ctx", l, k))
                    let_go(("xT", l, k, 0), "hT_ctx", l, k)
                zi = 0
                for item in SEQ:
                    if item in ("small", "glaq", "glak"):
                        for c in chunks_of(item, l):
                            act.wait_ge(*at("filled", "F", l, item, c))
                            dst = small[:] if item == "small" else glaqk[:, item == "glak", :]
                            act.activation(dst[:, c[0]:sum(c)], ps("F", l, item, c)[:, 0:c[1]], ACT.Copy)\
                                .then_inc(*up("act_proj", l, item, c))
                            let_go(("F", l, item, c), "act_proj", l, item, c)
                    elif item[0] == "z":
                        for c in chunks_of(item, l):
                            act.wait_ge(*at("filled", "F", l, item, c))
                            if zi >= 2:
                                act.wait_ge(*at("zgate", l, zi - 2))
                            act.activation(tz[:, zi % 2, 0:c[1]], ps("F", l, item, c)[:, 0:c[1]], ACT.Tanh,
                                           scale=0.5).then_inc(*up("ztanh", l, zi))
                            zi += 1
                    elif item == "tok":
                        for t in range(TILES):
                            act.wait_ge(*at("filled", "tok", l, t))
                            act.activation(glav[:, t, :], ps("tok", l, t)[:, 0:256], ACT.Copy)\
                                .then_inc(*up("glav", l, t))
                    elif item == "ga":
                        for d in range(2):
                            col = (V_GBF, V_GBB)[d] + l
                            for c in (CTX, LAT):
                                act.wait_ge(*at("filled", "ga", l, d, c))
                                act.activation(kd[d][:, c[0]:sum(c)], ps("ga", l, d, c)[:, 0:c[1]], ACT.Abs,
                                               bias=vt[:, col:col + 1]).then_inc(*up("g_abs", l, d, c))
                            act.wait_ge(*at("g_abs", l, d, LAT))
                            act.activation(kd[d], kd[d], ACT.Exp, scale=-1.0).then_inc(*up("g_exp", l, d))
                            act.wait_ge(*at("g_exp", l, d))
                            act.activation(kd[d], kd[d], ACT.Ln, bias=ones[:, 0:1]).then_inc(*up("g_ln", l, d))
                    elif item == "ga2":
                        for d in range(2):
                            act.wait_ge(*at("g_cum", l, d))
                            act.activation(Ef[d], cum[d], ACT.Exp, scale=1 / 16).then_inc(*up("g_E", l, d))
                            act.activation(ki[d], cum[d], ACT.Exp, scale=-1 / 16).then_inc(*up("g_Ei", l, d))
                            act.wait_ge(*at("g_rest", l, d))
                            act.activation(kd[d], kd[d], ACT.Exp, scale=1 / 16).then_inc(*up("kd_exp", l, d))
                    elif item[:2] == "ss":
                        j = int(item[2])
                        for c in chunks_of("q" if j == 0 else "kv", l):
                            act.wait_ge(*at("dve_proj", l, ("cq1", "ckv1")[j], c))
                            if prev_norm:
                                act.wait_ge(*at(*prev_norm))
                            act.activation(sq[:, :, 0:c[1]], cqkv[:, 2 * j:2 * j + 2, c[0]:sum(c)], ACT.Square)\
                                .then_inc(*up("lora_sq", l, j, c))
                            rms("lora", ("ss", l, j, c), c[1], 1.0 / LORA, l, j, c)
                            prev_norm = ("lora_norm", l, j, c)
                    elif item[:3] == "gss":
                        i = int(item[3])
                        name = ("gq0", "gq1", "gq2", "gk")[i]
                        for c in chunks_of(name, l):
                            act.wait_ge(*at("dve_proj", l, name, c))
                            act.wait_ge(*at(*prev_norm))
                            act.activation(sq[:, 0, 0:c[1]], gqk[:, i, c[0]:sum(c)], ACT.Square)\
                                .then_inc(*up("gqa_sq", l, i, c))
                            rms("gqa", ("gss", l, i, c), c[1], 1.0 / HD, l, i, c)
                            prev_norm = ("gqa_norm", l, i, c)
                    elif item == "kdT":
                        for d in range(2):
                            for half in range(2):
                                act.wait_ge(*at("filled", "kdT", l, d, half))
                                act.wait_ge(*at("gla_factors", l, d))
                                act.activation(kdtok[d][:, 3 * half:3 * half + 3, :],
                                               ps("kdT", l, d, half)[:, 0:384].rearrange("p (t c) -> p t c", t=3),
                                               ACT.Copy).then_inc(*up("kdtok", l, d, half))
                                let_go(("kdT", l, d, half), "kdtok", l, d, half)
                before = None
                for t in out_tiles(l):
                    act.wait_ge(*at("filled", "o", l, t))
                    if before is not None:
                        act.wait_ge(*at("o_norm", l, before))
                        if before - 1 in out_tiles(l):
                            act.wait_ge(*at("filled", "oT", l, before - 1))
                    act.activation(on[:, t % 2, :], ps("o", l, t)[:, 0:256], ACT.Copy).then_inc(*up("o_copy", l, t))
                    let_go(("o", l, t), "o_copy", l, t)
                    act.wait_ge(*at("o_ss", l, t))
                    act.activation(ss4[:], ss4[:], ACT.Ln, bias=eps[:, 0:1], scale=1.0 / GLA_DV)\
                        .then_inc(*up("o_ln", l, t))
                    act.wait_ge(*at("o_ln", l, t))
                    act.activation(ss4[:], ss4[:], ACT.Exp, scale=-0.5).then_inc(*up("o_rstd", l, t))
                    before = t

                def head_in(h):
                    b = h % 2
                    if h >= 1:
                        free = at("filled", "mx", l, h - 1, qbs(l)[-1][0], TILES - 1, 1)
                    elif l:
                        free = at("filled", "mx", l - 1, 11, 256, TILES - 1, 1)
                    else:
                        free = None
                    if h < MLA_H:
                        if h == 0:
                            act.wait_ge(*at("filled", "F", l, "z7", LAT))
                        if h >= 2:
                            act.wait_ge(*at("filled", "sc", l, h - 2, 256, TILES - 1))
                        for c in chunks_of("q", l):
                            act.wait_ge(*at("filled", "qp", l, h, c))
                            r = 64 if c == LAT else 96
                            act.activation(qh[b][0:r, c[0]:sum(c)], ps("qp", l, h, c)[0:r, 0:c[1]], ACT.Copy)\
                                .then_inc(*up("q_in", l, h, c))
                            if c == CTX:
                                let_go(("qp", l, h, c), "q_in", l, h, c)
                        for c in (CTX, LAT):
                            act.wait_ge(*at("filled", "kp", l, h, c))
                            act.activation(kh[b][0:64, c[0]:sum(c)], ps("kp", l, h, c)[0:64, 0:c[1]], ACT.Copy)\
                                .then_inc(*up("k_in", l, h, c))
                            let_go(("kp", l, h, c), "k_in", l, h, c)
                        if free:
                            act.wait_ge(*free)
                        act.wait_ge(*at("k_in", l, h, LAT))
                        act.wait_ge(*at("kh_rope", l, 1))
                        act.activation(kr[:, :], kh[b][0:96, :], ACT.Copy).then_inc(*up("round", l, h))
                        act.wait_ge(*at("q_rope", l, h))
                        act.wait_ge(*at("q_in", l, h, LAT))
                        act.activation(qr[:, lat_of(l)], qh[b][0:96, lat_of(l)], ACT.Copy)\
                            .then_inc(*up("round", l, h))
                    else:
                        g = h - MLA_H
                        if g < 2:
                            act.wait_ge(*at("gqa_zero", l, b))
                        if h >= 2:
                            act.wait_ge(*at("filled", "sc", l, h - 2, 256, TILES - 1))
                        act.wait_ge(*at("gqa_rope", l, 3))
                        row, krow = 64 * (g % 2), 64 * (g // 3)
                        act.activation(qh[b][0:64, lat_of(l)], gqk[row:row + 64, g // 2, lat_of(l)], ACT.Copy)\
                            .then_inc(*up("q_in", l, h, LAT))
                        act.activation(kh[b][0:64, :], gqk[krow:krow + 64, 3, :], ACT.Copy)\
                            .then_inc(*up("k_in", l, h, LAT))
                        act.wait_ge(*free)
                        act.wait_ge(*at("q_in", l, h, LAT))
                        act.activation(qr[:, lat_of(l)], qh[b][0:96, lat_of(l)], ACT.Copy)\
                            .then_inc(*up("round", l, h))
                        act.wait_ge(*at("k_in", l, h, LAT))
                        act.activation(kr[:, :], kh[b][0:96, :], ACT.Copy).then_inc(*up("round", l, h))

                def neg_max(h):
                    for q0, nq, nk in qbs(l):
                        act.wait_ge(*at("filled", "nm", l, h, q0))
                        act.activation(qh[h % 2][96:97, q0:q0 + nq], ps("nm", l, h, q0)[96:97, 0:nq], ACT.Copy)\
                            .then_inc(*up("nm_row", l, h, q0))
                        let_go(("nm", l, h, q0), "nm_row", l, h, q0)

                slot = 0
                head_in(0)
                neg_max(0)
                for h in heads:
                    todo = [(q0, nq, kt) for q0, nq, nk in qbs(l) for kt in range(nk // P)]
                    if h + 1 < len(heads):
                        head_in(h + 1)
                    for q0, nq, kt in todo:
                        act.wait_ge(*at("filled", "sc", l, h, q0, kt))
                        if slot >= 4:
                            act.wait_ge(*at(*prob_reader(l, slot - 4)))
                        act.activation(prob[slot % 4][:, 0:nq], ps("sc", l, h, q0, kt)[:, 0:nq], ACT.Exp,
                                       scale=MLA_SCALE if h < MLA_H else GQA_SCALE)\
                            .then_inc(*up("prob", l, slot))
                        let_go(("sc", l, h, q0, kt), "prob", l, slot)
                        slot += 1
                    if h + 1 < len(heads):
                        neg_max(h + 1)
                act.wait_ge(*at("filled", "vp", l, TILES - 1))
                act.wait_ge(*at("filled", "kp", l, MLA_H - 1, LAT))
                for b in (4, 5):
                    mod_rows(l, b)
                if l + 1 < DEPTH:
                    for b in range(4):
                        mod_rows(l + 1, b)
            x_rstd(DEPTH, list(range(2, TILES)))

        @block.vector
        def _(dve):
            dve.wait_ge(*at("filled", "vec"))
            dve.tensor_copy(vt[:], ps("vec")[:, 0:V_ROWS]).then_inc(*up("vec_turned"))
            let_go(("vec",), "vec_turned")
            dve.wait_ge(*at("vec_turned"))
            dve.tensor_scalar(vth[:], vt[:], 0.5, None, ALU.mult).then_inc(*up("vec_half"))
            dve.wait_ge(*at("cond_tanh"))
            dve.wait_ge(*at("vec_half"))
            dve.wait_ge(*at("pool_init", "end"))
            dve.scalar_tensor_tensor(out=sc[:, :, 0:2].rearrange("p k s -> p s k"),
                                     in0=ct[:, 0, :].rearrange("p (s k) -> p s k", s=2), scalar=1.0,
                                     in1=vth[:, 0:16].rearrange("p (s k) -> p s k", s=2),
                                     op0=ALU.add, op1=ALU.mult).then_inc(*up("cond_silu"))

            def mod_cols(l, b):
                dve.wait_ge(*at("filled", "modT", l, b))
                if b == 0 and l:
                    dve.wait_ge(*at("mod_cols", l - 1))
                src = ps("modT", l, b)[:].rearrange("p (f j r) -> p f r j", f=4, j=4)[:, :, 0:2, :]
                dve.tensor_reduce(modc[:, 4 * b:4 * b + 4, :], src, AX, ALU.add).then_inc(*up("mod_sum", l, b))
                let_go(("modT", l, b), "mod_sum", l, b)
                if b == 3:
                    bm = V_BMOD + 24 * l
                    if l:
                        dve.wait_ge(*at("hT_ctx", l - 1, KD - 1))
                    dve.wait_ge(*at("mod_sum", l, 3))
                    dve.tensor_tensor(mB[:], modc[:, 0:8, :], vt[:, bm:bm + 8].unsqueeze(2).broadcast_to([P, 8, 2]),
                                      ALU.add).then_inc(*up("mod_b", l))
                    dve.tensor_tensor(mA[:], modc[:, 8:16, :],
                                      vt[:, bm + 8:bm + 16].unsqueeze(2).broadcast_to([P, 8, 2]),
                                      ALU.add).then_inc(*up("mod_a", l))
                    dve.wait_ge(*at("mod_a", l))
                    nw = V_NORM + 8 * l
                    dve.scalar_tensor_tensor(out=mA[:], in0=mA[:], scalar=1.0,
                                             in1=vt[:, nw:nw + 8].unsqueeze(2).broadcast_to([P, 8, 2]),
                                             op0=ALU.add, op1=ALU.mult).then_inc(*up("mod_cols", l))

            def xhat(l):
                dve.wait_ge(*at("x_rstd", l))
                for t in range(TILES):
                    if l and t == 0:
                        dve.wait_ge(*at("filled", "out", l - 1, out_tiles(l - 1)[-1], 1))
                    dve.tensor_scalar(xn[:, t, :], X[:, t, :], rx[:, t:t + 1], None, ALU.mult)\
                        .then_inc(*up("xhat", l, t))

            xhat(0)
            for b in range(4):
                mod_cols(0, b)

            for l in range(DEPTH):
                if l:
                    xhat(l)
                dve.wait_ge(*at("mod_cols", l))
                for k in range(KD):
                    dve.wait_ge(*at("filled", "xT", l, k, 1))
                    dve.tensor_scalar(hT[:, k, 256:T], ps("xT", l, k, 1)[:], mA[:, k, 0:1], mB[:, k, 0:1],
                                      ALU.mult, ALU.add).then_inc(*up("hT_lat", l, k))
                    let_go(("xT", l, k, 1), "hT_lat", l, k)
                zi = 0
                for item in SEQ:
                    if item == "small":
                        dve.wait_ge(*at("act_proj", l, "small", LAT))
                        lat = slice(256, T)
                        dve.tensor_tensor(rt[64:96, 0, :], small[96:128, lat], tabm[96:128, :], ALU.mult)\
                            .then_inc(*up("kr_mul", l))
                        dve.tensor_tensor(rt[64:96, 1, :], small[64:96, lat], tabm[64:96, :], ALU.mult)\
                            .then_inc(*up("kr_mul", l))
                        dve.wait_ge(*at("kr_mul", l))
                        dve.tensor_tensor(small[64:96, lat], rt[64:96, 0, :], rt[64:96, 1, :], ALU.add)\
                            .then_inc(*up("kr_rope", l))
                    elif item in ("cq0", "cq1", "ckv0", "ckv1", "gq0", "gq1", "gq2", "gk"):
                        i = ("cq0", "cq1", "ckv0", "ckv1", "gq0", "gq1", "gq2", "gk").index(item)
                        for c in chunks_of(item, l):
                            dve.wait_ge(*at("filled", "F", l, item, c))
                            dst = cqkv[:, i, :] if i < 4 else gqk[:, i - 4, :]
                            dve.tensor_copy(dst[:, c[0]:sum(c)], ps("F", l, item, c)[:, 0:c[1]])\
                                .then_inc(*up("dve_proj", l, item, c))
                            let_go(("F", l, item, c), "dve_proj", l, item, c)
                    elif item[0] == "z":
                        for c in chunks_of(item, l):
                            dve.wait_ge(*at("ztanh", l, zi))
                            dve.scalar_tensor_tensor(out=Y[:, int(item[1]), c[0]:sum(c)],
                                                     in0=tz[:, zi % 2, 0:c[1]], scalar=1.0,
                                                     in1=ps("F", l, item, c)[:, 0:c[1]], op0=ALU.add,
                                                     op1=ALU.mult).then_inc(*up("zgate", l, zi))
                            let_go(("F", l, item, c), "zgate", l, zi)
                            zi += 1
                    elif item == "tok":
                        for t in range(TILES):
                            dve.wait_ge(*at("glav", l, t))
                            src = ps("tok", l, t)[:, 256:384].rearrange("p (g v) -> p g v", g=2)
                            for half in range(2):
                                dve.tensor_copy(vg[:, t, :, 128 * half:128 * half + 64], src)\
                                    .then_inc(*up("vg", l, t, half))
                            let_go(("tok", l, t), "vg", l, t, 1)
                    elif item == "ga":
                        for d in range(2):
                            col = (V_GBF, V_GBB)[d] + l
                            for c in (CTX, LAT):
                                dve.wait_ge(*at("g_abs", l, d, c))
                                dve.tensor_scalar(qd[d][:, c[0]:sum(c)], ps("ga", l, d, c)[:, 0:c[1]],
                                                  vt[:, col:col + 1], 0.0, ALU.add, ALU.min)\
                                    .then_inc(*up("g_min", l, d, c))
                                let_go(("ga", l, d, c), "g_min", l, d, c)
                            dve.wait_ge(*at("g_ln", l, d))
                            dve.wait_ge(*at("g_min", l, d, LAT))
                            dve.tensor_tensor(qd[d], qd[d], kd[d], ALU.subtract).then_inc(*up("g_log", l, d))
                            dve.wait_ge(*at("g_log", l, d))
                            g, o = (qd[d], cum[d]) if d == 0 else (qd[d][:, ::-1], cum[d][:, ::-1])
                            if d == 0:
                                dve.wait_ge(*at("filled", "modT", l, 3))
                            dve.tensor_tensor_scan(o, keep[:], g, 0.0, ALU.mult, ALU.add)\
                                .then_inc(*up("g_cum", l, d))
                    elif item == "ga2":
                        for d in range(2):
                            e = CHUNK - 1 if d == 0 else 0
                            last = cum[d][:, e:T:CHUNK].unsqueeze(2).broadcast_to([P, NCHUNK, CHUNK])
                            dve.wait_ge(*at("g_cum", l, d))
                            dve.tensor_tensor(kd[d].rearrange("p (n c) -> p n c", n=NCHUNK), last,
                                              cum[d].rearrange("p (n c) -> p n c", n=NCHUNK), ALU.subtract)\
                                .then_inc(*up("g_rest", l, d))
                    elif item == "glamul":
                        dve.wait_ge(*at("act_proj", l, "glaq", LAT))
                        dve.wait_ge(*at("act_proj", l, "glak", LAT))
                        for d in range(2):
                            dve.wait_ge(*at("kd_exp", l, d))
                            dve.tensor_tensor(kd[d], kd[d], glaqk[:, 1, :], ALU.mult).then_inc(*up("gla_kd", l, d))
                            dve.tensor_tensor(ki[d], ki[d], glaqk[:, 1, :], ALU.mult).then_inc(*up("gla_ki", l, d))
                            e = CHUNK - 1 if d == 0 else 0
                            dve.tensor_copy(dec[:, d, :], Ef[d][:, e:T:CHUNK]).then_inc(*up("gla_dec", l, d))
                            lat = lat_of(l)
                            dve.scalar_tensor_tensor(out=qd[d][:, lat], in0=glaqk[:, 0, lat],
                                                     scalar=GLA_DK ** -0.5, in1=Ef[d][:, lat], op0=ALU.mult,
                                                     op1=ALU.mult).then_inc(*up("gla_factors", l, d))
                    elif item[:2] == "ss":
                        j = int(item[2])
                        for c in chunks_of("q" if j == 0 else "kv", l):
                            dve.wait_ge(*at("lora_rstd", l, j, c))
                            for f in range(2):
                                col = (V_MQ, V_MKV)[j] + 2 * l + f
                                v = cqkv[:, 2 * j + f, c[0]:sum(c)]
                                dve.scalar_tensor_tensor(out=v, in0=v, scalar=vt[:, col:col + 1],
                                                         in1=rs[:, 0:c[1]], op0=ALU.mult, op1=ALU.mult)\
                                    .then_inc(*up("lora_norm", l, j, c))
                    elif item[:3] == "gss":
                        i = int(item[3])
                        col = (V_QN if i < 3 else V_KN) + l
                        for c in chunks_of(("gq0", "gq1", "gq2", "gk")[i], l):
                            dve.wait_ge(*at("gqa_rstd", l, i, c))
                            v = gqk[:, i, c[0]:sum(c)]
                            dve.scalar_tensor_tensor(out=v, in0=v, scalar=vt[:, col:col + 1], in1=rs[:, 0:c[1]],
                                                     op0=ALU.mult, op1=ALU.mult).then_inc(*up("gqa_norm", l, i, c))
                    elif item[:4] == "rope":
                        i = int(item[4])
                        v = gqk[:, i, 256:T]
                        dve.wait_ge(*at("filled", "rope", l, i))
                        dve.wait_ge(*(at("gqa_rope", l, i - 1) if i else at("kr_rope", l)))
                        dve.tensor_tensor(rt[:, 0, :], ps("rope", l, i)[:], sing, ALU.mult)\
                            .then_inc(*up("gqa_sin", l, i))
                        let_go(("rope", l, i), "gqa_sin", l, i)
                        dve.wait_ge(*at("gqa_norm", l, i, LAT))
                        dve.tensor_tensor(v, v, cosg, ALU.mult).then_inc(*up("gqa_cos", l, i))
                        dve.wait_ge(*at("gqa_cos", l, i))
                        dve.tensor_tensor(v, v, rt[:, 0, :], ALU.add).then_inc(*up("gqa_rope", l, i))
                    elif item == "ds":
                        for d in range(2):
                            for par in range(2):
                                dve.wait_ge(*at("filled", "ds", l, d, par))
                            order = chunk_order(d)
                            dve.memset(St[d][:, order[0], :], 0.0).then_inc(*up("state", l, d, order[0]))
                            for n, m in zip(order, order[1:]):
                                dve.wait_ge(*at("state", l, d, n))
                                dve.scalar_tensor_tensor(
                                    out=St[d][:, m, :], in0=St[d][:, n, :], scalar=dec[:, d, n:n + 1],
                                    in1=ps("ds", l, d, n % 2)[:, 64 * (n // 2):64 * (n // 2) + 64],
                                    op0=ALU.mult, op1=ALU.add).then_inc(*up("state", l, d, m))
                            tally.mark[("state", (l, d))] = tally.count["state"]
                            for par in range(2):
                                let_go(("ds", l, d, par), "state", l, d)

                def a_mask(t, d, before):
                    dve.wait_ge(*at("filled", "A", l, t, d))
                    dve.wait_ge(*at("bd_zero", l))
                    if before is not None:
                        dve.wait_ge(*at("filled", "o", l, before))
                    dve.copy_predicated(Ab[d], mask[d].unsqueeze(1).broadcast_to([P, 4, P]),
                                        ps("A", l, t, d)[:].rearrange("p (h t) -> p h t", h=4))\
                        .then_inc(*up("A_masked", l, t, d))
                    let_go(("A", l, t, d), "A_masked", l, t, d)

                def o_finish(t, before):
                    dve.wait_ge(*at("o_copy", l, t))
                    if before is not None:
                        dve.wait_ge(*at("o_ss", l, before))
                    o = on[:, t % 2, :]
                    dve.tensor_tensor(sqo, o, o, ALU.mult).then_inc(*up("o_sq", l, t))
                    dve.wait_ge(*at("o_sq", l, t))
                    dve.tensor_reduce(ss4[:], sqo.rearrange("p (h v) -> p h v", h=4), AX, ALU.add)\
                        .then_inc(*up("o_ss", l, t))
                    dve.wait_ge(*at("o_rstd", l, t))
                    o4 = o.rearrange("p (h v) -> p h v", h=4)
                    dve.tensor_tensor(o4, o4, ss4[:].unsqueeze(2).broadcast_to([P, 4, 64]), ALU.mult)\
                        .then_inc(*up("o_norm", l, t))
                    dve.wait_ge(*at("filled", "oT", l, t))
                    y = Y[:, 0:2, t * P:(t + 1) * P]
                    dve.scalar_tensor_tensor(out=y, in0=ps("oT", l, t)[:, 0:256].rearrange("p (f t) -> p f t", f=2),
                                             scalar=vth[:, V_GN + l:V_GN + l + 1], in1=y, op0=ALU.mult,
                                             op1=ALU.mult).then_inc(*up("y_gla", l, t))
                    let_go(("oT", l, t), "y_gla", l, t)

                before = None
                for t in out_tiles(l):
                    for d in range(2):
                        a_mask(t, d, before)
                    o_finish(t, before)
                    before = t

                def mla_v():
                    dve.wait_ge(*at("vm_ones", l))
                    for t in range(TILES):
                        dve.wait_ge(*at("filled", "vp", l, t))
                        src = ps("vp", l, t)[:, 0:384].rearrange("p (r e v) -> p r e v", r=3, e=2)
                        for e in range(2):
                            dve.tensor_copy(vm[:, t, :, 128 * e:128 * e + 64], src[:, :, e, :])\
                                .then_inc(*up("vm", l, t, e))
                        let_go(("vp", l, t), "vm", l, t, 1)

                def q_rope(h):
                    if h >= MLA_H:
                        return
                    p = ps("qp", l, h, LAT)
                    dve.wait_ge(*at("q_in", l, h, LAT))
                    if h:
                        dve.wait_ge(*at("q_rope", l, h - 1))
                    dve.tensor_tensor(rt[64:96, 0, :], p[96:128, :], tabm[96:128, :], ALU.mult)\
                        .then_inc(*up("q_mul", l, h, 0))
                    dve.tensor_tensor(rt[64:96, 1, :], p[64:96, :], tabm[64:96, :], ALU.mult)\
                        .then_inc(*up("q_mul", l, h, 1))
                    let_go(("qp", l, h, LAT), "q_mul", l, h, 1)
                    dve.wait_ge(*at("q_mul", l, h, 1))
                    if h >= 2:
                        dve.wait_ge(*at("filled", "sc", l, h - 2, 256, TILES - 1))
                    dve.tensor_tensor(qh[h % 2][64:96, 256:T], rt[64:96, 0, :], rt[64:96, 1, :], ALU.add)\
                        .then_inc(*up("q_rope", l, h))

                def maxima(h):
                    if h >= 2:
                        dve.wait_ge(*at("filled", "nm", l, h - 2, 256))
                    elif l:
                        dve.wait_ge(*at("filled", "nm", l - 1, 10 + h, 256))
                    for q0, nq, nk in qbs(l):
                        for t in range(q0 // P, (q0 + nq) // P):
                            if q0 == 0:
                                dve.wait_ge(*at("filled", "mx", l, h, q0, t, 0))
                                dve.tensor_reduce(nmx[:, h % 2, t:t + 1], ps("mx", l, h, q0, t, 0)[:, 0:256], AX,
                                                  ALU.max, negate=True).then_inc(*up("part_max", l, h, q0, t, 0))
                                let_go(("mx", l, h, q0, t, 0), "part_max", l, h, q0, t, 0)
                                continue
                            for half in range(2):
                                dve.wait_ge(*at("filled", "mx", l, h, q0, t, half))
                                if h and t == 2 and not half:
                                    dve.wait_ge(*at("neg_max", l, h - 1))
                                dve.tensor_reduce(mxp[:, t, half:half + 1], ps("mx", l, h, q0, t, half)[:, 0:384],
                                                  AX, ALU.max).then_inc(*up("part_max", l, h, q0, t, half))
                                let_go(("mx", l, h, q0, t, half), "part_max", l, h, q0, t, half)
                    dve.wait_ge(*at("part_max", l, h, 256, TILES - 1, 1))
                    dve.tensor_reduce(nmx[:, h % 2, 2:TILES], mxp[:, 2:TILES, :], AX, ALU.max, negate=True)\
                        .then_inc(*up("neg_max", l, h))

                last_y = [None]

                def normalise(h, q0, nq):
                    pv = pv_banks[pv_index(l, h, q0) % 2]
                    r, s = 64 * (h % 2), 64 - 64 * (h % 2)
                    tile = (2 + h // 2) if h < MLA_H else (5 + (h - MLA_H) // 2)
                    dve.wait_ge(*at("pv_filled", l, h, q0))
                    if last_y[0]:
                        dve.wait_ge(*at("y_attn", *last_y[0]))
                    dve.reciprocal(rd[r:r + 64, 0:nq], pv[s:s + 64, 0:nq]).then_inc(*up("recip", l, h, q0))
                    dve.wait_ge(*at("recip", l, h, q0))
                    dve.scalar_tensor_tensor(out=un[r:r + 64, 0:nq], in0=pv[r:r + 64, 0:nq], scalar=0.5,
                                             in1=rd[r:r + 64, 0:nq], op0=ALU.mult, op1=ALU.mult)\
                        .then_inc(*up("o_scaled", l, h, q0))
                    dve.wait_ge(*at("o_scaled", l, h, q0))
                    y = Y[r:r + 64, tile, q0:q0 + nq]
                    dve.tensor_tensor(y, un[r:r + 64, 0:nq], y, ALU.mult).then_inc(*up("y_attn", l, h, q0))
                    last_y[0] = (l, h, q0)

                q_rope(0)
                maxima(0)
                mla_v()
                for h in heads:
                    if h + 1 < len(heads):
                        q_rope(h + 1)
                        maxima(h + 1)
                    for q0, nq, nk in qbs(l):
                        normalise(h, q0, nq)

                for b in (0, 1):
                    dve.wait_ge(*at("filled", "mod", l, 4 + b))
                    dve.wait_ge(*at("brow_in", l))
                    dve.wait_ge(*(at("filled", "gate", l, 0, 1) if b else at("filled", "modT", l, 3)))
                    dve.tensor_tensor(modrow, ps("mod", l, 4 + b)[:], brow[:, b, :], ALU.add)\
                        .then_inc(*up("modrow_gate", l, b))
                    let_go(("mod", l, 4 + b), "modrow_gate", l, b)
                if l + 1 < DEPTH:
                    for b in range(4):
                        mod_cols(l + 1, b)
                dve.wait_ge(*at("x_back", l))
                done = []
                for n in range(2):
                    for t in out_tiles(l):
                        s = 1 if t < 2 else 0
                        dve.wait_ge(*at("filled", "out", l, t, n))
                        dve.wait_ge(*at("gate_row", l, n, s))
                        i = len(done)
                        if i >= 2:
                            dve.wait_ge(*at("resid", l, *done[i - 2]))
                        dve.tensor_tensor(rt[:, i % 2, :], ps("out", l, t, n)[:], gate[:, s, 512 * n:512 * n + 512],
                                          ALU.mult).then_inc(*up("gated", l, t, n))
                        let_go(("out", l, t, n), "gated", l, t, n)
                        dve.wait_ge(*at("gated", l, t, n))
                        xs = X[:, t, 512 * n:512 * n + 512]
                        dve.tensor_tensor(xs, xs, rt[:, i % 2, :], ALU.add).then_inc(*up("resid", l, t, n))
                        done.append((t, n))
            dve.wait_ge(*at("x_rstd", DEPTH))
            dve.wait_ge(*at("fnw_in"))
            for t in range(2, TILES):
                dve.scalar_tensor_tensor(out=xn[:, t, :], in0=X[:, t, :], scalar=rx[:, t:t + 1], in1=fnw,
                                         op0=ALU.mult, op1=ALU.mult).then_inc(*up("final", t))

        @block.tensor
        def _(pe):
            def open_(*group):
                tally.order.append(group)
                i = len(tally.order) - 1
                if tally.before and i >= RING:
                    for stage, step in tally.before.freed[tally.before.order[i - RING]]:
                        pe.wait_ge(*at(stage, *step))
                return banks[i % RING]

            def close(mm, *group):
                mm.then_inc(*up("filled", *group))
                mm_group[0] = group

            mm_group = [None]

            def block_done(i):
                tally.mark[("filled", ("block", i))] = tally.count["filled"]

            def block_wait(i):
                pe.wait_ge(*at(f"w_half{i % 2}", i))

            pe.wait_ge(*at("vec_in"))
            pe.wait_ge(*at("con_in"))
            p = open_("vec")
            close(pe.transpose(p[:, 0:V_ROWS], vec, ident[0:V_ROWS, 0:V_ROWS]), "vec")

            def mod(l, b):
                i = W_POS[("mod", l, b)]
                p = open_("mod", l, b)
                block_wait(i)
                for r in range(2):
                    for j in range(4):
                        k = 4 * r + j
                        mm = pe.matmul(p[32 * j:32 * j + 32, :], sc[:, k, :], W[:, i % 2, k, :], start=(r == 0),
                                       stop=(r == 1), skip_group_check=True)
                close(mm, "mod", l, b)
                block_done(i)
                if b < 4:
                    q = open_("modT", l, b)
                    pe.wait_ge(*at("modrow", l, b))
                    for f in range(4):
                        mm = pe.transpose(q[:, P * f:P * f + P], modrow[:, P * f:P * f + P], ident)
                    close(mm, "modT", l, b)
                else:
                    for s in range(2):
                        q = open_("gate", l, b - 4, s)
                        pe.wait_ge(*at("modrow_gate", l, b - 4))
                        close(pe.matmul(q[:], sel[:, s, :], modrow, start=True, stop=True), "gate", l, b - 4, s)

            pe.wait_ge(*at("cond_silu"))
            for b in range(4):
                mod(0, b)

            for l in range(DEPTH):
                for k in range(KD):
                    for part, tiles in ((0, (0, 1)), (1, (2, 3, 4, 5))):
                        p = open_("xT", l, k, part)
                        for j, t in enumerate(tiles):
                            pe.wait_ge(*at("xhat", l, t))
                            mm = pe.transpose(p[:, P * j:P * j + P], xn[:, t, P * k:P * k + P], ident)
                        close(mm, "xT", l, k, part)
                pe.wait_ge(*at("hT_ctx", l, KD - 1))
                pe.wait_ge(*at("hT_lat", l, KD - 1))
                for item in SEQ:
                    if item in SLOT:
                        b, s = SLOT[item]
                        i = W_POS[("in", l, b)]
                        w = W[:, i % 2]
                        if s == 0:
                            block_wait(i)
                        if item == "small":
                            pe.wait_ge(*at("swap_kr", l))
                    if item == "tok":
                        for t in range(TILES):
                            p = open_("tok", l, t)
                            for k in range(KD):
                                mm = pe.matmul(p[:, 0:384], hT[:, k, t * P:(t + 1) * P], w[:, k, 0:384],
                                               start=(k == 0), stop=(k == KD - 1))
                            close(mm, "tok", l, t)
                    elif item in SLOT:
                        for c in chunks_of(item, l):
                            p = open_("F", l, item, c)
                            for k in range(KD):
                                mm = pe.matmul(p[:, 0:c[1]], w[:, k, s * P:s * P + P], hT[:, k, c[0]:sum(c)],
                                               start=(k == 0), stop=(k == KD - 1))
                            close(mm, "F", l, item, c)
                        if item in LAST_OF:
                            block_done(i)
                    elif item == "ga":
                        pe.wait_ge(*at("wa_in", l))
                        pe.wait_ge(*at("act_proj", l, "small", LAT))
                        for d in range(2):
                            for c in (CTX, LAT):
                                p = open_("ga", l, d, c)
                                close(pe.matmul(p[:, 0:c[1]], wa[:, d, :], small[0:32, c[0]:sum(c)], start=True,
                                                stop=True), "ga", l, d, c)
                    elif item[:2] == "ss":
                        j = int(item[2])
                        for c in chunks_of("q" if j == 0 else "kv", l):
                            p = open_("ss", l, j, c)
                            pe.wait_ge(*at("lora_sq", l, j, c))
                            for f in range(2):
                                mm = pe.matmul(p[:, 0:c[1]], ones[:], sq[:, f, 0:c[1]], start=(f == 0), stop=(f == 1))
                            close(mm, "ss", l, j, c)
                    elif item[:3] == "gss":
                        i = int(item[3])
                        for c in chunks_of(("gq0", "gq1", "gq2", "gk")[i], l):
                            p = open_("gss", l, i, c)
                            pe.wait_ge(*at("gqa_sq", l, i, c))
                            close(pe.matmul(p[:, 0:c[1]], blk, sq[:, 0, 0:c[1]], start=True, stop=True),
                                  "gss", l, i, c)
                    elif item[:4] == "rope":
                        i = int(item[4])
                        p = open_("rope", l, i)
                        pe.wait_ge(*at("gqa_norm", l, i, LAT))
                        close(pe.matmul(p[:], perm, gqk[:, i, 256:T], start=True, stop=True), "rope", l, i)
                    elif item == "kdT":
                        for d in range(2):
                            pe.wait_ge(*at("gla_kd", l, d))
                            for half in range(2):
                                p = open_("kdT", l, d, half)
                                for j in range(3):
                                    t = 3 * half + j
                                    mm = pe.transpose(p[:, P * j:P * j + P], kd[d][:, t * P:t * P + P], ident)
                                close(mm, "kdT", l, d, half)
                    elif item == "ds":
                        pe.wait_ge(*at("glav", l, TILES - 1))
                        for d in range(2):
                            pe.wait_ge(*at("kdtok", l, d, 1))
                            for par in range(2):
                                p = open_("ds", l, d, par)
                                r = slice(64 * par, 64 * par + 64)
                                for j in range(TILES):
                                    for h in range(GLA_H):
                                        mm = pe.matmul(p[32 * h:32 * h + 32, 64 * j:64 * j + 64],
                                                       kdtok[d][r, j, 32 * h:32 * h + 32],
                                                       glav[r, j, 64 * h:64 * h + 64], start=True, stop=True)
                                close(mm, "ds", l, d, par)

                def gla_a(t):
                    for d in range(2):
                        p = open_("A", l, t, d)
                        pe.wait_ge(*at("qbd", l, t, d))
                        pe.wait_ge(*at("gla_ki", l, d))
                        close(pe.matmul(p[:], ki[d][:, t * P:t * P + P], qbd[d].rearrange("p h t -> p (h t)"),
                                        start=True, stop=True), "A", l, t, d)

                def gla_o(t):
                    p = open_("o", l, t)
                    for d in range(2):
                        pe.wait_ge(*at("Sbd", l, t, d))
                        for c in range(2):
                            pe.matmul(p[64 * c:64 * c + 64, 0:256], qd[d][:, t * P + 64 * c:t * P + 64 * c + 64],
                                      Sbd[d][:, c].rearrange("p h v -> p (h v)"), start=(d == 0), stop=False,
                                      skip_group_check=True)
                    for d in range(2):
                        pe.wait_ge(*at("A_masked", l, t, d))
                        for h in range(GLA_H):
                            mm = pe.matmul(p[:, 64 * h:64 * h + 64], Ab[d][:, h, :], glav[:, t, 64 * h:64 * h + 64],
                                           start=False, stop=(d == 1), skip_group_check=True)
                    close(mm, "o", l, t)

                def gla_t(t):
                    p = open_("oT", l, t)
                    pe.wait_ge(*at("o_norm", l, t))
                    for f in range(2):
                        mm = pe.transpose(p[:, P * f:P * f + P], on[:, t % 2, P * f:P * f + P], ident)
                    close(mm, "oT", l, t)

                tiles = out_tiles(l)
                for t in tiles:
                    gla_a(t)
                    gla_o(t)
                    gla_t(t)

                def project(h):
                    if h >= MLA_H:
                        return
                    if h == 0:
                        pe.wait_ge(*at("swap_q", l))
                        pe.wait_ge(*at("lora_norm", l, 1, LAT))
                    for c in chunks_of("q", l):
                        p = open_("qp", l, h, c)
                        for f in range(2):
                            mm = pe.matmul(p[:, 0:c[1]], wuq[:, f, h, :], cqkv[:, f, c[0]:sum(c)], start=(f == 0),
                                           stop=(f == 1))
                        close(mm, "qp", l, h, c)
                    for c in (CTX, LAT):
                        p = open_("kp", l, h, c)
                        for f in range(2):
                            mm = pe.matmul(p[0:64, 0:c[1]], wukv[:, f, h, 0:64], cqkv[:, 2 + f, c[0]:sum(c)],
                                           start=(f == 0), stop=(f == 1))
                        close(mm, "kp", l, h, c)

                def maxes(h):
                    pe.wait_ge(*at("round", l, h))
                    for q0, nq, nk in qbs(l):
                        n = min(nk, 384)
                        for t in range(q0 // P, (q0 + nq) // P):
                            for half in range(nk // n):
                                p = open_("mx", l, h, q0, t, half)
                                close(pe.matmul(p[:, 0:n], qr[:, t * P:t * P + P], kr[:, n * half:n * half + n],
                                                start=True, stop=True), "mx", l, h, q0, t, half)
                        if nk == 256:
                            continue

                def max_rows(h):
                    pe.wait_ge(*at("neg_max", l, h))
                    for q0, nq, nk in qbs(l):
                        p = open_("nm", l, h, q0)
                        for j in range(nq // P):
                            t = q0 // P + j
                            mm = pe.matmul(p[96:97, P * j:P * j + P], nmx[:, h % 2, t:t + 1], ident, start=True,
                                           stop=True)
                        close(mm, "nm", l, h, q0)

                def values():
                    for t in range(TILES):
                        p = open_("vp", l, t)
                        for f in range(2):
                            mm = pe.matmul(p[:, 0:384].rearrange("p (h v) -> p h v", h=MLA_H),
                                           cqkv[:, 2 + f, t * P:t * P + P], wukv[:, f, :, 64:128],
                                           start=(f == 0), stop=(f == 1))
                        close(mm, "vp", l, t)

                slot = [0]
                pend = []

                def pv(h, q0, nq, kt, nkt, sl):
                    i = pv_index(l, h, q0)
                    if kt == 0 and i >= 2:
                        lb, hb, qb = pv_owner(i - 2)
                        pe.wait_ge(*at("o_scaled", lb, hb, qb))
                    pe.wait_ge(*at("prob", l, sl))
                    e = h % 2
                    if h < MLA_H:
                        v = vm[:, kt, h // 2, 64 * e:64 * e + P]
                    else:
                        v = vg[:, kt, (h - MLA_H) // 3, 64 * e:64 * e + P]
                    if h == 0 and kt == 0:
                        pe.wait_ge(*at("vm", l, TILES - 1, 1))
                        pe.wait_ge(*at("vg", l, TILES - 1, 1))
                    mm = pe.matmul(pv_banks[i % 2][:, 0:nq], v, prob[sl % 4][:, 0:nq], start=(kt == 0),
                                   stop=(kt == nkt - 1))
                    if kt == nkt - 1:
                        mm.then_inc(*up("pv_filled", l, h, q0))
                    else:
                        mm.then_inc(*up("prob_used", l, sl))

                def flush(keep_n):
                    while len(pend) > keep_n:
                        pv(*pend.pop(0))

                project(0)
                maxes(0)
                values()
                max_rows(0)
                for h in heads:
                    if h + 1 < len(heads):
                        project(h + 1)
                    units = [(q0, nq, kt, nk // P) for q0, nq, nk in qbs(l) for kt in range(nk // P)]
                    for j, (q0, nq, kt, nkt) in enumerate(units):
                        if kt == 0:
                            pe.wait_ge(*at("nm_row", l, h, q0))
                            pe.wait_ge(*at("kh_ones", l, 1))
                        if j == len(units) - 3 and h + 1 < len(heads):
                            maxes(h + 1)
                        p = open_("sc", l, h, q0, kt)
                        close(pe.matmul(p[:, 0:nq], kh[h % 2][0:97, kt * P:kt * P + P], qh[h % 2][0:97, q0:q0 + nq],
                                        start=True, stop=True), "sc", l, h, q0, kt)
                        pend.append((h, q0, nq, kt, nkt, slot[0]))
                        slot[0] += 1
                        flush(2)
                    if h + 1 < len(heads):
                        max_rows(h + 1)
                flush(0)
                mod(l, 4)
                mod(l, 5)
                if l + 1 < DEPTH:
                    for b in range(4):
                        mod(l + 1, b)
                pe.wait_ge(*at("y_attn", l, 11, 256))
                for n in range(2):
                    i = W_POS[("out", l, n)]
                    block_wait(i)
                    for t in out_tiles(l):
                        p = open_("out", l, t, n)
                        for k in range(KD):
                            mm = pe.matmul(p[:], Y[:, k, t * P:t * P + P], W[:, i % 2, k, :], start=(k == 0),
                                           stop=(k == KD - 1))
                        close(mm, "out", l, t, n)
                    block_done(i)


NAMES = ["x", "c", "ctx", "c_ctx", "norm_w", "w_mod", "b_mod", "w_in", "gla_w_a_fwd", "gla_b_a_fwd",
         "gla_w_a_bwd", "gla_b_a_bwd", "gla_norm_w", "mla_q_norm_w", "mla_w_uq", "mla_kv_norm_w", "mla_w_ukv",
         "gqa_q_norm_w", "gqa_k_norm_w", "w_out", "final_norm_w"]


def constants():
    c = np.zeros((P, C_END), np.float32)
    i = np.arange(P)
    c[:, C_ID:C_ID + P] = np.eye(P)
    c[:, C_BLK:C_BLK + P] = (i[:, None] // 64 == i[None, :] // 64)
    c[:, C_PERM:C_PERM + P] = (i[:, None] == (i[None, :] ^ 16))
    for s in range(2):
        c[s::32, C_SEL + s * P:C_SEL + (s + 1) * P] = 1.0
    same = i[:, None] // CHUNK == i[None, :] // CHUNK
    c[:, C_MF:C_MF + P] = same & (i[:, None] <= i[None, :])
    c[:, C_MB:C_MB + P] = same & (i[:, None] >= i[None, :])
    t = np.arange(NL_TOK)
    pos = np.stack([t // 64, t % 64]).astype(np.float32)

    def table(width):
        quarter = width // 4
        f = (np.float32(10000.0) ** (-np.arange(quarter, dtype=np.float32) / np.float32(quarter))).astype(np.float32)
        cos, sin = np.zeros((2, width, NL_TOK), np.float32)
        for d in range(width):
            ang = (pos[d // (width // 2)] * f[d % quarter]).astype(np.float32)
            cos[d] = np.cos(ang)
            sin[d] = np.sin(ang) * (-1.0 if d % (width // 2) < quarter else 1.0)
        return cos, sin

    cos, sin = table(HD)
    c[:, C_COSG:C_COSG + 512] = np.concatenate([cos, cos])
    c[:, C_SING:C_SING + 512] = np.concatenate([sin, sin])
    cos, sin = table(ROPE)
    c[64:96, C_TABM:C_TABM + 512] = cos
    c[96:128, C_TABM:C_TABM + 512] = sin
    return c


def kernel(**inputs):
    import concourse.bacc as bacc
    from concourse.bass_utils import run_bass_kernel_spmd as run

    arrays = {f"in_{n}": np.ascontiguousarray(inputs[n]) for n in NAMES}
    arrays["in_consts"] = constants()

    def trace(tally):
        nc = bacc.Bacc("TRN2", target_bir_lowering=False, num_devices=1)
        aps = {n[3:]: nc.dram_tensor(n, v.shape, mybir.dt.from_np(v.dtype), kind="ExternalInput").ap()
               for n, v in arrays.items()}
        out = nc.dram_tensor("out_0", (1, NL_TOK, D), F32, kind="ExternalOutput").ap()
        build(nc, tally, aps, out)
        return nc

    counted = Tally()
    trace(counted)
    nc = trace(Tally(counted))
    r = run(nc, [arrays], core_ids=[0])
    return r.results[0]["out_0"]
```

```python
from contextlib import ExitStack

import numpy as np

import concourse.bass as bass
from concourse import mybir

ALU = mybir.AluOpType
ACT = mybir.ActivationFunctionType
F32 = mybir.dt.float32
F32R = mybir.dt.float32r
BF16 = mybir.dt.bfloat16
I32 = mybir.dt.int32
AX = mybir.AxisListType.X

P = 128
DEPTH = 2
D = 1024
KD = D // P
NC_TOK, NL_TOK = 256, 512
T = NC_TOK + NL_TOK
TILES = T // P
CTX, LAT = (0, NC_TOK), (NC_TOK, NL_TOK)
EPS = 1e-6
GLA_H, GLA_DK, GLA_DV, CHUNK, RANK = 4, 32, 64, 64, 16
NCHUNK = T // CHUNK
MLA_H, NOPE, ROPE, LORA = 6, 64, 32, 256
GQA_H, HD = 6, 64
MLA_SCALE = (NOPE + ROPE) ** -0.5
GQA_SCALE = HD ** -0.5

GLA_Q, GLA_K, GLA_V, GLA_Z, GLA_A = 0, 128, 256, 512, 768
MLA_CQ, MLA_CKV, MLA_KR, MLA_Z = 800, 1056, 1312, 1344
GQA_Q, GQA_K, GQA_V, GQA_Z = 1728, 2112, 2240, 2368

V_C, V_CC, V_NORM, V_BMOD, V_MQ, V_MKV, V_GBF, V_GBB, V_GN, V_QN, V_KN, V_ROWS = \
    0, 8, 16, 32, 80, 84, 88, 90, 92, 94, 96, 98

C_ID, C_BLK, C_PERM, C_SEL, C_MF, C_MB, C_COSG, C_SING, C_TABM, C_BD, C_END = \
    0, 128, 256, 384, 640, 768, 896, 1408, 1920, 2432, 2436

SEQ = ["small", "cq0", "ga", "cq1", "ga2", "ckv0", "ss0c", "ckv1", "ss0l", "gq0", "ss1c", "gq1", "ss1l",
       "gq2", "gss0c", "gk", "gss0l", "glaq", "gss1c", "glak", "glamul", "gss1l", "tok0", "gss2c", "tok1",
       "gss2l", "tok2", "gss3c", "tok3", "gss3l", "tok4", "kdT", "rope0", "tok5", "rope1", "z0", "rope2",
       "rope3", "z1", "z2", "z3", "ds0", "z4", "z5", "ds1", "z6", "z7"]
IN_BLOCKS = [
    [(1, MLA_CQ, 384)],
    [(0, MLA_CKV + 128, 128), (1, GQA_Q, 384)],
    [(0, GQA_K, 128), (1, GLA_Q, 256)],
    [(0, GLA_V, 256), (2, GQA_V, 128)],
    [(0, GLA_Z, 256), (2, MLA_Z, 256)],
    [(0, MLA_Z + 256, 128), (1, GQA_Z, 384)],
]
SLOT = {"small": (0, 0), "cq0": (0, 1), "cq1": (0, 2), "ckv0": (0, 3), "ckv1": (1, 0), "gq0": (1, 1),
        "gq1": (1, 2), "gq2": (1, 3), "gk": (2, 0), "glaq": (2, 1), "glak": (2, 2),
        **{f"tok{t}": (3, 0) for t in range(TILES)},
        **{f"z{i}": (4 + i // 4, i % 4) for i in range(8)}}
LAST_OF = ["ckv0", "gq2", "glak", "tok5", "z3", "z7"]
RING = 6
MAX_FROM = (3, 2)


def chunks_of(name, layer):
    query = name[0] == "z" or name in ("cq0", "cq1", "gq0", "gq1", "gq2", "glaq", "q")
    return [LAT] if layer == DEPTH - 1 and query else [CTX, LAT]


def norm_chunk(item, name, layer):
    c = CTX if item[-1] == "c" else LAT
    return [c] if c in chunks_of(name, layer) else []


def out_tiles(layer):
    return list(range(2, TILES)) if layer == DEPTH - 1 else list(range(TILES))


def w_blocks():
    seq = [("mod", 0, b) for b in range(4)]
    for l in range(DEPTH):
        seq += [("in", l, b) for b in range(6)] + [("mod", l, 4), ("mod", l, 5)]
        if l + 1 < DEPTH:
            seq += [("mod", l + 1, b) for b in range(4)]
        seq += [("out", l, b) for b in range(2)]
    return seq


W_SEQ = w_blocks()
W_POS = {b: i for i, b in enumerate(W_SEQ)}


class Tally:

    def __init__(self, before=None):
        self.before = before
        self.sems, self.count, self.mark = {}, {}, {}
        self.order, self.freed = [], {}
        self.pv_order, self.pv_freed = [], {}

    def sem(self, stage):
        if stage not in self.sems:
            self.sems[stage] = self.ctx.enter_context(self.nc.semaphore(stage))
            self.count[stage] = 0
        return self.sems[stage]

    def up(self, stage, *step, by=1):
        s = self.sem(stage)
        self.count[stage] += by
        self.mark[(stage, step)] = self.count[stage]
        return s, by

    def dma(self, stage, *step):
        return self.up(stage, *step, by=16)

    def at(self, stage, *step):
        return self.sem(stage), self.before.mark[(stage, step)] if self.before else 1

    def let_go(self, group, stage, *step):
        self.freed.setdefault(group, []).append((stage, step))

    def bank(self, group):
        return self.before.order.index(group) % RING if self.before else 0


def build(nc, tally, a, out):
    up, dma, at, let_go = tally.up, tally.dma, tally.at, tally.let_go
    with ExitStack() as ctx:
        tally.ctx, tally.nc = ctx, nc

        def sb(name, shape, dt=F32):
            return ctx.enter_context(nc.sbuf_tensor(name, shape, dt))

        banks = [ctx.enter_context(nc.psum_tensor(f"bank{i}", [P, 512], F32)) for i in range(RING)]
        pv_banks = [ctx.enter_context(nc.psum_tensor(f"pv{i}", [P, 512], F32)) for i in range(2)]

        def ps(*group):
            return banks[tally.bank(group)]

        hA = sb("hA", [P, KD * T])
        hT = hA[:].rearrange("p (k t) -> p k t", k=KD)
        qh = [hA[:, 2 * i * T:(2 * i + 1) * T] for i in range(2)]
        kh = [hA[:, (2 * i + 1) * T:(2 * i + 2) * T] for i in range(2)]
        prob = [hA[:, 3072 + 512 * i:3584 + 512 * i] for i in range(4)]
        rd, un = hA[:, 5120:5632], hA[:, 5632:6144]
        Ab = [[hA[:, o + 512 * d:o + 512 * d + 512].rearrange("p (h t) -> p h t", h=4) for d in range(2)]
              for o in (3072, 2048)]
        qbd = [hA[:, 4096 + 512 * d:4608 + 512 * d].rearrange("p (h t) -> p h t", h=4) for d in range(2)]
        Sbd = [hA[:, 5120 + 512 * d:5632 + 512 * d].rearrange("p (c h v) -> p c h v", c=2, h=4)
               for d in range(2)]
        W = sb("W", [P, 2, KD, 512])
        XA = sb("XA", [P, TILES * D])
        X = XA[:].rearrange("p (t n) -> p t n", t=TILES)
        Ef = [XA[:, d * T:(d + 1) * T] for d in range(2)]
        ki = [XA[:, (2 + d) * T:(3 + d) * T] for d in range(2)]
        qd = [XA[:, (4 + d) * T:(5 + d) * T] for d in range(2)]
        kd = [XA[:, (6 + d) * T:(7 + d) * T] for d in range(2)]
        kdtok = [e.rearrange("p (t c) -> p t c", t=TILES) for e in Ef]
        St = [e.rearrange("p (n v) -> p n v", n=NCHUNK) for e in Ef]
        vm = XA[:, 0:3456].rearrange("p (t r c) -> p t r c", t=TILES, r=3)
        YA = sb("YA", [P, KD * T])
        xn = YA[:].rearrange("p (t n) -> p t n", t=TILES)
        Y = YA[:].rearrange("p (k t) -> p k t", k=KD)
        glaqk = sb("glaqk", [P, 2, T])
        small = sb("small", [P, T])
        cqkv = sb("cqkv", [P, 4, T])
        CQ = cqkv[:].rearrange("p f t -> p (f t)")
        gate = CQ[:, 0:2048].rearrange("p (s n) -> p s n", s=2)
        fnw = CQ[:, 2048:3072]
        gqk = sb("gqk", [P, 4, T])
        glav = sb("glav", [P, TILES, 256])
        vg = sb("vg", [P, TILES, 2, 192])
        wuq = sb("wuq", [P, 2, MLA_H, 128])
        wukv = sb("wukv", [P, 2, MLA_H, 128])
        wa = sb("wa", [32, 2, P])
        sq = sb("sq", [P, 2, 512])
        rs = sb("rs", [P, 512])
        tz = sb("tz", [P, 2, 512])
        rt = sb("rt", [P, 2, 512])
        cumA = sb("cumA", [P, 2 * T])
        cum = [cumA[:, d * T:(d + 1) * T] for d in range(2)]
        brow = cumA[:, 0:1024].rearrange("p (b n) -> p b n", b=2)
        modrow = cumA[:, 1024:1536]
        qr = sb("qr", [96, T], F32R)
        kr = sb("kr", [96, T], F32R)
        con = sb("con", [P, C_END])
        ident, blk, perm = con[:, C_ID:C_ID + P], con[:, C_BLK:C_BLK + P], con[:, C_PERM:C_PERM + P]
        sel = con[:, C_SEL:C_SEL + 256].rearrange("p (s n) -> p s n", s=2)
        mask = [con[:, c:c + P].bitcast(I32) for c in (C_MF, C_MB)]
        headed = con[:, C_BD:C_BD + GLA_H]
        cosg, sing, tabm = (con[:, c:c + 512] for c in (C_COSG, C_SING, C_TABM))
        ones = sb("ones", [P, P])
        keep = sb("keep", [P, T], BF16)
        eps = sb("eps", [P, 1])
        vec = rt[0:V_ROWS, 0, 0:P]
        vt = sb("vt", [P, V_ROWS])
        vth = sb("vth", [P, V_ROWS])
        ct = sb("ct", [P, 2, 16])
        sc = sb("sc", [P, KD, 32])
        modc = sb("modc", [P, 16, 2])
        mA = sb("mA", [P, KD, 2])
        mB = sb("mB", [P, KD, 2])
        ssx = sb("ssx", [P, TILES])
        rx = sb("rx", [P, TILES])
        dec = sb("dec", [P, 2, NCHUNK])
        on = sq[:, 0, :].rearrange("p (b c) -> p b c", b=2)
        sqo = sq[:, 1, 0:256]
        ss4 = sb("ss4", [P, 2, 4])
        mxp = sb("mxp", [P, TILES, 2])
        nmx = sb("nmx", [P, 2, TILES])
        x_dram = nc.dram_tensor("x_between_layers", [NL_TOK, D], F32, kind="Internal").ap()

        heads = list(range(MLA_H + GQA_H))

        def new_kh(h):
            return h < MLA_H or (h - MLA_H) % 3 != 2

        def new_kr(h):
            return h <= MLA_H or h == MLA_H + 3

        def qbs(l):
            return ([(0, 256, 256)] if l < DEPTH - 1 else []) + [(256, 512, T)]

        def chunk_order(d):
            nctx = NC_TOK // CHUNK
            if d == 0:
                return list(range(NCHUNK))
            return list(range(nctx - 1, -1, -1)) + list(range(NCHUNK - 1, nctx - 1, -1))

        def lat_of(l):
            return slice(NC_TOK, T) if l == DEPTH - 1 else slice(0, T)

        def pv_index(l, h, q0):
            if l == 0:
                return 2 * h + (q0 > 0)
            return 24 + h

        def pv_owner(i):
            return (0, i // 2, (0, 256)[i % 2]) if i < 24 else (1, i - 24, 256)

        def prob_reader(l, slot):
            per = sum(nk // P for _, _, nk in qbs(l))
            h, u = divmod(slot, per)
            if u == per - 1:
                return "pv_filled", l, h, 256
            if l < DEPTH - 1 and u == 1:
                return "pv_filled", l, h, 0
            return "prob_used", l, slot

        block = ctx.enter_context(nc.Block())

        @block.sync
        def _(sp):
            def rows(r, n, src):
                sp.dma_start(vec[r:r + n, :], src).then_inc(*dma("vec_in"))
            rows(V_C, 8, a["c"][0, :].rearrange("(k p) -> k p", p=P))
            rows(V_CC, 8, a["c_ctx"].rearrange("(k p) -> k p", p=P))
            rows(V_NORM, 16, a["norm_w"].rearrange("l (k p) -> (l k) p", p=P))
            rows(V_BMOD, 48, a["b_mod"].rearrange("l (k p) -> (l k) p", p=P))
            rows(V_MQ, 4, a["mla_q_norm_w"].rearrange("l (k p) -> (l k) p", p=P))
            rows(V_MKV, 4, a["mla_kv_norm_w"].rearrange("l (k p) -> (l k) p", p=P))
            rows(V_GBF, 2, a["gla_b_a_fwd"])
            rows(V_GBB, 2, a["gla_b_a_bwd"])
            for r, name in ((V_GN, "gla_norm_w"), (V_QN, "gqa_q_norm_w"), (V_KN, "gqa_k_norm_w")):
                for half in range(2):
                    sp.dma_start(vec[r:r + 2, half * 64:half * 64 + 64], a[name]).then_inc(*dma("vec_in"))
            sp.dma_start(con[:, C_ID:C_ID + P], a["consts"][:, C_ID:C_ID + P]).then_inc(*dma("ident_in"))

            def block_dma(i):
                kind, l, b = W_SEQ[i]
                if i >= 2:
                    sp.wait_ge(*at("filled", "block", i - 2))
                dst = W[:, i % 2]
                stage = f"w_half{i % 2}"
                if kind == "in":
                    src = a["w_in"][l].rearrange("(k p) n -> p k n", p=P)
                    for s, c, n in IN_BLOCKS[b]:
                        sp.dma_start(dst[:, :, s * P:s * P + n], src[:, :, c:c + n]).then_inc(*dma(stage, i))
                    if b == 0:
                        for o, c in ((0, GLA_A), (32, GLA_A), (64, MLA_KR)):
                            sp.dma_start(dst[:, :, o:o + 32], src[:, :, c:c + 32]).then_inc(*dma(stage, i))
                else:
                    src = a["w_mod" if kind == "mod" else "w_out"][l].rearrange("(k p) n -> p k n", p=P)
                    sp.dma_start(dst, src[:, :, 512 * b:512 * b + 512]).then_inc(*dma(stage, i))

            block_dma(0)
            for t in range(TILES):
                src = a["ctx"][0, t * P:(t + 1) * P, :] if t < 2 else a["x"][0, (t - 2) * P:(t - 1) * P, :]
                sp.dma_start(X[:, t, :], src).then_inc(*dma("x_in", 0))
            for i in range(1, 4):
                block_dma(i)
            sp.dma_start(con[:, P:C_END], a["consts"][:, P:C_END]).then_inc(*dma("con_in"))
            for i in range(4, len(W_SEQ)):
                block_dma(i)

        @block.gpsimd
        def _(pool):
            pool.memset(ones[:], 1.0).then_inc(*up("pool_init"))
            pool.memset(eps[:], EPS).then_inc(*up("pool_init"))
            pool.memset(sc[:], 0.0).then_inc(*up("pool_init", "sc"))
            pool.memset(keep[:], 1.0).then_inc(*up("pool_init", "keep1"))
            pool.memset(vg[:, :, :, 64:128], 1.0).then_inc(*up("pool_init"))
            pool.memset(wa[:], 0.0).then_inc(*up("pool_init", "wa"))
            pool.wait_ge(*at("pool_init", "keep1"))
            pool.memset(keep[:, 0:T:CHUNK], 0.0).then_inc(*up("pool_init", "end"))
            def round_k(l, h):
                if new_kr(h):
                    pool.wait_ge(*at("k_in", l, h, LAT))
                    if h < MLA_H:
                        pool.wait_ge(*at("kh_rope", l, h % 2))
                    if h >= 1:
                        pool.wait_ge(*at("filled", "mx", l, h - 1, 256, TILES - 1, 1))
                    elif l:
                        pool.wait_ge(*at("filled", "mx", l - 1, heads[-1], 256, TILES - 1, 1))
                    pool.tensor_copy(kr[:, :], kh[h % 2][0:96, :]).then_inc(*up("round_k", l, h))
                else:
                    tally.mark[("round_k", (l, h))] = tally.count["round_k"]

            for l in range(DEPTH):
                pool.wait_ge(*at("pool_init", "wa"))
                if l:
                    pool.wait_ge(*at("filled", "ga", l - 1, 1, LAT))
                    pool.wait_ge(*at("filled", "kp", l - 1, MLA_H - 1, LAT))
                    pool.wait_ge(*at("filled", "vp", l - 1, TILES - 1))
                pool.dma_start(wa[0:RANK, 0, :], a["gla_w_a_fwd"][l]).then_inc(*dma("wa_in", l))
                pool.dma_start(wa[RANK:2 * RANK, 1, :], a["gla_w_a_bwd"][l]).then_inc(*dma("wa_in", l))
                for f in range(2):
                    pool.dma_start(wuq[:, f, :, 0:96], a["mla_w_uq"][l, f * P:(f + 1) * P, :].rearrange(
                        "p (h c) -> p h c", h=MLA_H)).then_inc(*dma("wu_in", l))
                    pool.dma_start(wukv[:, f, :, :], a["mla_w_ukv"][l, f * P:(f + 1) * P, :].rearrange(
                        "p (h c) -> p h c", h=MLA_H)).then_inc(*dma("wu_in", l))
                i = W_POS[("in", l, 0)]
                pool.wait_ge(*at(f"w_half{i % 2}", i))
                for h in range(2):
                    w = W[:, i % 2, :, 0:P].rearrange("p k (g b s j) -> p k g b s j", g=4, b=2, s=2)
                    pool.tensor_copy(w[:, :, 3, :, 1 - h, :], w[:, :, 2, :, h, :]).then_inc(*up("swap_kr", l))
                pool.wait_ge(*at("wu_in", l))
                for h in range(2):
                    w = wuq[:].rearrange("p f h (g b s j) -> p (f h) g b s j", g=4, b=2, s=2)
                    pool.tensor_copy(w[:, :, 3, :, 1 - h, :], w[:, :, 2, :, h, :]).then_inc(*up("swap_q", l))

                pool.wait_ge(*at("filled", "F", l, "z7", LAT))
                pool.memset(hA[:, 2048:4096], 0.0).then_inc(*up("bd_zero", l))
                def head_ones(b):
                    pool.wait_ge(*at("bd_zero", l))
                    pool.memset(kh[b][96:97, :], 1.0).then_inc(*up("kh_ones", l, b))
                    pool.wait_ge(*at("kr_rope", l))
                    pool.wait_ge(*at("kh_ones", l, b))
                    pool.tensor_copy(kh[b][64:96, :], small[64:96, :]).then_inc(*up("kh_rope", l, b))

                head_ones(0)
                round_k(l, 0)
                pool.wait_ge(*at("con_in"))
                for t in out_tiles(l):
                    for d in range(2):
                        pool.wait_ge(*at("state", l, d))
                        if t - 1 in out_tiles(l):
                            pool.wait_ge(*at("filled", "o", l, t - 1))
                        pool.tensor_tensor(Sbd[d], St[d][:, 2 * t:2 * t + 2, :].unsqueeze(2).broadcast_to([P, 2, 4, 64]),
                                           headed.unsqueeze(1).unsqueeze(3).broadcast_to([P, 2, 4, 64]), ALU.mult)\
                            .then_inc(*up("Sbd", l, t, d))
                pool.wait_ge(*at("filled", "o", l, TILES - 1))
                pool.wait_ge(*at("round_k", l, 0))
                pool.memset(vm[:, :, :, 64:128], 1.0).then_inc(*up("vm_ones", l))
                pool.wait_ge(*at("vm_ones", l))
                head_ones(1)
                for h in heads[1:]:
                    if h in (MLA_H, MLA_H + 1):
                        b = h % 2
                        pool.wait_ge(*at("filled", "sc", l, h - 2, 256, TILES - 1))
                        pool.wait_ge(*at("round_k", l, h - 1))
                        pool.memset(qh[b][64:96, :], 0.0).then_inc(*up("gqa_zero", l, b))
                        pool.memset(kh[b][64:96, :], 0.0).then_inc(*up("gqa_zero", l, b))
                        pool.wait_ge(*at("gqa_zero", l, b))
                    round_k(l, h)
                pool.wait_ge(*at("pv_filled", l, MLA_H - 1, 256))
                if l == 0:
                    for t in range(TILES):
                        src = a["ctx"][0, t * P:(t + 1) * P, :] if t < 2 else a["x"][0, (t - 2) * P:(t - 1) * P, :]
                        pool.dma_start(X[:, t, :], src).then_inc(*dma("x_back", l))
                else:
                    pool.wait_ge(*at("x_saved", l - 1))
                    for t in range(2, TILES):
                        pool.dma_start(X[:, t, :], x_dram[(t - 2) * P:(t - 1) * P, :]).then_inc(*dma("x_back", l))
                pool.wait_ge(*at("kd_exp", l, 1))
                pool.wait_ge(*at("round_k", l, heads[-1]))
                pool.memset(brow, 0.0).then_inc(*up("brow_zero", l))
                pool.wait_ge(*at("brow_zero", l))
                for b in range(2):
                    for s in range(2):
                        pool.dma_start(brow[s:s + 1, b, :], a["b_mod"][l:l + 1, 2048 + 512 * b:2560 + 512 * b])\
                            .then_inc(*dma("brow_in", l))
                if l == DEPTH - 1:
                    pool.dma_start(fnw, a["final_norm_w"].partition_broadcast(P)).then_inc(*dma("fnw_in"))
                if l < DEPTH - 1:
                    for t in range(2, TILES):
                        pool.wait_ge(*at("resid", l, t, 1))
                        pool.dma_start(x_dram[(t - 2) * P:(t - 1) * P, :], X[:, t, :]).then_inc(*dma("x_saved", l))
            for t in range(2, TILES):
                pool.wait_ge(*at("final", t))
                pool.dma_start(out[0, (t - 2) * P:(t - 1) * P, :], xn[:, t, :]).then_inc(*dma("stored"))
            pool.wait_ge(*at("stored"))

        @block.scalar
        def _(act):
            act.wait_ge(*at("vec_turned"))
            act.activation(ct[:, 0, :], vt[:, 0:16], ACT.Tanh, scale=0.5).then_inc(*up("cond_tanh"))
            act.preload_act_table_set("natural_log_exp_and_others")

            def mod_rows(l, b):
                act.wait_ge(*at("filled", "mod", l, b))
                if b < 4:
                    if (l, b) != (0, 0):
                        act.wait_ge(*at("filled", *(("modT", l, b - 1) if b else ("gate", l - 1, 1, 1))))
                    act.activation(modrow, ps("mod", l, b)[:], ACT.Copy).then_inc(*up("modrow", l, b))
                    let_go(("mod", l, b), "modrow", l, b)
                else:
                    for s in range(2):
                        act.wait_ge(*at("filled", "gate", l, b - 4, s))
                        act.activation(gate[:, s, 512 * (b - 4):512 * (b - 3)], ps("gate", l, b - 4, s)[:],
                                       ACT.Copy).then_inc(*up("gate_row", l, b - 4, s))
                        let_go(("gate", l, b - 4, s), "gate_row", l, b - 4, s)

            def rms(stage, group, n, scale, *key):
                act.wait_ge(*at("filled", *group))
                act.activation(rs[:, 0:n], ps(*group)[:, 0:n], ACT.Ln, bias=eps[:, 0:1], scale=scale)\
                    .then_inc(*up(stage + "_ln", *key))
                let_go(group, stage + "_ln", *key)
                act.wait_ge(*at(stage + "_ln", *key))
                act.activation(rs[:, 0:n], rs[:, 0:n], ACT.Exp, scale=-0.5).then_inc(*up(stage + "_rstd", *key))

            def x_rstd(l, tiles):
                if l == 0:
                    act.wait_ge(*at("x_in", 0))
                    act.wait_ge(*at("pool_init", "end"))
                for t in tiles:
                    if 0 < l < DEPTH:
                        act.wait_ge(*at("resid", l - 1, t, 1))
                    elif l == DEPTH:
                        act.wait_ge(*at("resid", l - 1, t, 1))
                    if t > tiles[0]:
                        act.wait_ge(*at("x_sq", l, t - 1))
                    act.activation(tz[:].rearrange("p a b -> p (a b)"), X[:, t, :], ACT.Square,
                                   accum_out=ssx[:, t:t + 1]).then_inc(*up("x_sq", l, t))
                act.wait_ge(*at("x_sq", l, tiles[-1]))
                act.activation(rx[:, tiles[0]:TILES], ssx[:, tiles[0]:TILES], ACT.Ln, bias=eps[:, 0:1],
                               scale=1.0 / D).then_inc(*up("x_ln", l))
                act.wait_ge(*at("x_ln", l))
                act.activation(rx[:, tiles[0]:TILES], rx[:, tiles[0]:TILES], ACT.Exp, scale=-0.5)\
                    .then_inc(*up("x_rstd", l))

            prev_norm = None
            for l in range(DEPTH):
                if l == 0:
                    mod_rows(0, 0)
                x_rstd(l, list(range(TILES)))
                if l == 0:
                    for b in range(1, 4):
                        mod_rows(0, b)
                act.wait_ge(*at("mod_cols", l))
                for k in range(KD):
                    act.wait_ge(*at("filled", "xT", l, k, 0))
                    act.activation(hT[:, k, 0:256], ps("xT", l, k, 0)[:, 0:256], ACT.Identity,
                                   bias=mB[:, k, 1:2], scale=mA[:, k, 1:2]).then_inc(*up("hT_ctx", l, k))
                    let_go(("xT", l, k, 0), "hT_ctx", l, k)
                zi = 0
                for item in SEQ:
                    if item in ("small", "glaq", "glak"):
                        for c in chunks_of(item, l):
                            act.wait_ge(*at("filled", "F", l, item, c))
                            dst = small[:] if item == "small" else glaqk[:, item == "glak", :]
                            act.activation(dst[:, c[0]:sum(c)], ps("F", l, item, c)[:, 0:c[1]], ACT.Copy)\
                                .then_inc(*up("act_proj", l, item, c))
                            let_go(("F", l, item, c), "act_proj", l, item, c)
                    elif item[0] == "z":
                        for c in chunks_of(item, l):
                            act.wait_ge(*at("filled", "F", l, item, c))
                            if zi >= 2:
                                act.wait_ge(*at("zgate", l, zi - 2))
                            act.activation(tz[:, zi % 2, 0:c[1]], ps("F", l, item, c)[:, 0:c[1]], ACT.Tanh,
                                           scale=0.5).then_inc(*up("ztanh", l, zi))
                            zi += 1
                    elif item[:3] == "tok":
                        for t in [int(item[3])]:
                            act.wait_ge(*at("filled", "tok", l, t))
                            act.activation(glav[:, t, :], ps("tok", l, t)[:, 0:256], ACT.Copy)\
                                .then_inc(*up("glav", l, t))
                    elif item == "ga":
                        for d in range(2):
                            col = (V_GBF, V_GBB)[d] + l
                            for c in (CTX, LAT):
                                act.wait_ge(*at("filled", "ga", l, d, c))
                                act.activation(kd[d][:, c[0]:sum(c)], ps("ga", l, d, c)[:, 0:c[1]], ACT.Abs,
                                               bias=vt[:, col:col + 1]).then_inc(*up("g_abs", l, d, c))
                            act.wait_ge(*at("g_abs", l, d, LAT))
                            act.activation(kd[d], kd[d], ACT.Exp, scale=-1.0).then_inc(*up("g_exp", l, d))
                            act.wait_ge(*at("g_exp", l, d))
                            act.activation(kd[d], kd[d], ACT.Ln, bias=ones[:, 0:1]).then_inc(*up("g_ln", l, d))
                    elif item == "ga2":
                        for d in range(2):
                            act.wait_ge(*at("g_cum", l, d))
                            act.activation(Ef[d], cum[d], ACT.Exp, scale=1 / 16).then_inc(*up("g_E", l, d))
                            act.activation(ki[d], cum[d], ACT.Exp, scale=-1 / 16).then_inc(*up("g_Ei", l, d))
                            act.wait_ge(*at("g_rest", l, d))
                            act.activation(kd[d], kd[d], ACT.Exp, scale=1 / 16).then_inc(*up("kd_exp", l, d))
                    elif item[:2] == "ss":
                        j = int(item[2])
                        for c in norm_chunk(item, "q" if j == 0 else "kv", l):
                            act.wait_ge(*at("dve_proj", l, ("cq1", "ckv1")[j], c))
                            if prev_norm:
                                act.wait_ge(*at(*prev_norm))
                            act.activation(sq[:, :, 0:c[1]], cqkv[:, 2 * j:2 * j + 2, c[0]:sum(c)], ACT.Square)\
                                .then_inc(*up("lora_sq", l, j, c))
                            rms("lora", ("ss", l, j, c), c[1], 1.0 / LORA, l, j, c)
                            prev_norm = ("lora_norm", l, j, c)
                    elif item[:3] == "gss":
                        i = int(item[3])
                        name = ("gq0", "gq1", "gq2", "gk")[i]
                        for c in norm_chunk(item, name, l):
                            act.wait_ge(*at("dve_proj", l, name, c))
                            act.wait_ge(*at(*prev_norm))
                            act.activation(sq[:, 0, 0:c[1]], gqk[:, i, c[0]:sum(c)], ACT.Square)\
                                .then_inc(*up("gqa_sq", l, i, c))
                            rms("gqa", ("gss", l, i, c), c[1], 1.0 / HD, l, i, c)
                            prev_norm = ("gqa_norm", l, i, c)
                    elif item == "kdT":
                        for d in range(2):
                            for half in range(2):
                                act.wait_ge(*at("filled", "kdT", l, d, half))
                                act.wait_ge(*at("gla_factors", l, d))
                                act.activation(kdtok[d][:, 3 * half:3 * half + 3, :],
                                               ps("kdT", l, d, half)[:, 0:384].rearrange("p (t c) -> p t c", t=3),
                                               ACT.Copy).then_inc(*up("kdtok", l, d, half))
                                let_go(("kdT", l, d, half), "kdtok", l, d, half)
                act.preload_act_table_set("natural_log_exp_and_others")

                def o_out(t):
                    act.wait_ge(*at("filled", "o", l, t))
                    if t - 2 in out_tiles(l):
                        act.wait_ge(*at("filled", "oT", l, t - 2))
                    act.activation(on[:, t % 2, :], ps("o", l, t)[:, 0:256], ACT.Copy).then_inc(*up("o_copy", l, t))
                    let_go(("o", l, t), "o_copy", l, t)
                    act.wait_ge(*at("o_ss", l, t))
                    act.activation(ss4[:, t % 2, :], ss4[:, t % 2, :], ACT.Ln, bias=eps[:, 0:1],
                                   scale=1.0 / GLA_DV).then_inc(*up("o_ln", l, t))
                    act.wait_ge(*at("o_ln", l, t))
                    act.activation(ss4[:, t % 2, :], ss4[:, t % 2, :], ACT.Exp, scale=-0.5)\
                        .then_inc(*up("o_rstd", l, t))

                def head_in(h):
                    b = h % 2
                    if h >= 2:
                        act.wait_ge(*at("filled", "sc", l, h - 2, 256, TILES - 1))
                    if h < MLA_H:
                        for c in chunks_of("q", l):
                            act.wait_ge(*at("filled", "qp", l, h, c))
                            r = 64 if c == LAT else 96
                            act.activation(qh[b][0:r, c[0]:sum(c)], ps("qp", l, h, c)[0:r, 0:c[1]], ACT.Copy)\
                                .then_inc(*up("q_in", l, h, c))
                            if c == CTX:
                                let_go(("qp", l, h, c), "q_in", l, h, c)
                        for c in (CTX, LAT):
                            act.wait_ge(*at("filled", "kp", l, h, c))
                            act.activation(kh[b][0:64, c[0]:sum(c)], ps("kp", l, h, c)[0:64, 0:c[1]], ACT.Copy)\
                                .then_inc(*up("k_in", l, h, c))
                            let_go(("kp", l, h, c), "k_in", l, h, c)
                    else:
                        g = h - MLA_H
                        act.wait_ge(*at("gqa_rope", l, 3))
                        row, krow = 64 * (g % 2), 64 * (g // 3)
                        if new_kh(h):
                            act.activation(kh[b][0:64, :], gqk[krow:krow + 64, 3, :], ACT.Copy)\
                                .then_inc(*up("k_in", l, h, LAT))
                        act.activation(qh[b][0:64, lat_of(l)], gqk[row:row + 64, g // 2, lat_of(l)], ACT.Copy)\
                            .then_inc(*up("q_in", l, h, LAT))

                def round_q(h):
                    if h >= 1:
                        act.wait_ge(*at("filled", "mx", l, h - 1, 256, TILES - 1, 1))
                    elif l:
                        act.wait_ge(*at("filled", "mx", l - 1, heads[-1], 256, TILES - 1, 1))
                    act.wait_ge(*at("q_in", l, h, LAT))
                    if h < MLA_H:
                        act.wait_ge(*at("q_rope", l, h))
                    elif h < MLA_H + 2:
                        act.wait_ge(*at("gqa_zero", l, h % 2))
                    act.activation(qr[:, lat_of(l)], qh[h % 2][0:96, lat_of(l)], ACT.Copy)\
                        .then_inc(*up("round_q", l, h))

                def recip(h, q0, nq):
                    pv = pv_banks[pv_index(l, h, q0) % 2]
                    r, s = 64 * (h % 2), 64 - 64 * (h % 2)
                    act.wait_ge(*at("pv_filled", l, h, q0))
                    if recips:
                        act.wait_ge(*at("o_scaled", *recips[-1]))
                    act.activation(rd[r:r + 64, 0:nq], pv[s:s + 64, 0:nq], ACT.Ln).then_inc(*up("den_ln", l, h, q0))
                    act.wait_ge(*at("den_ln", l, h, q0))
                    act.activation(rd[r:r + 64, 0:nq], rd[r:r + 64, 0:nq], ACT.Exp, scale=-1.0)\
                        .then_inc(*up("recip", l, h, q0))
                    recips.append((l, h, q0))

                def neg_max(h):
                    for q0, nq, nk in qbs(l):
                        act.wait_ge(*at("filled", "nm", l, h, q0))
                        act.activation(qh[h % 2][96:97, q0:q0 + nq], ps("nm", l, h, q0)[96:97, 0:nq], ACT.Copy)\
                            .then_inc(*up("nm_row", l, h, q0))
                        let_go(("nm", l, h, q0), "nm_row", l, h, q0)

                head_in(0)
                round_q(0)
                for t in out_tiles(l):
                    o_out(t)
                slot = 0
                recips = [] if l == 0 else [(0, heads[-1], 256)]
                neg_max(0)
                for h in heads:
                    todo = [(q0, nq, kt) for q0, nq, nk in qbs(l) for kt in range(nk // P)]
                    more = h + 1 < len(heads)
                    if more:
                        if h == 0:
                            act.wait_ge(*at("filled", "o", l, TILES - 1))
                        head_in(h + 1)
                    if h:
                        recip(h - 1, *qbs(l)[-1][:2])
                    for j, (q0, nq, kt) in enumerate(todo):
                        act.wait_ge(*at("filled", "sc", l, h, q0, kt))
                        if slot >= 4:
                            act.wait_ge(*at(*prob_reader(l, slot - 4)))
                        act.activation(prob[slot % 4][:, 0:nq], ps("sc", l, h, q0, kt)[:, 0:nq], ACT.Exp,
                                       scale=MLA_SCALE if h < MLA_H else GQA_SCALE)\
                            .then_inc(*up("prob", l, slot))
                        let_go(("sc", l, h, q0, kt), "prob", l, slot)
                        slot += 1
                        if j == 0 and more:
                            round_q(h + 1)
                        if j == 3 and len(qbs(l)) == 2:
                            recip(h, *qbs(l)[0][:2])
                    if more:
                        neg_max(h + 1)
                recip(heads[-1], *qbs(l)[-1][:2])
                act.wait_ge(*at("filled", "vp", l, TILES - 1))
                act.wait_ge(*at("filled", "kp", l, MLA_H - 1, LAT))
                for b in (4, 5):
                    mod_rows(l, b)
                if l + 1 < DEPTH:
                    for b in range(4):
                        mod_rows(l + 1, b)
            x_rstd(DEPTH, list(range(2, TILES)))

        @block.vector
        def _(dve):
            dve.wait_ge(*at("filled", "vec"))
            dve.tensor_copy(vt[:], ps("vec")[:, 0:V_ROWS]).then_inc(*up("vec_turned"))
            let_go(("vec",), "vec_turned")
            dve.wait_ge(*at("vec_turned"))
            dve.tensor_scalar(vth[:], vt[:], 0.5, None, ALU.mult).then_inc(*up("vec_half"))
            dve.wait_ge(*at("cond_tanh"))
            dve.wait_ge(*at("vec_half"))
            dve.wait_ge(*at("pool_init", "end"))
            dve.scalar_tensor_tensor(out=sc[:, :, 0:2].rearrange("p k s -> p s k"),
                                     in0=ct[:, 0, :].rearrange("p (s k) -> p s k", s=2), scalar=1.0,
                                     in1=vth[:, 0:16].rearrange("p (s k) -> p s k", s=2),
                                     op0=ALU.add, op1=ALU.mult).then_inc(*up("cond_silu"))

            def mod_cols(l, b):
                dve.wait_ge(*at("filled", "modT", l, b))
                if b == 0 and l:
                    dve.wait_ge(*at("mod_cols", l - 1))
                src = ps("modT", l, b)[:].rearrange("p (f j r) -> p f r j", f=4, j=4)[:, :, 0:2, :]
                dve.tensor_reduce(modc[:, 4 * b:4 * b + 4, :], src, AX, ALU.add).then_inc(*up("mod_sum", l, b))
                let_go(("modT", l, b), "mod_sum", l, b)
                if b == 3:
                    bm = V_BMOD + 24 * l
                    if l:
                        dve.wait_ge(*at("hT_ctx", l - 1, KD - 1))
                    dve.wait_ge(*at("mod_sum", l, 3))
                    dve.tensor_tensor(mB[:], modc[:, 0:8, :], vt[:, bm:bm + 8].unsqueeze(2).broadcast_to([P, 8, 2]),
                                      ALU.add).then_inc(*up("mod_b", l))
                    dve.tensor_tensor(mA[:], modc[:, 8:16, :],
                                      vt[:, bm + 8:bm + 16].unsqueeze(2).broadcast_to([P, 8, 2]),
                                      ALU.add).then_inc(*up("mod_a", l))
                    dve.wait_ge(*at("mod_a", l))
                    nw = V_NORM + 8 * l
                    dve.scalar_tensor_tensor(out=mA[:], in0=mA[:], scalar=1.0,
                                             in1=vt[:, nw:nw + 8].unsqueeze(2).broadcast_to([P, 8, 2]),
                                             op0=ALU.add, op1=ALU.mult).then_inc(*up("mod_cols", l))

            def xhat(l):
                dve.wait_ge(*at("x_rstd", l))
                for t in range(TILES):
                    if l and t == 0:
                        dve.wait_ge(*at("filled", "out", l - 1, out_tiles(l - 1)[-1], 1))
                    dve.tensor_scalar(xn[:, t, :], X[:, t, :], rx[:, t:t + 1], None, ALU.mult)\
                        .then_inc(*up("xhat", l, t))

            mod_cols(0, 0)
            xhat(0)
            for b in range(1, 4):
                mod_cols(0, b)

            for l in range(DEPTH):
                if l:
                    xhat(l)
                dve.wait_ge(*at("mod_cols", l))
                for k in range(KD):
                    dve.wait_ge(*at("filled", "xT", l, k, 1))
                    dve.tensor_scalar(hT[:, k, 256:T], ps("xT", l, k, 1)[:], mA[:, k, 0:1], mB[:, k, 0:1],
                                      ALU.mult, ALU.add).then_inc(*up("hT_lat", l, k))
                    let_go(("xT", l, k, 1), "hT_lat", l, k)
                zi = 0
                for item in SEQ:
                    if item == "small":
                        dve.wait_ge(*at("act_proj", l, "small", LAT))
                        dve.wait_ge(*at("con_in"))
                        lat = slice(256, T)
                        dve.tensor_tensor(rt[64:96, 0, :], small[96:128, lat], tabm[96:128, :], ALU.mult)\
                            .then_inc(*up("kr_mul", l))
                        dve.tensor_tensor(rt[64:96, 1, :], small[64:96, lat], tabm[64:96, :], ALU.mult)\
                            .then_inc(*up("kr_mul", l))
                        dve.wait_ge(*at("kr_mul", l))
                        dve.tensor_tensor(small[64:96, lat], rt[64:96, 0, :], rt[64:96, 1, :], ALU.add)\
                            .then_inc(*up("kr_rope", l))
                    elif item in ("cq0", "cq1", "ckv0", "ckv1", "gq0", "gq1", "gq2", "gk"):
                        i = ("cq0", "cq1", "ckv0", "ckv1", "gq0", "gq1", "gq2", "gk").index(item)
                        for c in chunks_of(item, l):
                            dve.wait_ge(*at("filled", "F", l, item, c))
                            dst = cqkv[:, i, :] if i < 4 else gqk[:, i - 4, :]
                            dve.tensor_copy(dst[:, c[0]:sum(c)], ps("F", l, item, c)[:, 0:c[1]])\
                                .then_inc(*up("dve_proj", l, item, c))
                            let_go(("F", l, item, c), "dve_proj", l, item, c)
                    elif item[0] == "z":
                        for c in chunks_of(item, l):
                            dve.wait_ge(*at("ztanh", l, zi))
                            dve.scalar_tensor_tensor(out=Y[:, int(item[1]), c[0]:sum(c)],
                                                     in0=tz[:, zi % 2, 0:c[1]], scalar=1.0,
                                                     in1=ps("F", l, item, c)[:, 0:c[1]], op0=ALU.add,
                                                     op1=ALU.mult).then_inc(*up("zgate", l, zi))
                            let_go(("F", l, item, c), "zgate", l, zi)
                            zi += 1
                    elif item[:3] == "tok":
                        for t in [int(item[3])]:
                            dve.wait_ge(*at("glav", l, t))
                            src = ps("tok", l, t)[:, 256:384].rearrange("p (g v) -> p g v", g=2)
                            for half in range(2):
                                dve.tensor_copy(vg[:, t, :, 128 * half:128 * half + 64], src)\
                                    .then_inc(*up("vg", l, t, half))
                            let_go(("tok", l, t), "vg", l, t, 1)
                    elif item == "ga":
                        for d in range(2):
                            col = (V_GBF, V_GBB)[d] + l
                            for c in (CTX, LAT):
                                dve.wait_ge(*at("g_abs", l, d, c))
                                dve.tensor_scalar(qd[d][:, c[0]:sum(c)], ps("ga", l, d, c)[:, 0:c[1]],
                                                  vt[:, col:col + 1], 0.0, ALU.add, ALU.min)\
                                    .then_inc(*up("g_min", l, d, c))
                                let_go(("ga", l, d, c), "g_min", l, d, c)
                            dve.wait_ge(*at("g_ln", l, d))
                            dve.wait_ge(*at("g_min", l, d, LAT))
                            dve.tensor_tensor(qd[d], qd[d], kd[d], ALU.subtract).then_inc(*up("g_log", l, d))
                            dve.wait_ge(*at("g_log", l, d))
                            g, o = (qd[d], cum[d]) if d == 0 else (qd[d][:, ::-1], cum[d][:, ::-1])
                            if d == 0:
                                dve.wait_ge(*at("filled", "modT", l, 3))
                            dve.tensor_tensor_scan(o, keep[:], g, 0.0, ALU.mult, ALU.add)\
                                .then_inc(*up("g_cum", l, d))
                    elif item == "ga2":
                        for d in range(2):
                            e = CHUNK - 1 if d == 0 else 0
                            last = cum[d][:, e:T:CHUNK].unsqueeze(2).broadcast_to([P, NCHUNK, CHUNK])
                            dve.wait_ge(*at("g_cum", l, d))
                            dve.tensor_tensor(kd[d].rearrange("p (n c) -> p n c", n=NCHUNK), last,
                                              cum[d].rearrange("p (n c) -> p n c", n=NCHUNK), ALU.subtract)\
                                .then_inc(*up("g_rest", l, d))
                    elif item == "glamul":
                        dve.wait_ge(*at("act_proj", l, "glaq", LAT))
                        dve.wait_ge(*at("act_proj", l, "glak", LAT))
                        for d in range(2):
                            dve.wait_ge(*at("kd_exp", l, d))
                            dve.tensor_tensor(kd[d], kd[d], glaqk[:, 1, :], ALU.mult).then_inc(*up("gla_kd", l, d))
                            dve.tensor_tensor(ki[d], ki[d], glaqk[:, 1, :], ALU.mult).then_inc(*up("gla_ki", l, d))
                            e = CHUNK - 1 if d == 0 else 0
                            dve.tensor_copy(dec[:, d, :], Ef[d][:, e:T:CHUNK]).then_inc(*up("gla_dec", l, d))
                            lat = lat_of(l)
                            dve.scalar_tensor_tensor(out=qd[d][:, lat], in0=glaqk[:, 0, lat],
                                                     scalar=GLA_DK ** -0.5, in1=Ef[d][:, lat], op0=ALU.mult,
                                                     op1=ALU.mult).then_inc(*up("gla_factors", l, d))
                    elif item[:2] == "ss":
                        j = int(item[2])
                        for c in norm_chunk(item, "q" if j == 0 else "kv", l):
                            dve.wait_ge(*at("lora_rstd", l, j, c))
                            for f in range(2):
                                col = (V_MQ, V_MKV)[j] + 2 * l + f
                                v = cqkv[:, 2 * j + f, c[0]:sum(c)]
                                dve.scalar_tensor_tensor(out=v, in0=v, scalar=vt[:, col:col + 1],
                                                         in1=rs[:, 0:c[1]], op0=ALU.mult, op1=ALU.mult)\
                                    .then_inc(*up("lora_norm", l, j, c))
                    elif item[:3] == "gss":
                        i = int(item[3])
                        col = (V_QN if i < 3 else V_KN) + l
                        for c in norm_chunk(item, ("gq0", "gq1", "gq2", "gk")[i], l):
                            dve.wait_ge(*at("gqa_rstd", l, i, c))
                            v = gqk[:, i, c[0]:sum(c)]
                            dve.scalar_tensor_tensor(out=v, in0=v, scalar=vt[:, col:col + 1], in1=rs[:, 0:c[1]],
                                                     op0=ALU.mult, op1=ALU.mult).then_inc(*up("gqa_norm", l, i, c))
                    elif item[:4] == "rope":
                        i = int(item[4])
                        v = gqk[:, i, 256:T]
                        dve.wait_ge(*at("filled", "rope", l, i))
                        dve.wait_ge(*(at("gqa_rope", l, i - 1) if i else at("kr_rope", l)))
                        dve.tensor_tensor(rt[:, 0, :], ps("rope", l, i)[:], sing, ALU.mult)\
                            .then_inc(*up("gqa_sin", l, i))
                        let_go(("rope", l, i), "gqa_sin", l, i)
                        dve.wait_ge(*at("gqa_norm", l, i, LAT))
                        dve.tensor_tensor(v, v, cosg, ALU.mult).then_inc(*up("gqa_cos", l, i))
                        dve.wait_ge(*at("gqa_cos", l, i))
                        dve.tensor_tensor(v, v, rt[:, 0, :], ALU.add).then_inc(*up("gqa_rope", l, i))
                    elif item[:2] == "ds":
                        for d in [int(item[2])]:
                            for par in range(2):
                                dve.wait_ge(*at("filled", "ds", l, d, par))
                            order = chunk_order(d)
                            dve.memset(St[d][:, order[0], :], 0.0).then_inc(*up("state", l, d, order[0]))
                            for n, m in zip(order, order[1:]):
                                dve.wait_ge(*at("state", l, d, n))
                                dve.scalar_tensor_tensor(
                                    out=St[d][:, m, :], in0=St[d][:, n, :], scalar=dec[:, d, n:n + 1],
                                    in1=ps("ds", l, d, n % 2)[:, 64 * (n // 2):64 * (n // 2) + 64],
                                    op0=ALU.mult, op1=ALU.add).then_inc(*up("state", l, d, m))
                            tally.mark[("state", (l, d))] = tally.count["state"]
                            for par in range(2):
                                let_go(("ds", l, d, par), "state", l, d)

                def a_in(t, d):
                    dve.wait_ge(*at("filled", "F", l, "z7", LAT))
                    dve.wait_ge(*at("gla_factors", l, d))
                    if t - 1 in out_tiles(l):
                        dve.wait_ge(*at("filled", "A", l, t - 1, d))
                    dve.tensor_tensor(qbd[d], qd[d][:, t * P:t * P + P].unsqueeze(1).broadcast_to([P, 4, P]),
                                      headed.unsqueeze(2).broadcast_to([P, 4, P]), ALU.mult)\
                        .then_inc(*up("qbd", l, t, d))

                def a_mask(t, d):
                    dve.wait_ge(*at("filled", "A", l, t, d))
                    dve.wait_ge(*at("bd_zero", l))
                    if t - 2 in out_tiles(l):
                        dve.wait_ge(*at("filled", "o", l, t - 2))
                    dve.copy_predicated(Ab[t % 2][d], mask[d].unsqueeze(1).broadcast_to([P, 4, P]),
                                        ps("A", l, t, d)[:].rearrange("p (h t) -> p h t", h=4))\
                        .then_inc(*up("A_masked", l, t, d))
                    let_go(("A", l, t, d), "A_masked", l, t, d)

                def o_square(t):
                    dve.wait_ge(*at("o_copy", l, t))
                    if t - 1 in out_tiles(l):
                        dve.wait_ge(*at("o_ss", l, t - 1))
                    dve.tensor_tensor(sqo, on[:, t % 2, :], on[:, t % 2, :], ALU.mult).then_inc(*up("o_sq", l, t))
                    dve.wait_ge(*at("o_sq", l, t))
                    if t - 2 in out_tiles(l):
                        dve.wait_ge(*at("o_norm", l, t - 2))
                    dve.tensor_reduce(ss4[:, t % 2, :], sqo.rearrange("p (h v) -> p h v", h=4), AX, ALU.add)\
                        .then_inc(*up("o_ss", l, t))

                def o_scale(t):
                    dve.wait_ge(*at("o_rstd", l, t))
                    o4 = on[:, t % 2, :].rearrange("p (h v) -> p h v", h=4)
                    dve.tensor_tensor(o4, o4, ss4[:, t % 2, :].unsqueeze(2).broadcast_to([P, 4, 64]), ALU.mult)\
                        .then_inc(*up("o_norm", l, t))

                def o_gate(t):
                    dve.wait_ge(*at("filled", "oT", l, t))
                    y = Y[:, 0:2, t * P:(t + 1) * P]
                    dve.scalar_tensor_tensor(out=y, in0=ps("oT", l, t)[:, 0:256].rearrange("p (f t) -> p f t", f=2),
                                             scalar=vth[:, V_GN + l:V_GN + l + 1], in1=y, op0=ALU.mult,
                                             op1=ALU.mult).then_inc(*up("y_gla", l, t))
                    let_go(("oT", l, t), "y_gla", l, t)

                def mla_v():
                    dve.wait_ge(*at("vm_ones", l))
                    for t in range(TILES):
                        dve.wait_ge(*at("filled", "vp", l, t))
                        src = ps("vp", l, t)[:, 0:384].rearrange("p (r e v) -> p r e v", r=3, e=2)
                        for e in range(2):
                            dve.tensor_copy(vm[:, t, :, 128 * e:128 * e + 64], src[:, :, e, :])\
                                .then_inc(*up("vm", l, t, e))
                        let_go(("vp", l, t), "vm", l, t, 1)

                def q_rope(h):
                    if h >= MLA_H:
                        return
                    p = ps("qp", l, h, LAT)
                    dve.wait_ge(*at("q_in", l, h, LAT))
                    if h:
                        dve.wait_ge(*at("q_rope", l, h - 1))
                    if l == 0 and h == 0:
                        dve.wait_ge(*at("gqa_rope", l, 3))
                    dve.tensor_tensor(rt[64:96, 0, :], p[96:128, :], tabm[96:128, :], ALU.mult)\
                        .then_inc(*up("q_mul", l, h, 0))
                    dve.tensor_tensor(rt[64:96, 1, :], p[64:96, :], tabm[64:96, :], ALU.mult)\
                        .then_inc(*up("q_mul", l, h, 1))
                    let_go(("qp", l, h, LAT), "q_mul", l, h, 1)
                    dve.wait_ge(*at("q_mul", l, h, 1))
                    if h >= 2:
                        dve.wait_ge(*at("filled", "sc", l, h - 2, 256, TILES - 1))
                    dve.tensor_tensor(qh[h % 2][64:96, 256:T], rt[64:96, 0, :], rt[64:96, 1, :], ALU.add)\
                        .then_inc(*up("q_rope", l, h))

                def maxima(h):
                    if h >= 2:
                        dve.wait_ge(*at("filled", "nm", l, h - 2, 256))
                    elif l:
                        dve.wait_ge(*at("filled", "nm", l - 1, 10 + h, 256))
                    for q0, nq, nk in qbs(l):
                        for t in range(q0 // P, (q0 + nq) // P):
                            if q0 == 0:
                                dve.wait_ge(*at("filled", "mx", l, h, q0, t, 0))
                                dve.tensor_reduce(nmx[:, h % 2, t:t + 1], ps("mx", l, h, q0, t, 0)[:, 0:256], AX,
                                                  ALU.max, negate=True).then_inc(*up("part_max", l, h, q0, t, 0))
                                let_go(("mx", l, h, q0, t, 0), "part_max", l, h, q0, t, 0)
                                continue
                            for half in range(2):
                                dve.wait_ge(*at("filled", "mx", l, h, q0, t, half))
                                if h and t == 2 and not half:
                                    dve.wait_ge(*at("neg_max", l, h - 1))
                                dve.tensor_reduce(mxp[:, t, half:half + 1], ps("mx", l, h, q0, t, half)[:, 0:384],
                                                  AX, ALU.max).then_inc(*up("part_max", l, h, q0, t, half))
                                let_go(("mx", l, h, q0, t, half), "part_max", l, h, q0, t, half)
                    dve.wait_ge(*at("part_max", l, h, 256, TILES - 1, 1))
                    dve.tensor_reduce(nmx[:, h % 2, 2:TILES], mxp[:, 2:TILES, :], AX, ALU.max, negate=True)\
                        .then_inc(*up("neg_max", l, h))

                last_y = [None]

                def normalise(h, q0, nq):
                    pv = pv_banks[pv_index(l, h, q0) % 2]
                    r, s = 64 * (h % 2), 64 - 64 * (h % 2)
                    tile = (2 + h // 2) if h < MLA_H else (5 + (h - MLA_H) // 2)
                    dve.wait_ge(*at("pv_filled", l, h, q0))
                    if last_y[0]:
                        dve.wait_ge(*at("y_attn", *last_y[0]))
                    dve.wait_ge(*at("recip", l, h, q0))
                    dve.scalar_tensor_tensor(out=un[r:r + 64, 0:nq], in0=pv[r:r + 64, 0:nq], scalar=0.5,
                                             in1=rd[r:r + 64, 0:nq], op0=ALU.mult, op1=ALU.mult)\
                        .then_inc(*up("o_scaled", l, h, q0))
                    dve.wait_ge(*at("o_scaled", l, h, q0))
                    y = Y[r:r + 64, tile, q0:q0 + nq]
                    dve.tensor_tensor(y, un[r:r + 64, 0:nq], y, ALU.mult).then_inc(*up("y_attn", l, h, q0))
                    last_y[0] = (l, h, q0)

                tiles = out_tiles(l)
                q_rope(0)
                for t in [tiles[0]]:
                    for d in range(2):
                        a_in(t, d)
                    for d in range(2):
                        a_mask(t, d)
                    for d in range(2):
                        a_in(t + 1, d)
                maxima(0)
                for t in tiles:
                    if t + 1 < TILES:
                        for d in range(2):
                            a_mask(t + 1, d)
                    if t + 2 < TILES:
                        for d in range(2):
                            a_in(t + 2, d)
                    o_square(t)
                    o_scale(t)
                    if t - 1 in tiles:
                        o_gate(t - 1)
                o_gate(TILES - 1)
                mla_v()
                for h in heads:
                    if h + 1 < len(heads):
                        q_rope(h + 1)
                    if h:
                        normalise(h - 1, *qbs(l)[-1][:2])
                    if len(qbs(l)) == 2:
                        normalise(h, *qbs(l)[0][:2])
                    if h + 1 < len(heads):
                        maxima(h + 1)
                normalise(heads[-1], *qbs(l)[-1][:2])

                for b in (0, 1):
                    dve.wait_ge(*at("filled", "mod", l, 4 + b))
                    dve.wait_ge(*at("brow_in", l))
                    dve.wait_ge(*(at("filled", "gate", l, 0, 1) if b else at("filled", "modT", l, 3)))
                    dve.tensor_tensor(modrow, ps("mod", l, 4 + b)[:], brow[:, b, :], ALU.add)\
                        .then_inc(*up("modrow_gate", l, b))
                    let_go(("mod", l, 4 + b), "modrow_gate", l, b)
                if l + 1 < DEPTH:
                    for b in range(4):
                        mod_cols(l + 1, b)
                dve.wait_ge(*at("x_back", l))
                done = []
                for n in range(2):
                    for t in out_tiles(l):
                        s = 1 if t < 2 else 0
                        dve.wait_ge(*at("filled", "out", l, t, n))
                        dve.wait_ge(*at("gate_row", l, n, s))
                        i = len(done)
                        if i >= 2:
                            dve.wait_ge(*at("resid", l, *done[i - 2]))
                        dve.tensor_tensor(rt[:, i % 2, :], ps("out", l, t, n)[:], gate[:, s, 512 * n:512 * n + 512],
                                          ALU.mult).then_inc(*up("gated", l, t, n))
                        let_go(("out", l, t, n), "gated", l, t, n)
                        dve.wait_ge(*at("gated", l, t, n))
                        xs = X[:, t, 512 * n:512 * n + 512]
                        dve.tensor_tensor(xs, xs, rt[:, i % 2, :], ALU.add).then_inc(*up("resid", l, t, n))
                        done.append((t, n))
            dve.wait_ge(*at("x_rstd", DEPTH))
            dve.wait_ge(*at("fnw_in"))
            for t in range(2, TILES):
                dve.scalar_tensor_tensor(out=xn[:, t, :], in0=X[:, t, :], scalar=rx[:, t:t + 1], in1=fnw,
                                         op0=ALU.mult, op1=ALU.mult).then_inc(*up("final", t))

        @block.tensor
        def _(pe):
            def open_(*group):
                tally.order.append(group)
                i = len(tally.order) - 1
                if tally.before and i >= RING:
                    for stage, step in tally.before.freed[tally.before.order[i - RING]]:
                        pe.wait_ge(*at(stage, *step))
                return banks[i % RING]

            def close(mm, *group):
                mm.then_inc(*up("filled", *group))
                mm_group[0] = group

            mm_group = [None]

            def block_done(i):
                tally.mark[("filled", ("block", i))] = tally.count["filled"]

            def block_wait(i):
                pe.wait_ge(*at(f"w_half{i % 2}", i))

            pe.wait_ge(*at("vec_in"))
            pe.wait_ge(*at("ident_in"))
            p = open_("vec")
            close(pe.transpose(p[:, 0:V_ROWS], vec, ident[0:V_ROWS, 0:V_ROWS]), "vec")

            def mod(l, b):
                i = W_POS[("mod", l, b)]
                p = open_("mod", l, b)
                block_wait(i)
                for r in range(2):
                    for j in range(4):
                        k = 4 * r + j
                        mm = pe.matmul(p[32 * j:32 * j + 32, :], sc[:, k, :], W[:, i % 2, k, :], start=(r == 0),
                                       stop=(r == 1), skip_group_check=True)
                close(mm, "mod", l, b)
                block_done(i)
                if b < 4:
                    q = open_("modT", l, b)
                    pe.wait_ge(*at("modrow", l, b))
                    for f in range(4):
                        mm = pe.transpose(q[:, P * f:P * f + P], modrow[:, P * f:P * f + P], ident)
                    close(mm, "modT", l, b)
                else:
                    for s in range(2):
                        q = open_("gate", l, b - 4, s)
                        pe.wait_ge(*at("modrow_gate", l, b - 4))
                        close(pe.matmul(q[:], sel[:, s, :], modrow, start=True, stop=True), "gate", l, b - 4, s)

            pe.wait_ge(*at("cond_silu"))
            for b in range(4):
                mod(0, b)

            for l in range(DEPTH):
                for k in range(KD):
                    for part, tiles in ((0, (0, 1)), (1, (2, 3, 4, 5))):
                        p = open_("xT", l, k, part)
                        for j, t in enumerate(tiles):
                            pe.wait_ge(*at("xhat", l, t))
                            mm = pe.transpose(p[:, P * j:P * j + P], xn[:, t, P * k:P * k + P], ident)
                        close(mm, "xT", l, k, part)
                pe.wait_ge(*at("hT_ctx", l, KD - 1))
                pe.wait_ge(*at("hT_lat", l, KD - 1))
                for item in SEQ:
                    if item in SLOT:
                        b, s = SLOT[item]
                        i = W_POS[("in", l, b)]
                        w = W[:, i % 2]
                        if s == 0 and item not in ("tok1", "tok2", "tok3", "tok4", "tok5"):
                            block_wait(i)
                        if item == "small":
                            pe.wait_ge(*at("swap_kr", l))
                    if item[:3] == "tok":
                        for t in [int(item[3])]:
                            p = open_("tok", l, t)
                            for k in range(KD):
                                mm = pe.matmul(p[:, 0:384], hT[:, k, t * P:(t + 1) * P], w[:, k, 0:384],
                                               start=(k == 0), stop=(k == KD - 1))
                            close(mm, "tok", l, t)
                        if item in LAST_OF:
                            block_done(i)
                    elif item in SLOT:
                        for c in chunks_of(item, l):
                            p = open_("F", l, item, c)
                            for k in range(KD):
                                mm = pe.matmul(p[:, 0:c[1]], w[:, k, s * P:s * P + P], hT[:, k, c[0]:sum(c)],
                                               start=(k == 0), stop=(k == KD - 1))
                            close(mm, "F", l, item, c)
                        if item in LAST_OF:
                            block_done(i)
                    elif item == "ga":
                        pe.wait_ge(*at("wa_in", l))
                        pe.wait_ge(*at("act_proj", l, "small", LAT))
                        for d in range(2):
                            for c in (CTX, LAT):
                                p = open_("ga", l, d, c)
                                close(pe.matmul(p[:, 0:c[1]], wa[:, d, :], small[0:32, c[0]:sum(c)], start=True,
                                                stop=True), "ga", l, d, c)
                    elif item[:2] == "ss":
                        j = int(item[2])
                        for c in norm_chunk(item, "q" if j == 0 else "kv", l):
                            p = open_("ss", l, j, c)
                            pe.wait_ge(*at("lora_sq", l, j, c))
                            for f in range(2):
                                mm = pe.matmul(p[:, 0:c[1]], ones[:], sq[:, f, 0:c[1]], start=(f == 0), stop=(f == 1))
                            close(mm, "ss", l, j, c)
                    elif item[:3] == "gss":
                        i = int(item[3])
                        for c in norm_chunk(item, ("gq0", "gq1", "gq2", "gk")[i], l):
                            p = open_("gss", l, i, c)
                            pe.wait_ge(*at("gqa_sq", l, i, c))
                            close(pe.matmul(p[:, 0:c[1]], blk, sq[:, 0, 0:c[1]], start=True, stop=True),
                                  "gss", l, i, c)
                    elif item[:4] == "rope":
                        i = int(item[4])
                        p = open_("rope", l, i)
                        pe.wait_ge(*at("gqa_norm", l, i, LAT))
                        close(pe.matmul(p[:], perm, gqk[:, i, 256:T], start=True, stop=True), "rope", l, i)
                    elif item == "kdT":
                        for d in range(2):
                            pe.wait_ge(*at("gla_kd", l, d))
                            for half in range(2):
                                p = open_("kdT", l, d, half)
                                for j in range(3):
                                    t = 3 * half + j
                                    mm = pe.transpose(p[:, P * j:P * j + P], kd[d][:, t * P:t * P + P], ident)
                                close(mm, "kdT", l, d, half)
                    elif item[:2] == "ds":
                        pe.wait_ge(*at("glav", l, TILES - 1))
                        for d in [int(item[2])]:
                            pe.wait_ge(*at("kdtok", l, d, 1))
                            for par in range(2):
                                p = open_("ds", l, d, par)
                                r = slice(64 * par, 64 * par + 64)
                                for j in range(TILES):
                                    for h in range(GLA_H):
                                        mm = pe.matmul(p[32 * h:32 * h + 32, 64 * j:64 * j + 64],
                                                       kdtok[d][r, j, 32 * h:32 * h + 32],
                                                       glav[r, j, 64 * h:64 * h + 64], start=True, stop=True)
                                close(mm, "ds", l, d, par)

                def gla_a(t):
                    for d in range(2):
                        p = open_("A", l, t, d)
                        pe.wait_ge(*at("qbd", l, t, d))
                        pe.wait_ge(*at("gla_ki", l, d))
                        close(pe.matmul(p[:], ki[d][:, t * P:t * P + P], qbd[d].rearrange("p h t -> p (h t)"),
                                        start=True, stop=True), "A", l, t, d)

                def gla_o(t):
                    p = open_("o", l, t)
                    for d in range(2):
                        pe.wait_ge(*at("Sbd", l, t, d))
                        for c in range(2):
                            pe.matmul(p[64 * c:64 * c + 64, 0:256], qd[d][:, t * P + 64 * c:t * P + 64 * c + 64],
                                      Sbd[d][:, c].rearrange("p h v -> p (h v)"), start=(d == 0), stop=False,
                                      skip_group_check=True)
                    for d in range(2):
                        pe.wait_ge(*at("A_masked", l, t, d))
                        for h in range(GLA_H):
                            mm = pe.matmul(p[:, 64 * h:64 * h + 64], Ab[t % 2][d][:, h, :], glav[:, t, 64 * h:64 * h + 64],
                                           start=False, stop=(d == 1), skip_group_check=True)
                    close(mm, "o", l, t)

                def gla_t(t):
                    p = open_("oT", l, t)
                    pe.wait_ge(*at("o_norm", l, t))
                    for f in range(2):
                        mm = pe.transpose(p[:, P * f:P * f + P], on[:, t % 2, P * f:P * f + P], ident)
                    close(mm, "oT", l, t)

                def project_q(h):
                    if h >= MLA_H:
                        return
                    if h == 0:
                        pe.wait_ge(*at("swap_q", l))
                        pe.wait_ge(*at("lora_norm", l, 1, LAT))
                    for c in chunks_of("q", l):
                        p = open_("qp", l, h, c)
                        for f in range(2):
                            mm = pe.matmul(p[:, 0:c[1]], wuq[:, f, h, :], cqkv[:, f, c[0]:sum(c)], start=(f == 0),
                                           stop=(f == 1))
                        close(mm, "qp", l, h, c)

                def project_k(h):
                    if h >= MLA_H:
                        return
                    for c in (CTX, LAT):
                        p = open_("kp", l, h, c)
                        for f in range(2):
                            mm = pe.matmul(p[0:64, 0:c[1]], wukv[:, f, h, 0:64], cqkv[:, 2 + f, c[0]:sum(c)],
                                           start=(f == 0), stop=(f == 1))
                        close(mm, "kp", l, h, c)

                def max_groups(h):
                    return [(h, q0, t, half, min(nk, 384)) for q0, nq, nk in qbs(l)
                            for t in range(q0 // P, (q0 + nq) // P) for half in range(-(-nk // 384))]

                def maxes(groups):
                    for h, q0, t, half, n in groups:
                        pe.wait_ge(*at("round_q", l, h))
                        pe.wait_ge(*at("round_k", l, h))
                        p = open_("mx", l, h, q0, t, half)
                        close(pe.matmul(p[:, 0:n], qr[:, t * P:t * P + P], kr[:, n * half:n * half + n],
                                        start=True, stop=True), "mx", l, h, q0, t, half)

                def max_rows(h):
                    pe.wait_ge(*at("neg_max", l, h))
                    for q0, nq, nk in qbs(l):
                        p = open_("nm", l, h, q0)
                        for j in range(nq // P):
                            t = q0 // P + j
                            mm = pe.matmul(p[96:97, P * j:P * j + P], nmx[:, h % 2, t:t + 1], ident, start=True,
                                           stop=True)
                        close(mm, "nm", l, h, q0)

                def values(tiles):
                    for t in tiles:
                        p = open_("vp", l, t)
                        for f in range(2):
                            mm = pe.matmul(p[:, 0:384].rearrange("p (h v) -> p h v", h=MLA_H),
                                           cqkv[:, 2 + f, t * P:t * P + P], wukv[:, f, :, 64:128],
                                           start=(f == 0), stop=(f == 1))
                        close(mm, "vp", l, t)

                slot = [0]
                pend = []

                def pv(h, q0, nq, kt, nkt, sl):
                    i = pv_index(l, h, q0)
                    if kt == 0 and i >= 2:
                        lb, hb, qb = pv_owner(i - 2)
                        pe.wait_ge(*at("o_scaled", lb, hb, qb))
                    pe.wait_ge(*at("prob", l, sl))
                    e = h % 2
                    if h < MLA_H:
                        v = vm[:, kt, h // 2, 64 * e:64 * e + P]
                    else:
                        v = vg[:, kt, (h - MLA_H) // 3, 64 * e:64 * e + P]
                    if h == 0 and kt == 0:
                        pe.wait_ge(*at("vm", l, TILES - 1, 1))
                        pe.wait_ge(*at("vg", l, TILES - 1, 1))
                    mm = pe.matmul(pv_banks[i % 2][:, 0:nq], v, prob[sl % 4][:, 0:nq], start=(kt == 0),
                                   stop=(kt == nkt - 1))
                    if kt == nkt - 1:
                        mm.then_inc(*up("pv_filled", l, h, q0))
                    else:
                        mm.then_inc(*up("prob_used", l, sl))

                def flush(keep_n):
                    while len(pend) > keep_n:
                        pv(*pend.pop(0))

                tiles = out_tiles(l)
                project_q(0)
                project_k(0)
                gla_a(tiles[0])
                maxes(max_groups(0))
                for t in tiles:
                    if t + 1 < TILES:
                        gla_a(t + 1)
                    gla_o(t)
                    if t - 1 in tiles:
                        gla_t(t - 1)
                values(range(3))
                gla_t(TILES - 1)
                values(range(3, TILES))
                for h in heads:
                    if h + 1 < len(heads):
                        project_q(h + 1)
                        groups = max_groups(h + 1)
                    else:
                        groups = []
                    flush(1)
                    max_rows(h)
                    if h + 1 < len(heads):
                        project_k(h + 1)
                    flush(0)
                    units = [(q0, nq, kt, nk // P) for q0, nq, nk in qbs(l) for kt in range(nk // P)]
                    for j, (q0, nq, kt, nkt) in enumerate(units):
                        if kt == 0:
                            pe.wait_ge(*at("nm_row", l, h, q0))
                            pe.wait_ge(*at("kh_ones", l, 1))
                        p = open_("sc", l, h, q0, kt)
                        close(pe.matmul(p[:, 0:nq], kh[h % 2][0:97, kt * P:kt * P + P], qh[h % 2][0:97, q0:q0 + nq],
                                        start=True, stop=True), "sc", l, h, q0, kt)
                        pend.append((h, q0, nq, kt, nkt, slot[0]))
                        slot[0] += 1
                        if j >= MAX_FROM[l]:
                            maxes(groups[:2])
                            groups = groups[2:]
                        flush(2)
                flush(0)
                mod(l, 4)
                mod(l, 5)
                if l + 1 < DEPTH:
                    for b in range(4):
                        mod(l + 1, b)
                pe.wait_ge(*at("y_attn", l, 11, 256))
                for n in range(2):
                    i = W_POS[("out", l, n)]
                    block_wait(i)
                    for t in out_tiles(l):
                        p = open_("out", l, t, n)
                        for k in range(KD):
                            mm = pe.matmul(p[:], Y[:, k, t * P:t * P + P], W[:, i % 2, k, :], start=(k == 0),
                                           stop=(k == KD - 1))
                        close(mm, "out", l, t, n)
                    block_done(i)


NAMES = ["x", "c", "ctx", "c_ctx", "norm_w", "w_mod", "b_mod", "w_in", "gla_w_a_fwd", "gla_b_a_fwd",
         "gla_w_a_bwd", "gla_b_a_bwd", "gla_norm_w", "mla_q_norm_w", "mla_w_uq", "mla_kv_norm_w", "mla_w_ukv",
         "gqa_q_norm_w", "gqa_k_norm_w", "w_out", "final_norm_w"]


def constants():
    c = np.zeros((P, C_END), np.float32)
    i = np.arange(P)
    c[:, C_ID:C_ID + P] = np.eye(P)
    c[:, C_BLK:C_BLK + P] = (i[:, None] // 64 == i[None, :] // 64)
    c[:, C_PERM:C_PERM + P] = (i[:, None] == (i[None, :] ^ 16))
    for s in range(2):
        c[s::32, C_SEL + s * P:C_SEL + (s + 1) * P] = 1.0
    same = i[:, None] // CHUNK == i[None, :] // CHUNK
    c[:, C_MF:C_MF + P] = same & (i[:, None] <= i[None, :])
    c[:, C_MB:C_MB + P] = same & (i[:, None] >= i[None, :])
    c[:, C_BD:C_BD + GLA_H] = i[:, None] // GLA_DK == np.arange(GLA_H)[None, :]
    t = np.arange(NL_TOK)
    pos = np.stack([t // 64, t % 64]).astype(np.float32)

    def table(width):
        quarter = width // 4
        f = (np.float32(10000.0) ** (-np.arange(quarter, dtype=np.float32) / np.float32(quarter))).astype(np.float32)
        cos, sin = np.zeros((2, width, NL_TOK), np.float32)
        for d in range(width):
            ang = (pos[d // (width // 2)] * f[d % quarter]).astype(np.float32)
            cos[d] = np.cos(ang)
            sin[d] = np.sin(ang) * (-1.0 if d % (width // 2) < quarter else 1.0)
        return cos, sin

    cos, sin = table(HD)
    c[:, C_COSG:C_COSG + 512] = np.concatenate([cos, cos])
    c[:, C_SING:C_SING + 512] = np.concatenate([sin, sin])
    cos, sin = table(ROPE)
    c[64:96, C_TABM:C_TABM + 512] = cos
    c[96:128, C_TABM:C_TABM + 512] = sin
    return c


def kernel(**inputs):
    import concourse.bacc as bacc
    from concourse.bass_utils import run_bass_kernel_spmd as run

    arrays = {f"in_{n}": np.ascontiguousarray(inputs[n]) for n in NAMES}
    arrays["in_consts"] = constants()

    def trace(tally):
        nc = bacc.Bacc("TRN2", target_bir_lowering=False, num_devices=1)
        aps = {n[3:]: nc.dram_tensor(n, v.shape, mybir.dt.from_np(v.dtype), kind="ExternalInput").ap()
               for n, v in arrays.items()}
        out = nc.dram_tensor("out_0", (1, NL_TOK, D), F32, kind="ExternalOutput").ap()
        build(nc, tally, aps, out)
        return nc

    counted = Tally()
    trace(counted)
    nc = trace(Tally(counted))
    r = run(nc, [arrays], core_ids=[0])
    return r.results[0]["out_0"]
```

```python
from contextlib import ExitStack

import numpy as np

import concourse.bass as bass
from concourse import mybir

ALU = mybir.AluOpType
ACT = mybir.ActivationFunctionType
F32 = mybir.dt.float32
F32R = mybir.dt.float32r
BF16 = mybir.dt.bfloat16
I32 = mybir.dt.int32
AX = mybir.AxisListType.X

P = 128
DEPTH = 2
D = 1024
KD = D // P
NC_TOK, NL_TOK = 256, 512
T = NC_TOK + NL_TOK
TILES = T // P
CTX, LAT = (0, NC_TOK), (NC_TOK, NL_TOK)
EPS = 1e-6
GLA_H, GLA_DK, GLA_DV, CHUNK, RANK = 4, 32, 64, 64, 16
NCHUNK = T // CHUNK
MLA_H, NOPE, ROPE, LORA = 6, 64, 32, 256
GQA_H, HD = 6, 64
MLA_SCALE = (NOPE + ROPE) ** -0.5
GQA_SCALE = HD ** -0.5

GLA_Q, GLA_K, GLA_V, GLA_Z, GLA_A = 0, 128, 256, 512, 768
MLA_CQ, MLA_CKV, MLA_KR, MLA_Z = 800, 1056, 1312, 1344
GQA_Q, GQA_K, GQA_V, GQA_Z = 1728, 2112, 2240, 2368

V_C, V_CC, V_NORM, V_BMOD, V_MQ, V_MKV, V_GBF, V_GBB, V_GN, V_QN, V_KN, V_ROWS = \
    0, 8, 16, 32, 80, 84, 88, 90, 92, 94, 96, 98

C_ID, C_BLK, C_PERM, C_SEL, C_MF, C_MB, C_COSG, C_SING, C_TABM, C_BD, C_END = \
    0, 128, 256, 384, 640, 768, 896, 1408, 1920, 2432, 2436

SEQ = ["small", "cq0", "ga", "cq1", "ga2", "ckv0", "ss0c", "ckv1", "ss0l", "gq0", "ss1c", "gq1", "ss1l",
       "gsq0c", "gq2", "gss0c", "gsq0l", "gk", "gss0l", "gsq1c", "glaq", "gss1c", "gsq1l", "glak", "glamul",
       "gss1l", "gsq2c", "tok0", "gss2c", "gsq2l", "tok1", "gss2l", "gsq3c", "tok2", "gss3c", "gsq3l", "tok3",
       "gss3l", "tok4", "kdT", "rope0", "tok5", "rope1", "z0", "rope2", "rope3", "z1", "z2", "z3", "ds0", "z4",
       "z5", "ds1", "z6", "z7"]
IN_BLOCKS = [
    [(1, MLA_CQ, 384)],
    [(0, MLA_CKV + 128, 128), (1, GQA_Q, 384)],
    [(0, GQA_K, 128), (1, GLA_Q, 256)],
    [(0, GLA_V, 256), (2, GQA_V, 128)],
    [(0, GLA_Z, 256), (2, MLA_Z, 256)],
    [(0, MLA_Z + 256, 128), (1, GQA_Z, 384)],
]
SLOT = {"small": (0, 0), "cq0": (0, 1), "cq1": (0, 2), "ckv0": (0, 3), "ckv1": (1, 0), "gq0": (1, 1),
        "gq1": (1, 2), "gq2": (1, 3), "gk": (2, 0), "glaq": (2, 1), "glak": (2, 2),
        **{f"tok{t}": (3, 0) for t in range(TILES)},
        **{f"z{i}": (4 + i // 4, i % 4) for i in range(8)}}
LAST_OF = ["ckv0", "gq2", "glak", "tok5", "z3", "z7"]
RING = 6
MAX_FROM = (3, 2)


def chunks_of(name, layer):
    query = name[0] == "z" or name in ("cq0", "cq1", "gq0", "gq1", "gq2", "glaq", "q")
    return [LAT] if layer == DEPTH - 1 and query else [CTX, LAT]


def norm_chunk(item, name, layer):
    c = CTX if item[-1] == "c" else LAT
    return [c] if c in chunks_of(name, layer) else []


def gss_order(layer):
    return [(int(item[3]), c) for item in SEQ if item[:3] == "gss"
            for c in norm_chunk(item, ("gq0", "gq1", "gq2", "gk")[int(item[3])], layer)]


def out_tiles(layer):
    return list(range(2, TILES)) if layer == DEPTH - 1 else list(range(TILES))


def mod_of_head(l, h):
    if 1 <= h <= 4 and l + 1 < DEPTH:
        return "mod", l + 1, h - 1
    if h in (7, 8):
        return "mod", l, h - 3
    return None


def w_blocks():
    seq = [("mod", 0, b) for b in range(4)]
    for l in range(DEPTH):
        seq += [("in", l, b) for b in range(6)] + [mod_of_head(l, h) for h in range(12) if mod_of_head(l, h)]
        seq += [("out", l, b) for b in range(2)]
    return seq


W_SEQ = w_blocks()
W_POS = {b: i for i, b in enumerate(W_SEQ)}


class Tally:

    def __init__(self, before=None):
        self.before = before
        self.sems, self.count, self.mark = {}, {}, {}
        self.order, self.freed = [], {}
        self.pv_order, self.pv_freed = [], {}

    def sem(self, stage):
        if stage not in self.sems:
            self.sems[stage] = self.ctx.enter_context(self.nc.semaphore(stage))
            self.count[stage] = 0
        return self.sems[stage]

    def up(self, stage, *step, by=1):
        s = self.sem(stage)
        self.count[stage] += by
        self.mark[(stage, step)] = self.count[stage]
        return s, by

    def dma(self, stage, *step):
        return self.up(stage, *step, by=16)

    def at(self, stage, *step):
        return self.sem(stage), self.before.mark[(stage, step)] if self.before else 1

    def let_go(self, group, stage, *step):
        self.freed.setdefault(group, []).append((stage, step))

    def bank(self, group):
        return self.before.order.index(group) % RING if self.before else 0


def build(nc, tally, a, out):
    up, dma, at, let_go = tally.up, tally.dma, tally.at, tally.let_go
    with ExitStack() as ctx:
        tally.ctx, tally.nc = ctx, nc

        def sb(name, shape, dt=F32):
            return ctx.enter_context(nc.sbuf_tensor(name, shape, dt))

        def twice(name, shape):
            with nc.sbuf_tensor(name + "_parts", shape, F32R) as parts:
                pass
            return sb(name, shape), parts

        banks = [ctx.enter_context(nc.psum_tensor(f"bank{i}", [P, 512], F32)) for i in range(RING)]
        pv_banks = [ctx.enter_context(nc.psum_tensor(f"pv{i}", [P, 512], F32)) for i in range(2)]

        def ps(*group):
            return banks[tally.bank(group)]

        hA, y_hi = twice("hA", [P, KD * T])
        hT = hA[:].rearrange("p (k t) -> p k t", k=KD)
        qh = [hA[:, 2 * i * T:(2 * i + 1) * T] for i in range(2)]
        kh = [hA[:, (2 * i + 1) * T:(2 * i + 2) * T] for i in range(2)]
        prob = [hA[:, 3072 + 512 * i:3584 + 512 * i] for i in range(4)]
        rd, un = hA[:, 5120:5632], hA[:, 5632:6144]
        Ab = [[hA[:, o + 512 * d:o + 512 * d + 512].rearrange("p (h t) -> p h t", h=4) for d in range(2)]
              for o in (3072, 2048)]
        qbd = [hA[:, 4096 + 512 * d:4608 + 512 * d].rearrange("p (h t) -> p h t", h=4) for d in range(2)]
        Sbd = [hA[:, 5120 + 512 * d:5632 + 512 * d].rearrange("p (c h v) -> p c h v", c=2, h=4)
               for d in range(2)]
        W, w_lo = twice("W", [P, 2, KD, 512])
        XA = sb("XA", [P, TILES * D])
        X = XA[:].rearrange("p (t n) -> p t n", t=TILES)
        Ef = [XA[:, d * T:(d + 1) * T] for d in range(2)]
        ki = [XA[:, (2 + d) * T:(3 + d) * T] for d in range(2)]
        qd = [XA[:, (4 + d) * T:(5 + d) * T] for d in range(2)]
        kd = [XA[:, (6 + d) * T:(7 + d) * T] for d in range(2)]
        kdtok = [e.rearrange("p (t c) -> p t c", t=TILES) for e in Ef]
        St = [e.rearrange("p (n v) -> p n v", n=NCHUNK) for e in Ef]
        vm = XA[:, 0:3456].rearrange("p (t r c) -> p t r c", t=TILES, r=3)
        YA, y_lo = twice("YA", [P, KD * T])
        xn = YA[:].rearrange("p (t n) -> p t n", t=TILES)
        Y = YA[:].rearrange("p (k t) -> p k t", k=KD)
        glaqk, glaqk_parts = twice("glaqk", [P, 2, T])
        small = sb("small", [P, T])
        cqkv = sb("cqkv", [P, 4, T])
        CQ = cqkv[:].rearrange("p f t -> p (f t)")
        gate = CQ[:, 0:2048].rearrange("p (s n) -> p s n", s=2)
        fnw = CQ[:, 2048:3072]
        gqk, gqk_parts = twice("gqk", [P, 4, T])
        glav, glav_parts = twice("glav", [P, TILES, 256])
        vg = sb("vg", [P, TILES, 2, 192])
        wuq, wuq_parts = twice("wuq", [P, 2, MLA_H, 128])
        wukv, wukv_parts = twice("wukv", [P, 2, MLA_H, 128])
        wa = sb("wa", [32, 2, P])
        sq, sq_parts = twice("sq", [P, 2, 512])
        rs = sb("rs", [P, 512])
        tz = sb("tz", [P, 2, 512])
        rt = sb("rt", [P, 2, 512])
        cumA = sb("cumA", [P, 2 * T])
        cum = [cumA[:, d * T:(d + 1) * T] for d in range(2)]
        brow = cumA[:, 0:1024].rearrange("p (b n) -> p b n", b=2)
        modrow = cumA[:, 1024:1536]
        rounded = sb("rounded", [P, 2, T], F32R)
        qr, kr = rounded[0:96, 0, :], rounded[0:96, 1, :]
        con = sb("con", [P, C_END])
        ident, blk, perm = con[:, C_ID:C_ID + P], con[:, C_BLK:C_BLK + P], con[:, C_PERM:C_PERM + P]
        sel = con[:, C_SEL:C_SEL + 256].rearrange("p (s n) -> p s n", s=2)
        mask = [con[:, c:c + P].bitcast(I32) for c in (C_MF, C_MB)]
        headed = con[:, C_BD:C_BD + GLA_H]
        cosg, sing, tabm = (con[:, c:c + 512] for c in (C_COSG, C_SING, C_TABM))
        ones = sb("ones", [P, P])
        keep = sb("keep", [P, T], BF16)
        eps = sb("eps", [P, 1])
        vec = rt[0:V_ROWS, 0, 0:P]
        vt = sb("vt", [P, V_ROWS])
        vth = sb("vth", [P, V_ROWS])
        ct = sb("ct", [P, 2, 16])
        sc = sb("sc", [P, KD, 32])
        modc = sb("modc", [P, 16, 2])
        mA = sb("mA", [P, KD, 2])
        mB = sb("mB", [P, KD, 2])
        ssx = sb("ssx", [P, TILES])
        rx = sb("rx", [P, TILES])
        dec = sb("dec", [P, 2, NCHUNK])
        on = sq[:, 0, :].rearrange("p (b c) -> p b c", b=2)
        sqo = sq[:, 1, 0:256]
        ss4 = sb("ss4", [P, 2, 4])
        mxp = sb("mxp", [P, TILES, 2])
        nmx = sb("nmx", [P, 2, TILES])
        x_dram = nc.dram_tensor("x_between_layers", [NL_TOK, D], F32, kind="Internal").ap()

        q_both, q_high = ([y_hi[:, (2 * i + o) * T:(2 * i + o + 1) * T] for i in range(2)] for o in range(2))
        k_twice, k_low = ([e[:].rearrange("p f h c -> p (f h c)")[:, o * T:(o + 1) * T]
                           for e in (wuq_parts, wukv_parts)] for o in range(2))
        y_hi, y_lo = (e[:].rearrange("p (k t) -> p k t", k=KD) for e in (y_hi, y_lo))

        def pieces(*tensors):
            return [e[:, c:c + 512] for e in tensors for c in range(0, e.shape[1], 512)]

        w_hi = [pieces(gqk_parts[:].rearrange("p f t -> p (f t)"), glav_parts[:].rearrange("p t c -> p (t c)")),
                pieces(rounded[:].rearrange("p f t -> p (f t)"), glaqk_parts[:].rearrange("p f t -> p (f t)"),
                       sq_parts[:].rearrange("p a b -> p (a b)"))]

        heads = list(range(MLA_H + GQA_H))

        def qbs(l):
            return ([(0, 256, 256)] if l < DEPTH - 1 else []) + [(256, 512, T)]

        def chunk_order(d):
            nctx = NC_TOK // CHUNK
            if d == 0:
                return list(range(NCHUNK))
            return list(range(nctx - 1, -1, -1)) + list(range(NCHUNK - 1, nctx - 1, -1))

        def lat_of(l):
            return slice(NC_TOK, T) if l == DEPTH - 1 else slice(0, T)

        def pv_index(l, h, q0):
            if l == 0:
                return 2 * h + (q0 > 0)
            return 24 + h

        def pv_owner(i):
            return (0, i // 2, (0, 256)[i % 2]) if i < 24 else (1, i - 24, 256)

        def prob_reader(l, slot):
            per = sum(nk // P for _, _, nk in qbs(l))
            h, u = divmod(slot, per)
            if u == per - 1:
                return "pv_filled", l, h, 256
            if l < DEPTH - 1 and u == 1:
                return "pv_filled", l, h, 0
            return "prob_used", l, slot

        block = ctx.enter_context(nc.Block())

        @block.sync
        def _(sp):
            def block_dma(i):
                kind, l, b = W_SEQ[i]
                if i >= 2:
                    sp.wait_ge(*at("filled", "block", i - 2))
                dst = W[:, i % 2]
                stage = f"w_half{i % 2}"
                if kind == "in":
                    src = a["w_in"][l].rearrange("(k p) n -> p k n", p=P)
                    for s, c, n in IN_BLOCKS[b]:
                        sp.dma_start(dst[:, :, s * P:s * P + n], src[:, :, c:c + n]).then_inc(*dma(stage, i))
                    if b == 0:
                        for o, c in ((0, GLA_A), (32, GLA_A), (64, MLA_KR)):
                            sp.dma_start(dst[:, :, o:o + 32], src[:, :, c:c + 32]).then_inc(*dma(stage, i))
                else:
                    src = a["w_mod" if kind == "mod" else "w_out"][l].rearrange("(k p) n -> p k n", p=P)
                    sp.dma_start(dst, src[:, :, 512 * b:512 * b + 512]).then_inc(*dma(stage, i))

            def rows(r, n, src):
                sp.dma_start(vec[r:r + n, :], src).then_inc(*dma("vec_in"))
            block_dma(0)
            rows(V_C, 8, a["c"][0, :].rearrange("(k p) -> k p", p=P))
            rows(V_CC, 8, a["c_ctx"].rearrange("(k p) -> k p", p=P))
            rows(V_NORM, 16, a["norm_w"].rearrange("l (k p) -> (l k) p", p=P))
            rows(V_BMOD, 48, a["b_mod"].rearrange("l (k p) -> (l k) p", p=P))
            rows(V_MQ, 4, a["mla_q_norm_w"].rearrange("l (k p) -> (l k) p", p=P))
            rows(V_MKV, 4, a["mla_kv_norm_w"].rearrange("l (k p) -> (l k) p", p=P))
            rows(V_GBF, 2, a["gla_b_a_fwd"])
            rows(V_GBB, 2, a["gla_b_a_bwd"])
            for r, name in ((V_GN, "gla_norm_w"), (V_QN, "gqa_q_norm_w"), (V_KN, "gqa_k_norm_w")):
                for half in range(2):
                    sp.dma_start(vec[r:r + 2, half * 64:half * 64 + 64], a[name]).then_inc(*dma("vec_in"))
            sp.dma_start(con[:, C_ID:C_ID + P], a["consts"][:, C_ID:C_ID + P]).then_inc(*dma("ident_in"))

            for t in range(TILES):
                src = a["ctx"][0, t * P:(t + 1) * P, :] if t < 2 else a["x"][0, (t - 2) * P:(t - 1) * P, :]
                sp.dma_start(X[:, t, :], src).then_inc(*dma("x_in", 0))
            for i in range(1, 4):
                block_dma(i)
            sp.dma_start(con[:, P:C_END], a["consts"][:, P:C_END]).then_inc(*dma("con_in"))
            for i in range(4, len(W_SEQ)):
                block_dma(i)

        @block.gpsimd
        def _(pool):
            pool.memset(ones[:], 1.0).then_inc(*up("pool_init"))
            pool.memset(eps[:], EPS).then_inc(*up("pool_init"))
            pool.memset(sc[:], 0.0).then_inc(*up("pool_init", "sc"))
            pool.memset(keep[:], 1.0).then_inc(*up("pool_init", "keep1"))
            pool.memset(vg[:, :, :, 64:128], 1.0).then_inc(*up("pool_init"))
            pool.memset(wa[:], 0.0).then_inc(*up("pool_init", "wa"))
            pool.wait_ge(*at("pool_init", "keep1"))
            pool.memset(keep[:, 0:T:CHUNK], 0.0).then_inc(*up("pool_init", "end"))
            def round_k(l, h):
                pool.wait_ge(*at("k_in", l, h, LAT))
                pool.wait_ge(*at("kh_rope", l, h % 2))
                if h >= 1:
                    pool.wait_ge(*at("filled", "mx", l, h - 1, 256, TILES - 1, 1))
                elif l:
                    pool.wait_ge(*at("filled", "out", l - 1, TILES - 1, 1))
                pool.tensor_copy(kr, kh[h % 2][0:96, :]).then_inc(*up("round_k", l, h))

            for l in range(DEPTH):
                pool.wait_ge(*at("pool_init", "wa"))
                if l:
                    pool.wait_ge(*at("filled", "ga", l - 1, 1, LAT))
                    pool.wait_ge(*at("filled", "sc", l - 1, heads[-1], 256, TILES - 1))
                pool.dma_start(wa[0:RANK, 0, :], a["gla_w_a_fwd"][l]).then_inc(*dma("wa_in", l))
                pool.dma_start(wa[RANK:2 * RANK, 1, :], a["gla_w_a_bwd"][l]).then_inc(*dma("wa_in", l))
                for f in range(2):
                    pool.dma_start(wuq[:, f, :, 0:96], a["mla_w_uq"][l, f * P:(f + 1) * P, :].rearrange(
                        "p (h c) -> p h c", h=MLA_H)).then_inc(*dma("wu_in", l))
                    pool.dma_start(wukv[:, f, :, :], a["mla_w_ukv"][l, f * P:(f + 1) * P, :].rearrange(
                        "p (h c) -> p h c", h=MLA_H)).then_inc(*dma("wu_in", l))
                i = W_POS[("in", l, 0)]
                pool.wait_ge(*at(f"w_half{i % 2}", i))
                for h in range(2):
                    w = W[:, i % 2, :, 0:P].rearrange("p k (g b s j) -> p k g b s j", g=4, b=2, s=2)
                    pool.tensor_copy(w[:, :, 3, :, 1 - h, :], w[:, :, 2, :, h, :]).then_inc(*up("swap_kr", l))
                pool.wait_ge(*at("wu_in", l))
                for h in range(2):
                    w = wuq[:].rearrange("p f h (g b s j) -> p (f h) g b s j", g=4, b=2, s=2)
                    pool.tensor_copy(w[:, :, 3, :, 1 - h, :], w[:, :, 2, :, h, :]).then_inc(*up("swap_q", l))

                pool.wait_ge(*at("filled", "F", l, "z7", LAT))
                pool.memset(hA[:, 2048:4096], 0.0).then_inc(*up("bd_zero", l))
                def head_ones(b):
                    pool.wait_ge(*at("bd_zero", l))
                    pool.memset(kh[b][96:97, :], 1.0).then_inc(*up("kh_ones", l, b))
                    pool.wait_ge(*at("kr_rope", l))
                    pool.wait_ge(*at("kh_ones", l, b))
                    pool.tensor_copy(kh[b][64:96, :], small[64:96, :]).then_inc(*up("kh_rope", l, b))

                head_ones(0)
                round_k(l, 0)
                pool.wait_ge(*at("con_in"))
                for t in out_tiles(l):
                    for d in range(2):
                        pool.wait_ge(*at("state", l, d))
                        if t - 1 in out_tiles(l):
                            pool.wait_ge(*at("filled", "o", l, t - 1))
                        pool.tensor_tensor(Sbd[d], St[d][:, 2 * t:2 * t + 2, :].unsqueeze(2).broadcast_to([P, 2, 4, 64]),
                                           headed.unsqueeze(1).unsqueeze(3).broadcast_to([P, 2, 4, 64]), ALU.mult)\
                            .then_inc(*up("Sbd", l, t, d))
                pool.wait_ge(*at("filled", "o", l, TILES - 1))
                pool.wait_ge(*at("round_k", l, 0))
                pool.memset(vm[:, :, :, 64:128], 1.0).then_inc(*up("vm_ones", l))
                pool.wait_ge(*at("vm_ones", l))
                head_ones(1)
                pool.wait_ge(*at("kd_exp", l, 1))
                if l:
                    pool.wait_ge(*at("modrow_gate", l - 1, 1))
                pool.wait_ge(*at("kh_rope", l, 1))
                pool.memset(brow, 0.0).then_inc(*up("brow_zero", l))
                pool.wait_ge(*at("brow_zero", l))
                for b in range(2):
                    for s in range(2):
                        pool.dma_start(brow[s:s + 1, b, :], a["b_mod"][l:l + 1, 2048 + 512 * b:2560 + 512 * b])\
                            .then_inc(*dma("brow_in", l))
                for h in heads[1:MLA_H]:
                    round_k(l, h)
                pool.wait_ge(*at("filled", "kp", l, MLA_H - 1, LAT))
                pool.wait_ge(*at("round_k", l, MLA_H - 1))
                for g in range(2):
                    if g:
                        pool.wait_ge(*at("k_pad", l, 0, 1))
                    pool.memset(k_low[g][64:96, :].bitcast(F32), 0.0).then_inc(*up("k_pad", l, g, 0))
                    pool.memset(k_low[g][96:97, :].bitcast(F32), 1.0).then_inc(*up("k_pad", l, g, 1))
                pool.wait_ge(*at("k_pad", l, 1, 1))
                for b in range(2):
                    pool.wait_ge(*at("filled", "sc", l, MLA_H + b - 2, 256, TILES - 1))
                    pool.memset(q_high[b][64:96, :].bitcast(F32), 0.0).then_inc(*up("q_pad", l, b))
                pool.wait_ge(*at("q_pad", l, 1))
                for n in range(2):
                    i = W_POS[("out", l, n)]
                    for k in range(KD):
                        pool.wait_ge(*at("w_hi", l, n, k))
                        pool.tensor_tensor(w_lo[:, i % 2, k, :], W[:, i % 2, k, :], w_hi[n][k].bitcast(F32),
                                           ALU.subtract).then_inc(*up("w_lo", l, n, k))
                pool.wait_ge(*at("pv_filled", l, MLA_H - 1, 256))
                if l == 0:
                    for t in range(TILES):
                        src = a["ctx"][0, t * P:(t + 1) * P, :] if t < 2 else a["x"][0, (t - 2) * P:(t - 1) * P, :]
                        pool.dma_start(X[:, t, :], src).then_inc(*dma("x_back", l))
                else:
                    pool.wait_ge(*at("x_saved", l - 1))
                    for t in range(2, TILES):
                        pool.dma_start(X[:, t, :], x_dram[(t - 2) * P:(t - 1) * P, :]).then_inc(*dma("x_back", l))
                if l == DEPTH - 1:
                    pool.dma_start(fnw, a["final_norm_w"].partition_broadcast(P)).then_inc(*dma("fnw_in"))
                if l < DEPTH - 1:
                    for t in range(2, TILES):
                        pool.wait_ge(*at("resid", l, t, 1))
                        pool.dma_start(x_dram[(t - 2) * P:(t - 1) * P, :], X[:, t, :]).then_inc(*dma("x_saved", l))
            for t in range(2, TILES):
                pool.wait_ge(*at("final", t))
                pool.dma_start(out[0, (t - 2) * P:(t - 1) * P, :], X[:, t, :]).then_inc(*dma("stored"))
            pool.wait_ge(*at("stored"))

        @block.scalar
        def _(act):
            act.wait_ge(*at("vec_turned"))
            act.activation(ct[:, 0, :], vt[:, 0:16], ACT.Tanh, scale=0.5).then_inc(*up("cond_tanh"))
            act.preload_act_table_set("natural_log_exp_and_others")

            def mod_rows(l, b):
                if b < 4:
                    act.wait_ge(*at("filled", "mod", l, b))
                    if (l, b) != (0, 0):
                        act.wait_ge(*at("filled", "modT", *((l, b - 1) if b else (l - 1, 3))))
                    act.activation(modrow, ps("mod", l, b)[:], ACT.Copy).then_inc(*up("modrow", l, b))
                    let_go(("mod", l, b), "modrow", l, b)
                else:
                    for s in range(2):
                        act.wait_ge(*at("filled", "gate", l, b - 4, s))
                        act.activation(gate[:, s, 512 * (b - 4):512 * (b - 3)], ps("gate", l, b - 4, s)[:],
                                       ACT.Copy).then_inc(*up("gate_row", l, b - 4, s))
                        let_go(("gate", l, b - 4, s), "gate_row", l, b - 4, s)

            def rms(stage, group, n, scale, *key):
                act.wait_ge(*at("filled", *group))
                act.activation(rs[:, 0:n], ps(*group)[:, 0:n], ACT.Ln, bias=eps[:, 0:1], scale=scale)\
                    .then_inc(*up(stage + "_ln", *key))
                let_go(group, stage + "_ln", *key)
                act.wait_ge(*at(stage + "_ln", *key))
                act.activation(rs[:, 0:n], rs[:, 0:n], ACT.Exp, scale=-0.5).then_inc(*up(stage + "_rstd", *key))

            def x_rstd(l, tiles):
                if l == 0:
                    act.wait_ge(*at("x_in", 0))
                    act.wait_ge(*at("pool_init", "end"))
                for t in tiles:
                    if l:
                        act.wait_ge(*at("resid", l - 1, t, 1))
                    if t > tiles[0]:
                        act.wait_ge(*at("x_sq", l, t - 1))
                    act.activation(tz[:].rearrange("p a b -> p (a b)"), X[:, t, :], ACT.Square,
                                   accum_out=ssx[:, t:t + 1]).then_inc(*up("x_sq", l, t))
                    act.wait_ge(*at("x_sq", l, t))
                    act.activation(rx[:, t:t + 1], ssx[:, t:t + 1], ACT.Ln, bias=eps[:, 0:1],
                                   scale=1.0 / D).then_inc(*up("x_ln", l, t))
                    act.wait_ge(*at("x_ln", l, t))
                    act.activation(rx[:, t:t + 1], rx[:, t:t + 1], ACT.Exp, scale=-0.5)\
                        .then_inc(*up("x_rstd", l, t))

            prev_norm = None
            for l in range(DEPTH):
                if l == 0:
                    mod_rows(0, 0)
                x_rstd(l, list(range(TILES)))
                if l == 0:
                    for b in range(1, 4):
                        mod_rows(0, b)
                act.wait_ge(*at("mod_cols", l))
                for k in range(KD):
                    act.wait_ge(*at("filled", "xT", l, k, 0))
                    act.activation(hT[:, k, 0:256], ps("xT", l, k, 0)[:, 0:256], ACT.Identity,
                                   bias=mB[:, k, 1:2], scale=mA[:, k, 1:2]).then_inc(*up("hT_ctx", l, k))
                    let_go(("xT", l, k, 0), "hT_ctx", l, k)
                zi = 0
                for item in SEQ:
                    if item in ("small", "glaq", "glak"):
                        for c in chunks_of(item, l):
                            act.wait_ge(*at("filled", "F", l, item, c))
                            dst = small[:] if item == "small" else glaqk[:, item == "glak", :]
                            act.activation(dst[:, c[0]:sum(c)], ps("F", l, item, c)[:, 0:c[1]], ACT.Copy)\
                                .then_inc(*up("act_proj", l, item, c))
                            let_go(("F", l, item, c), "act_proj", l, item, c)
                    elif item[0] == "z":
                        for c in chunks_of(item, l):
                            act.wait_ge(*at("filled", "F", l, item, c))
                            if zi >= 2:
                                act.wait_ge(*at("zgate", l, zi - 2))
                            act.activation(tz[:, zi % 2, 0:c[1]], ps("F", l, item, c)[:, 0:c[1]], ACT.Tanh,
                                           scale=0.5).then_inc(*up("ztanh", l, zi))
                            zi += 1
                    elif item[:3] == "tok":
                        for t in [int(item[3])]:
                            act.wait_ge(*at("filled", "tok", l, t))
                            act.activation(glav[:, t, :], ps("tok", l, t)[:, 0:256], ACT.Copy)\
                                .then_inc(*up("glav", l, t))
                    elif item == "ga":
                        for d in range(2):
                            col = (V_GBF, V_GBB)[d] + l
                            for c in (CTX, LAT):
                                act.wait_ge(*at("filled", "ga", l, d, c))
                                act.activation(kd[d][:, c[0]:sum(c)], ps("ga", l, d, c)[:, 0:c[1]], ACT.Abs,
                                               bias=vt[:, col:col + 1]).then_inc(*up("g_abs", l, d, c))
                            act.wait_ge(*at("g_abs", l, d, LAT))
                            act.activation(kd[d], kd[d], ACT.Exp, scale=-1.0).then_inc(*up("g_exp", l, d))
                            act.wait_ge(*at("g_exp", l, d))
                            act.activation(kd[d], kd[d], ACT.Ln, bias=ones[:, 0:1]).then_inc(*up("g_ln", l, d))
                    elif item == "ga2":
                        for d in range(2):
                            act.wait_ge(*at("g_cum", l, d))
                            act.activation(Ef[d], cum[d], ACT.Exp, scale=1 / 16).then_inc(*up("g_E", l, d))
                            act.activation(ki[d], cum[d], ACT.Exp, scale=-1 / 16).then_inc(*up("g_Ei", l, d))
                            act.wait_ge(*at("g_rest", l, d))
                            act.activation(kd[d], kd[d], ACT.Exp, scale=1 / 16).then_inc(*up("kd_exp", l, d))
                    elif item[:2] == "ss":
                        j = int(item[2])
                        for c in norm_chunk(item, "q" if j == 0 else "kv", l):
                            act.wait_ge(*at("dve_proj", l, ("cq1", "ckv1")[j], c))
                            if prev_norm:
                                act.wait_ge(*at(*prev_norm))
                            act.activation(sq[:, :, 0:c[1]], cqkv[:, 2 * j:2 * j + 2, c[0]:sum(c)], ACT.Square)\
                                .then_inc(*up("lora_sq", l, j, c))
                            rms("lora", ("ss", l, j, c), c[1], 1.0 / LORA, l, j, c)
                            prev_norm = ("lora_norm", l, j, c)
                    elif item[:3] == "gsq":
                        i = int(item[3])
                        name = ("gq0", "gq1", "gq2", "gk")[i]
                        for c in norm_chunk(item, name, l):
                            act.wait_ge(*at("dve_proj", l, name, c))
                            j = gss_order(l).index((i, c))
                            act.wait_ge(*at("filled", *(("gss", l, *gss_order(l)[j - 2]) if j >= 2 else
                                                        ("ss", l, 1, LAT))))
                            act.activation(sq[:, j % 2, 0:c[1]], gqk[:, i, c[0]:sum(c)], ACT.Square)\
                                .then_inc(*up("gqa_sq", l, i, c))
                    elif item[:3] == "gss":
                        i = int(item[3])
                        name = ("gq0", "gq1", "gq2", "gk")[i]
                        for c in norm_chunk(item, name, l):
                            act.wait_ge(*at(*prev_norm))
                            rms("gqa", ("gss", l, i, c), c[1], 1.0 / HD, l, i, c)
                            prev_norm = ("gqa_norm", l, i, c)
                    elif item == "kdT":
                        for d in range(2):
                            for half in range(2):
                                act.wait_ge(*at("filled", "kdT", l, d, half))
                                act.wait_ge(*at("gla_factors", l, d))
                                act.activation(kdtok[d][:, 3 * half:3 * half + 3, :],
                                               ps("kdT", l, d, half)[:, 0:384].rearrange("p (t c) -> p t c", t=3),
                                               ACT.Copy).then_inc(*up("kdtok", l, d, half))
                                let_go(("kdT", l, d, half), "kdtok", l, d, half)
                act.preload_act_table_set("natural_log_exp_and_others")

                def o_out(t):
                    act.wait_ge(*at("filled", "o", l, t))
                    if t - 2 in out_tiles(l):
                        act.wait_ge(*at("filled", "oT", l, t - 2))
                    act.activation(on[:, t % 2, :], ps("o", l, t)[:, 0:256], ACT.Copy).then_inc(*up("o_copy", l, t))
                    let_go(("o", l, t), "o_copy", l, t)
                    act.wait_ge(*at("o_ss", l, t))
                    act.activation(ss4[:, t % 2, :], ss4[:, t % 2, :], ACT.Ln, bias=eps[:, 0:1],
                                   scale=1.0 / GLA_DV).then_inc(*up("o_ln", l, t))
                    act.wait_ge(*at("o_ln", l, t))
                    act.activation(ss4[:, t % 2, :], ss4[:, t % 2, :], ACT.Exp, scale=-0.5)\
                        .then_inc(*up("o_rstd", l, t))

                def head_in(h):
                    b = h % 2
                    if h >= 2:
                        act.wait_ge(*at("filled", "sc", l, h - 2, 256, TILES - 1))
                    for c in chunks_of("q", l):
                        act.wait_ge(*at("filled", "qp", l, h, c))
                        r = 64 if c == LAT else 96
                        act.activation(qh[b][0:r, c[0]:sum(c)], ps("qp", l, h, c)[0:r, 0:c[1]], ACT.Copy)\
                            .then_inc(*up("q_in", l, h, c))
                        if c == CTX:
                            let_go(("qp", l, h, c), "q_in", l, h, c)
                    for c in (CTX, LAT):
                        act.wait_ge(*at("filled", "kp", l, h, c))
                        act.activation(kh[b][0:64, c[0]:sum(c)], ps("kp", l, h, c)[0:64, 0:c[1]], ACT.Copy)\
                            .then_inc(*up("k_in", l, h, c))
                        let_go(("kp", l, h, c), "k_in", l, h, c)

                def gqa_in(h, part):
                    g, lat, b = h - MLA_H, lat_of(l), h % 2
                    src = gqk[64 * (g % 2):64 * (g % 2) + 64, g // 2, lat]
                    if part == 1 and g == 0:
                        act.wait_ge(*at("filled", "mx", l, MLA_H - 1, 256, TILES - 1, 1))
                        act.wait_ge(*at("filled", "kp", l, MLA_H - 1, LAT))
                        act.activation(rounded[:, 1, :], gqk[:, 3, :], ACT.Copy).then_inc(*up("k_high", l))
                    if part == 1 and g < 2:
                        r = g
                        act.activation(k_twice[r][0:64, :], gqk[64 * r:64 * r + 64, 3, :], ACT.Copy)\
                            .then_inc(*up("k_once", l, r))
                    if part == 0:
                        act.wait_ge(*at("gqa_rope", l, 3))
                        act.wait_ge(*at("filled", "sc", l, h - 2, 256, TILES - 1))
                        if g % 2 == 0:
                            if g:
                                act.wait_ge(*at("q_low", l, h - 1))
                            act.activation(rounded[:, 0, lat], gqk[:, g // 2, lat], ACT.Copy)\
                                .then_inc(*up("q_rounded", l, g // 2))
                        act.activation(q_high[b][0:64, lat], src, ACT.Copy).then_inc(*up("q_high", l, h))
                    if part == 2:
                        act.activation(q_both[b][0:64, lat], src, ACT.Copy).then_inc(*up("q_both", l, h))

                def round_q(h):
                    if h >= 1:
                        act.wait_ge(*at("filled", "mx", l, h - 1, 256, TILES - 1, 1))
                    act.wait_ge(*at("q_in", l, h, LAT))
                    act.wait_ge(*at("q_rope", l, h))
                    act.activation(qr[:, lat_of(l)], qh[h % 2][0:96, lat_of(l)], ACT.Copy)\
                        .then_inc(*up("round_q", l, h))

                def recip(h, q0, nq):
                    pv = pv_banks[pv_index(l, h, q0) % 2]
                    r, s = 64 * (h % 2), 64 - 64 * (h % 2)
                    act.wait_ge(*at("pv_filled", l, h, q0))
                    if recips:
                        act.wait_ge(*at("o_scaled", *recips[-1]))
                    act.activation(rd[r:r + 64, 0:nq], pv[s:s + 64, 0:nq], ACT.Ln).then_inc(*up("den_ln", l, h, q0))
                    act.wait_ge(*at("den_ln", l, h, q0))
                    act.activation(rd[r:r + 64, 0:nq], rd[r:r + 64, 0:nq], ACT.Exp, scale=-1.0)\
                        .then_inc(*up("recip", l, h, q0))
                    recips.append((l, h, q0))

                def w_high(n, ks):
                    i = W_POS[("out", l, n)]
                    for k in ks:
                        act.wait_ge(*at(f"w_half{i % 2}", i))
                        if n == 0:
                            act.wait_ge(*at("q_both", l, heads[-1]))
                            act.wait_ge(*at("k_low", l, 1))
                            act.wait_ge(*at("q_low", l, heads[-1]))
                            act.wait_ge(*at("filled", "o", l, TILES - 1))
                        else:
                            act.wait_ge(*at("k_low", l, 1))
                            act.wait_ge(*at("q_low", l, heads[-1]))
                            act.wait_ge(*at("y_gla", l, TILES - 1))
                        act.activation(w_hi[n][k], W[:, i % 2, k, :], ACT.Copy).then_inc(*up("w_hi", l, n, k))

                def y_high(ks):
                    for k in ks:
                        act.activation(y_hi[:, k, lat_of(l)], Y[:, k, lat_of(l)], ACT.Copy)\
                            .then_inc(*up("y_hi", l, k))

                def neg_max(h):
                    for q0, nq, nk in qbs(l):
                        act.wait_ge(*at("filled", "nm", l, h, q0))
                        queries = (qh if h < MLA_H else q_high)[h % 2]
                        act.activation(queries[96:97, q0:q0 + nq], ps("nm", l, h, q0)[96:97, 0:nq], ACT.Copy)\
                            .then_inc(*up("nm_row", l, h, q0))
                        let_go(("nm", l, h, q0), "nm_row", l, h, q0)

                head_in(0)
                round_q(0)
                for t in out_tiles(l):
                    o_out(t)
                slot = 0
                recips = [] if l == 0 else [(0, heads[-1], 256)]
                neg_max(0)
                for h in heads:
                    todo = [(q0, nq, kt) for q0, nq, nk in qbs(l) for kt in range(nk // P)]
                    more = h + 1 < len(heads)
                    if more:
                        if h == 0:
                            act.wait_ge(*at("filled", "o", l, TILES - 1))
                        if h + 1 < MLA_H:
                            head_in(h + 1)
                        else:
                            gqa_in(h + 1, 0)
                    for j, (q0, nq, kt) in enumerate(todo):
                        act.wait_ge(*at("filled", "sc", l, h, q0, kt))
                        if slot >= 4:
                            act.wait_ge(*at(*prob_reader(l, slot - 4)))
                        act.activation(prob[slot % 4][:, 0:nq], ps("sc", l, h, q0, kt)[:, 0:nq], ACT.Exp,
                                       scale=MLA_SCALE if h < MLA_H else GQA_SCALE)\
                            .then_inc(*up("prob", l, slot))
                        let_go(("sc", l, h, q0, kt), "prob", l, slot)
                        slot += 1
                        if j == 0 and h:
                            recip(h - 1, *qbs(l)[-1][:2])
                        if j == 0 and h + 1 < MLA_H:
                            round_q(h + 1)
                        if j < 2 and more and h + 1 >= MLA_H:
                            gqa_in(h + 1, j + 1)
                        m = mod_of_head(l, h)
                        if m and m[2] < 4 and j == MAX_FROM[l] - 2:
                            mod_rows(*m[1:])
                        if m and m[2] >= 4 and j == MAX_FROM[l] + 1:
                            act.wait_ge(*at("filled", "vp", l, TILES - 1))
                            act.wait_ge(*at("filled", "kp", l, MLA_H - 1, LAT))
                            mod_rows(*m[1:])
                        if h == heads[-1] and j == TILES - 1:
                            act.wait_ge(*at("filled", "sc", l, h - 1, 256, TILES - 1))
                            act.wait_ge(*at("y_attn", l, MLA_H - 1, 256))
                            act.wait_ge(*at("y_gla", l, TILES - 1))
                            y_high((0, 1))
                        c = j - 3 if h == heads[-2] else j + len(todo) - 4 if h == heads[-1] and j else -1
                        if 0 <= c < KD:
                            w_high(2 * c // KD, (2 * c % KD, 2 * c % KD + 1))
                        if j == 3 and len(qbs(l)) == 2:
                            recip(h, *qbs(l)[0][:2])
                    if more:
                        neg_max(h + 1)
                y_high((2, 3))
                recip(heads[-1], *qbs(l)[-1][:2])
                act.wait_ge(*at("y_attn", l, heads[-2], 256))
                y_high((4, 5))
                act.wait_ge(*at("y_attn", l, heads[-1], 256))
                y_high((6, 7))
            x_rstd(DEPTH, list(range(2, TILES)))

        @block.vector
        def _(dve):
            dve.wait_ge(*at("filled", "vec"))
            dve.tensor_copy(vt[:], ps("vec")[:, 0:V_ROWS]).then_inc(*up("vec_turned"))
            let_go(("vec",), "vec_turned")
            dve.wait_ge(*at("vec_turned"))
            dve.tensor_scalar(vth[:], vt[:], 0.5, None, ALU.mult).then_inc(*up("vec_half"))
            dve.wait_ge(*at("cond_tanh"))
            dve.wait_ge(*at("vec_half"))
            dve.wait_ge(*at("pool_init", "end"))
            dve.scalar_tensor_tensor(out=sc[:, :, 0:2].rearrange("p k s -> p s k"),
                                     in0=ct[:, 0, :].rearrange("p (s k) -> p s k", s=2), scalar=1.0,
                                     in1=vth[:, 0:16].rearrange("p (s k) -> p s k", s=2),
                                     op0=ALU.add, op1=ALU.mult).then_inc(*up("cond_silu"))

            def mod_cols(l, b):
                dve.wait_ge(*at("filled", "modT", l, b))
                if b == 0 and l:
                    dve.wait_ge(*at("mod_cols", l - 1))
                src = ps("modT", l, b)[:].rearrange("p (f j r) -> p f r j", f=4, j=4)[:, :, 0:2, :]
                dve.tensor_reduce(modc[:, 4 * b:4 * b + 4, :], src, AX, ALU.add).then_inc(*up("mod_sum", l, b))
                let_go(("modT", l, b), "mod_sum", l, b)
                if b == 3:
                    bm = V_BMOD + 24 * l
                    if l:
                        dve.wait_ge(*at("hT_ctx", l - 1, KD - 1))
                    dve.wait_ge(*at("mod_sum", l, 3))
                    dve.tensor_tensor(mB[:], modc[:, 0:8, :], vt[:, bm:bm + 8].unsqueeze(2).broadcast_to([P, 8, 2]),
                                      ALU.add).then_inc(*up("mod_b", l))
                    dve.tensor_tensor(mA[:], modc[:, 8:16, :],
                                      vt[:, bm + 8:bm + 16].unsqueeze(2).broadcast_to([P, 8, 2]),
                                      ALU.add).then_inc(*up("mod_a", l))
                    dve.wait_ge(*at("mod_a", l))
                    nw = V_NORM + 8 * l
                    dve.scalar_tensor_tensor(out=mA[:], in0=mA[:], scalar=1.0,
                                             in1=vt[:, nw:nw + 8].unsqueeze(2).broadcast_to([P, 8, 2]),
                                             op0=ALU.add, op1=ALU.mult).then_inc(*up("mod_cols", l))

            def xhat(l):
                for t in range(TILES):
                    dve.wait_ge(*at("x_rstd", l, t))
                    if l and t == 0:
                        dve.wait_ge(*at("filled", "out", l - 1, out_tiles(l - 1)[-1], 1))
                    dve.tensor_scalar(xn[:, t, :], X[:, t, :], rx[:, t:t + 1], None, ALU.mult)\
                        .then_inc(*up("xhat", l, t))

            def final(t):
                dve.wait_ge(*at("x_rstd", DEPTH, t))
                dve.wait_ge(*at("fnw_in"))
                dve.scalar_tensor_tensor(out=X[:, t, :], in0=X[:, t, :], scalar=rx[:, t:t + 1], in1=fnw,
                                         op0=ALU.mult, op1=ALU.mult).then_inc(*up("final", t))

            mod_cols(0, 0)
            xhat(0)
            for b in range(1, 4):
                mod_cols(0, b)

            for l in range(DEPTH):
                if l:
                    xhat(l)
                dve.wait_ge(*at("mod_cols", l))
                for k in range(KD):
                    dve.wait_ge(*at("filled", "xT", l, k, 1))
                    dve.tensor_scalar(hT[:, k, 256:T], ps("xT", l, k, 1)[:], mA[:, k, 0:1], mB[:, k, 0:1],
                                      ALU.mult, ALU.add).then_inc(*up("hT_lat", l, k))
                    let_go(("xT", l, k, 1), "hT_lat", l, k)
                zi = 0
                for item in SEQ:
                    if item == "small":
                        dve.wait_ge(*at("act_proj", l, "small", LAT))
                        dve.wait_ge(*at("con_in"))
                        lat = slice(256, T)
                        dve.tensor_tensor(rt[64:96, 0, :], small[96:128, lat], tabm[96:128, :], ALU.mult)\
                            .then_inc(*up("kr_mul", l))
                        dve.tensor_tensor(rt[64:96, 1, :], small[64:96, lat], tabm[64:96, :], ALU.mult)\
                            .then_inc(*up("kr_mul", l))
                        dve.wait_ge(*at("kr_mul", l))
                        dve.tensor_tensor(small[64:96, lat], rt[64:96, 0, :], rt[64:96, 1, :], ALU.add)\
                            .then_inc(*up("kr_rope", l))
                    elif item in ("cq0", "cq1", "ckv0", "ckv1", "gq0", "gq1", "gq2", "gk"):
                        i = ("cq0", "cq1", "ckv0", "ckv1", "gq0", "gq1", "gq2", "gk").index(item)
                        for c in chunks_of(item, l):
                            dve.wait_ge(*at("filled", "F", l, item, c))
                            dst = cqkv[:, i, :] if i < 4 else gqk[:, i - 4, :]
                            dve.tensor_copy(dst[:, c[0]:sum(c)], ps("F", l, item, c)[:, 0:c[1]])\
                                .then_inc(*up("dve_proj", l, item, c))
                            let_go(("F", l, item, c), "dve_proj", l, item, c)
                    elif item[0] == "z":
                        for c in chunks_of(item, l):
                            dve.wait_ge(*at("ztanh", l, zi))
                            dve.scalar_tensor_tensor(out=Y[:, int(item[1]), c[0]:sum(c)],
                                                     in0=tz[:, zi % 2, 0:c[1]], scalar=1.0,
                                                     in1=ps("F", l, item, c)[:, 0:c[1]], op0=ALU.add,
                                                     op1=ALU.mult).then_inc(*up("zgate", l, zi))
                            let_go(("F", l, item, c), "zgate", l, zi)
                            zi += 1
                    elif item[:3] == "tok":
                        for t in [int(item[3])]:
                            dve.wait_ge(*at("glav", l, t))
                            src = ps("tok", l, t)[:, 256:384].rearrange("p (g v) -> p g v", g=2)
                            for half in range(2):
                                dve.tensor_copy(vg[:, t, :, 128 * half:128 * half + 64], src)\
                                    .then_inc(*up("vg", l, t, half))
                            let_go(("tok", l, t), "vg", l, t, 1)
                    elif item == "ga":
                        for d in range(2):
                            col = (V_GBF, V_GBB)[d] + l
                            for c in (CTX, LAT):
                                dve.wait_ge(*at("g_abs", l, d, c))
                                dve.tensor_scalar(qd[d][:, c[0]:sum(c)], ps("ga", l, d, c)[:, 0:c[1]],
                                                  vt[:, col:col + 1], 0.0, ALU.add, ALU.min)\
                                    .then_inc(*up("g_min", l, d, c))
                                let_go(("ga", l, d, c), "g_min", l, d, c)
                            dve.wait_ge(*at("g_ln", l, d))
                            dve.wait_ge(*at("g_min", l, d, LAT))
                            dve.tensor_tensor(qd[d], qd[d], kd[d], ALU.subtract).then_inc(*up("g_log", l, d))
                            dve.wait_ge(*at("g_log", l, d))
                            g, o = (qd[d], cum[d]) if d == 0 else (qd[d][:, ::-1], cum[d][:, ::-1])
                            if d == 0:
                                dve.wait_ge(*at("filled", "modT", l, 3))
                            dve.tensor_tensor_scan(o, keep[:], g, 0.0, ALU.mult, ALU.add)\
                                .then_inc(*up("g_cum", l, d))
                    elif item == "ga2":
                        for d in range(2):
                            e = CHUNK - 1 if d == 0 else 0
                            last = cum[d][:, e:T:CHUNK].unsqueeze(2).broadcast_to([P, NCHUNK, CHUNK])
                            dve.wait_ge(*at("g_cum", l, d))
                            dve.tensor_tensor(kd[d].rearrange("p (n c) -> p n c", n=NCHUNK), last,
                                              cum[d].rearrange("p (n c) -> p n c", n=NCHUNK), ALU.subtract)\
                                .then_inc(*up("g_rest", l, d))
                    elif item == "glamul":
                        dve.wait_ge(*at("act_proj", l, "glaq", LAT))
                        dve.wait_ge(*at("act_proj", l, "glak", LAT))
                        for d in range(2):
                            dve.wait_ge(*at("kd_exp", l, d))
                            dve.tensor_tensor(kd[d], kd[d], glaqk[:, 1, :], ALU.mult).then_inc(*up("gla_kd", l, d))
                            dve.tensor_tensor(ki[d], ki[d], glaqk[:, 1, :], ALU.mult).then_inc(*up("gla_ki", l, d))
                            e = CHUNK - 1 if d == 0 else 0
                            dve.tensor_copy(dec[:, d, :], Ef[d][:, e:T:CHUNK]).then_inc(*up("gla_dec", l, d))
                            lat = lat_of(l)
                            dve.scalar_tensor_tensor(out=qd[d][:, lat], in0=glaqk[:, 0, lat],
                                                     scalar=GLA_DK ** -0.5, in1=Ef[d][:, lat], op0=ALU.mult,
                                                     op1=ALU.mult).then_inc(*up("gla_factors", l, d))
                    elif item[:2] == "ss":
                        j = int(item[2])
                        for c in norm_chunk(item, "q" if j == 0 else "kv", l):
                            dve.wait_ge(*at("lora_rstd", l, j, c))
                            for f in range(2):
                                col = (V_MQ, V_MKV)[j] + 2 * l + f
                                v = cqkv[:, 2 * j + f, c[0]:sum(c)]
                                dve.scalar_tensor_tensor(out=v, in0=v, scalar=vt[:, col:col + 1],
                                                         in1=rs[:, 0:c[1]], op0=ALU.mult, op1=ALU.mult)\
                                    .then_inc(*up("lora_norm", l, j, c))
                    elif item[:3] == "gss":
                        i = int(item[3])
                        col = (V_QN if i < 3 else V_KN) + l
                        for c in norm_chunk(item, ("gq0", "gq1", "gq2", "gk")[i], l):
                            dve.wait_ge(*at("gqa_rstd", l, i, c))
                            v = gqk[:, i, c[0]:sum(c)]
                            dve.scalar_tensor_tensor(out=v, in0=v, scalar=vt[:, col:col + 1], in1=rs[:, 0:c[1]],
                                                     op0=ALU.mult, op1=ALU.mult).then_inc(*up("gqa_norm", l, i, c))
                    elif item[:4] == "rope":
                        i = int(item[4])
                        v = gqk[:, i, 256:T]
                        dve.wait_ge(*at("filled", "rope", l, i))
                        dve.wait_ge(*(at("gqa_rope", l, i - 1) if i else at("kr_rope", l)))
                        dve.tensor_tensor(rt[:, 0, :], ps("rope", l, i)[:], sing, ALU.mult)\
                            .then_inc(*up("gqa_sin", l, i))
                        let_go(("rope", l, i), "gqa_sin", l, i)
                        dve.wait_ge(*at("gqa_norm", l, i, LAT))
                        dve.tensor_tensor(v, v, cosg, ALU.mult).then_inc(*up("gqa_cos", l, i))
                        dve.wait_ge(*at("gqa_cos", l, i))
                        dve.tensor_tensor(v, v, rt[:, 0, :], ALU.add).then_inc(*up("gqa_rope", l, i))
                    elif item[:2] == "ds":
                        for d in [int(item[2])]:
                            for par in range(2):
                                dve.wait_ge(*at("filled", "ds", l, d, par))
                            order = chunk_order(d)
                            dve.memset(St[d][:, order[0], :], 0.0).then_inc(*up("state", l, d, order[0]))
                            for n, m in zip(order, order[1:]):
                                dve.wait_ge(*at("state", l, d, n))
                                dve.scalar_tensor_tensor(
                                    out=St[d][:, m, :], in0=St[d][:, n, :], scalar=dec[:, d, n:n + 1],
                                    in1=ps("ds", l, d, n % 2)[:, 64 * (n // 2):64 * (n // 2) + 64],
                                    op0=ALU.mult, op1=ALU.add).then_inc(*up("state", l, d, m))
                            tally.mark[("state", (l, d))] = tally.count["state"]
                            for par in range(2):
                                let_go(("ds", l, d, par), "state", l, d)

                def a_in(t, d):
                    dve.wait_ge(*at("filled", "F", l, "z7", LAT))
                    dve.wait_ge(*at("gla_factors", l, d))
                    if t - 1 in out_tiles(l):
                        dve.wait_ge(*at("filled", "A", l, t - 1, d))
                    dve.tensor_tensor(qbd[d], qd[d][:, t * P:t * P + P].unsqueeze(1).broadcast_to([P, 4, P]),
                                      headed.unsqueeze(2).broadcast_to([P, 4, P]), ALU.mult)\
                        .then_inc(*up("qbd", l, t, d))

                def a_mask(t, d):
                    dve.wait_ge(*at("filled", "A", l, t, d))
                    dve.wait_ge(*at("bd_zero", l))
                    if t - 2 in out_tiles(l):
                        dve.wait_ge(*at("filled", "o", l, t - 2))
                    dve.copy_predicated(Ab[t % 2][d], mask[d].unsqueeze(1).broadcast_to([P, 4, P]),
                                        ps("A", l, t, d)[:].rearrange("p (h t) -> p h t", h=4))\
                        .then_inc(*up("A_masked", l, t, d))
                    let_go(("A", l, t, d), "A_masked", l, t, d)

                def o_square(t):
                    dve.wait_ge(*at("o_copy", l, t))
                    if t - 1 in out_tiles(l):
                        dve.wait_ge(*at("o_ss", l, t - 1))
                    dve.tensor_tensor(sqo, on[:, t % 2, :], on[:, t % 2, :], ALU.mult).then_inc(*up("o_sq", l, t))
                    dve.wait_ge(*at("o_sq", l, t))
                    if t - 2 in out_tiles(l):
                        dve.wait_ge(*at("o_norm", l, t - 2))
                    dve.tensor_reduce(ss4[:, t % 2, :], sqo.rearrange("p (h v) -> p h v", h=4), AX, ALU.add)\
                        .then_inc(*up("o_ss", l, t))

                def o_scale(t):
                    dve.wait_ge(*at("o_rstd", l, t))
                    o4 = on[:, t % 2, :].rearrange("p (h v) -> p h v", h=4)
                    dve.tensor_tensor(o4, o4, ss4[:, t % 2, :].unsqueeze(2).broadcast_to([P, 4, 64]), ALU.mult)\
                        .then_inc(*up("o_norm", l, t))

                def o_gate(t):
                    dve.wait_ge(*at("filled", "oT", l, t))
                    y = Y[:, 0:2, t * P:(t + 1) * P]
                    dve.scalar_tensor_tensor(out=y, in0=ps("oT", l, t)[:, 0:256].rearrange("p (f t) -> p f t", f=2),
                                             scalar=vth[:, V_GN + l:V_GN + l + 1], in1=y, op0=ALU.mult,
                                             op1=ALU.mult).then_inc(*up("y_gla", l, t))
                    let_go(("oT", l, t), "y_gla", l, t)

                def mla_v():
                    dve.wait_ge(*at("vm_ones", l))
                    for t in range(TILES):
                        dve.wait_ge(*at("filled", "vp", l, t))
                        src = ps("vp", l, t)[:, 0:384].rearrange("p (r e v) -> p r e v", r=3, e=2)
                        for e in range(2):
                            dve.tensor_copy(vm[:, t, :, 128 * e:128 * e + 64], src[:, :, e, :])\
                                .then_inc(*up("vm", l, t, e))
                        let_go(("vp", l, t), "vm", l, t, 1)

                def q_rope(h):
                    p = ps("qp", l, h, LAT)
                    dve.wait_ge(*at("q_in", l, h, LAT))
                    if h:
                        dve.wait_ge(*at("q_rope", l, h - 1))
                    if l == 0 and h == 0:
                        dve.wait_ge(*at("gqa_rope", l, 3))
                    dve.tensor_tensor(rt[64:96, 0, :], p[96:128, :], tabm[96:128, :], ALU.mult)\
                        .then_inc(*up("q_mul", l, h, 0))
                    dve.tensor_tensor(rt[64:96, 1, :], p[64:96, :], tabm[64:96, :], ALU.mult)\
                        .then_inc(*up("q_mul", l, h, 1))
                    let_go(("qp", l, h, LAT), "q_mul", l, h, 1)
                    dve.wait_ge(*at("q_mul", l, h, 1))
                    if h >= 2:
                        dve.wait_ge(*at("filled", "sc", l, h - 2, 256, TILES - 1))
                    dve.tensor_tensor(qh[h % 2][64:96, 256:T], rt[64:96, 0, :], rt[64:96, 1, :], ALU.add)\
                        .then_inc(*up("q_rope", l, h))

                def low_parts(h):
                    g, lat = h - MLA_H, lat_of(l)
                    row = 64 * (g % 2)
                    if g < 2:
                        r = g
                        dve.wait_ge(*at("k_high", l))
                        dve.wait_ge(*at("filled", "kp", l, MLA_H - 1, LAT))
                        dve.tensor_copy(k_twice[r][64:P, :], gqk[64 * r:64 * r + 64, 3, :])\
                            .then_inc(*up("k_twice", l, r))
                        dve.tensor_tensor(k_low[r][0:64, :], gqk[64 * r:64 * r + 64, 3, :],
                                          rounded[64 * r:64 * r + 64, 1, :].bitcast(F32), ALU.subtract)\
                            .then_inc(*up("k_low", l, r))
                    dve.wait_ge(*at("q_rounded", l, g // 2))
                    dve.wait_ge(*at("filled", "sc", l, h - 2, 256, TILES - 1))
                    dve.tensor_tensor(q_both[h % 2][64:P, lat], gqk[row:row + 64, g // 2, lat],
                                      rounded[row:row + 64, 0, lat].bitcast(F32), ALU.subtract)\
                        .then_inc(*up("q_low", l, h))

                def maxima(h):
                    if h >= 2:
                        dve.wait_ge(*at("filled", "nm", l, h - 2, 256))
                    elif l:
                        dve.wait_ge(*at("filled", "nm", l - 1, 10 + h, 256))
                    for q0, nq, nk in qbs(l):
                        for t in range(q0 // P, (q0 + nq) // P):
                            if q0 == 0:
                                dve.wait_ge(*at("filled", "mx", l, h, q0, t, 0))
                                dve.tensor_reduce(nmx[:, h % 2, t:t + 1], ps("mx", l, h, q0, t, 0)[:, 0:256], AX,
                                                  ALU.max, negate=True).then_inc(*up("part_max", l, h, q0, t, 0))
                                let_go(("mx", l, h, q0, t, 0), "part_max", l, h, q0, t, 0)
                                continue
                            for half in range(2):
                                dve.wait_ge(*at("filled", "mx", l, h, q0, t, half))
                                if h and t == 2 and not half:
                                    dve.wait_ge(*at("neg_max", l, h - 1))
                                dve.tensor_reduce(mxp[:, t, half:half + 1], ps("mx", l, h, q0, t, half)[:, 0:384],
                                                  AX, ALU.max).then_inc(*up("part_max", l, h, q0, t, half))
                                let_go(("mx", l, h, q0, t, half), "part_max", l, h, q0, t, half)
                    dve.wait_ge(*at("part_max", l, h, 256, TILES - 1, 1))
                    dve.tensor_reduce(nmx[:, h % 2, 2:TILES], mxp[:, 2:TILES, :], AX, ALU.max, negate=True)\
                        .then_inc(*up("neg_max", l, h))

                last_y = [None]

                def normalise(h, q0, nq):
                    pv = pv_banks[pv_index(l, h, q0) % 2]
                    r, s = 64 * (h % 2), 64 - 64 * (h % 2)
                    tile = (2 + h // 2) if h < MLA_H else (5 + (h - MLA_H) // 2)
                    dve.wait_ge(*at("pv_filled", l, h, q0))
                    if last_y[0]:
                        dve.wait_ge(*at("y_attn", *last_y[0]))
                    dve.wait_ge(*at("recip", l, h, q0))
                    dve.scalar_tensor_tensor(out=un[r:r + 64, 0:nq], in0=pv[r:r + 64, 0:nq], scalar=0.5,
                                             in1=rd[r:r + 64, 0:nq], op0=ALU.mult, op1=ALU.mult)\
                        .then_inc(*up("o_scaled", l, h, q0))
                    dve.wait_ge(*at("o_scaled", l, h, q0))
                    y = Y[r:r + 64, tile, q0:q0 + nq]
                    dve.tensor_tensor(y, un[r:r + 64, 0:nq], y, ALU.mult).then_inc(*up("y_attn", l, h, q0))
                    last_y[0] = (l, h, q0)

                def gate_bias(l, b):
                    dve.wait_ge(*at("filled", "mod", l, b))
                    dve.wait_ge(*at("brow_in", l))
                    former = ("gate", l, 0, 1) if b == 5 else ("modT", l + 1, 3) if l + 1 < DEPTH else \
                        ("gate", l - 1, 1, 1)
                    dve.wait_ge(*at("filled", *former))
                    dve.tensor_tensor(modrow, ps("mod", l, b)[:], brow[:, b - 4, :], ALU.add)\
                        .then_inc(*up("modrow_gate", l, b - 4))
                    let_go(("mod", l, b), "modrow_gate", l, b - 4)

                def y_low(ks):
                    for k in ks:
                        dve.wait_ge(*at("y_hi", l, k))
                        lat = lat_of(l)
                        dve.tensor_tensor(y_lo[:, k, lat], Y[:, k, lat], y_hi[:, k, lat].bitcast(F32),
                                          ALU.subtract).then_inc(*up("y_lo", l, k))

                tiles = out_tiles(l)
                q_rope(0)
                for t in [tiles[0]]:
                    for d in range(2):
                        a_in(t, d)
                    for d in range(2):
                        a_mask(t, d)
                    for d in range(2):
                        a_in(t + 1, d)
                maxima(0)
                for t in tiles:
                    if t + 1 < TILES:
                        for d in range(2):
                            a_mask(t + 1, d)
                    if t + 2 < TILES:
                        for d in range(2):
                            a_in(t + 2, d)
                    o_square(t)
                    o_scale(t)
                    if t - 1 in tiles:
                        o_gate(t - 1)
                o_gate(TILES - 1)
                mla_v()
                for h in heads:
                    if h + 1 < MLA_H:
                        q_rope(h + 1)
                    if h:
                        normalise(h - 1, *qbs(l)[-1][:2])
                    m = mod_of_head(l, h)
                    if m:
                        (mod_cols if m[2] < 4 else gate_bias)(*m[1:])
                    if MLA_H <= h + 1 < len(heads):
                        low_parts(h + 1)
                    if len(qbs(l)) == 2:
                        normalise(h, *qbs(l)[0][:2])
                    if h + 1 < len(heads):
                        maxima(h + 1)
                y_low(range(4))
                normalise(heads[-1], *qbs(l)[-1][:2])
                y_low(range(4, KD))

                dve.wait_ge(*at("x_back", l))
                done = []
                for n in range(2):
                    for t in out_tiles(l):
                        s = 1 if t < 2 else 0
                        dve.wait_ge(*at("filled", "out", l, t, n))
                        dve.wait_ge(*at("gate_row", l, n, s))
                        i = len(done)
                        if i >= 2:
                            dve.wait_ge(*at("resid", l, *done[i - 2]))
                        dve.tensor_tensor(rt[:, i % 2, :], ps("out", l, t, n)[:], gate[:, s, 512 * n:512 * n + 512],
                                          ALU.mult).then_inc(*up("gated", l, t, n))
                        let_go(("out", l, t, n), "gated", l, t, n)
                        dve.wait_ge(*at("gated", l, t, n))
                        xs = X[:, t, 512 * n:512 * n + 512]
                        dve.tensor_tensor(xs, xs, rt[:, i % 2, :], ALU.add).then_inc(*up("resid", l, t, n))
                        done.append((t, n))
                        if l == DEPTH - 1 and n == 1 and t > 2:
                            final(t - 1)
            final(TILES - 1)

        @block.tensor
        def _(pe):
            def open_(*group):
                tally.order.append(group)
                i = len(tally.order) - 1
                if tally.before and i >= RING:
                    for stage, step in tally.before.freed[tally.before.order[i - RING]]:
                        pe.wait_ge(*at(stage, *step))
                return banks[i % RING]

            def close(mm, *group):
                mm.then_inc(*up("filled", *group))
                mm_group[0] = group

            mm_group = [None]

            def block_done(i):
                tally.mark[("filled", ("block", i))] = tally.count["filled"]

            def block_wait(i):
                pe.wait_ge(*at(f"w_half{i % 2}", i))

            pe.wait_ge(*at("vec_in"))
            pe.wait_ge(*at("ident_in"))
            p = open_("vec")
            close(pe.transpose(p[:, 0:V_ROWS], vec, ident[0:V_ROWS, 0:V_ROWS]), "vec")

            def mod(l, b):
                i = W_POS[("mod", l, b)]
                p = open_("mod", l, b)
                block_wait(i)
                for r in range(2):
                    for j in range(4):
                        k = 4 * r + j
                        mm = pe.matmul(p[32 * j:32 * j + 32, :], sc[:, k, :], W[:, i % 2, k, :], start=(r == 0),
                                       stop=(r == 1), skip_group_check=True)
                close(mm, "mod", l, b)
                block_done(i)

            def mod_turn(l, b):
                if b < 4:
                    q = open_("modT", l, b)
                    pe.wait_ge(*at("modrow", l, b))
                    for f in range(4):
                        mm = pe.transpose(q[:, P * f:P * f + P], modrow[:, P * f:P * f + P], ident)
                    close(mm, "modT", l, b)
                else:
                    for s in range(2):
                        q = open_("gate", l, b - 4, s)
                        pe.wait_ge(*at("modrow_gate", l, b - 4))
                        close(pe.matmul(q[:], sel[:, s, :], modrow, start=True, stop=True), "gate", l, b - 4, s)

            pe.wait_ge(*at("cond_silu"))
            for b in range(4):
                mod(0, b)
                mod_turn(0, b)

            for l in range(DEPTH):
                for k in range(KD):
                    for part, tiles in ((0, (0, 1)), (1, (2, 3, 4, 5))):
                        p = open_("xT", l, k, part)
                        for j, t in enumerate(tiles):
                            pe.wait_ge(*at("xhat", l, t))
                            mm = pe.transpose(p[:, P * j:P * j + P], xn[:, t, P * k:P * k + P], ident)
                        close(mm, "xT", l, k, part)
                pe.wait_ge(*at("hT_ctx", l, KD - 1))
                pe.wait_ge(*at("hT_lat", l, KD - 1))
                for item in SEQ:
                    if item in SLOT:
                        b, s = SLOT[item]
                        i = W_POS[("in", l, b)]
                        w = W[:, i % 2]
                        if s == 0 and item not in ("tok1", "tok2", "tok3", "tok4", "tok5"):
                            block_wait(i)
                        if item == "small":
                            pe.wait_ge(*at("swap_kr", l))
                    if item[:3] == "tok":
                        for t in [int(item[3])]:
                            p = open_("tok", l, t)
                            for k in range(KD):
                                mm = pe.matmul(p[:, 0:384], hT[:, k, t * P:(t + 1) * P], w[:, k, 0:384],
                                               start=(k == 0), stop=(k == KD - 1))
                            close(mm, "tok", l, t)
                        if item in LAST_OF:
                            block_done(i)
                    elif item in SLOT:
                        for c in chunks_of(item, l):
                            p = open_("F", l, item, c)
                            for k in range(KD):
                                mm = pe.matmul(p[:, 0:c[1]], w[:, k, s * P:s * P + P], hT[:, k, c[0]:sum(c)],
                                               start=(k == 0), stop=(k == KD - 1))
                            close(mm, "F", l, item, c)
                        if item in LAST_OF:
                            block_done(i)
                    elif item == "ga":
                        pe.wait_ge(*at("wa_in", l))
                        pe.wait_ge(*at("act_proj", l, "small", LAT))
                        for d in range(2):
                            for c in (CTX, LAT):
                                p = open_("ga", l, d, c)
                                close(pe.matmul(p[:, 0:c[1]], wa[:, d, :], small[0:32, c[0]:sum(c)], start=True,
                                                stop=True), "ga", l, d, c)
                    elif item[:2] == "ss":
                        j = int(item[2])
                        for c in norm_chunk(item, "q" if j == 0 else "kv", l):
                            p = open_("ss", l, j, c)
                            pe.wait_ge(*at("lora_sq", l, j, c))
                            for f in range(2):
                                mm = pe.matmul(p[:, 0:c[1]], ones[:], sq[:, f, 0:c[1]], start=(f == 0), stop=(f == 1))
                            close(mm, "ss", l, j, c)
                    elif item[:3] == "gss":
                        i = int(item[3])
                        for c in norm_chunk(item, ("gq0", "gq1", "gq2", "gk")[i], l):
                            p = open_("gss", l, i, c)
                            pe.wait_ge(*at("gqa_sq", l, i, c))
                            half = gss_order(l).index((i, c)) % 2
                            close(pe.matmul(p[:, 0:c[1]], blk, sq[:, half, 0:c[1]], start=True, stop=True),
                                  "gss", l, i, c)
                    elif item[:4] == "rope":
                        i = int(item[4])
                        p = open_("rope", l, i)
                        pe.wait_ge(*at("gqa_norm", l, i, LAT))
                        close(pe.matmul(p[:], perm, gqk[:, i, 256:T], start=True, stop=True), "rope", l, i)
                    elif item == "kdT":
                        for d in range(2):
                            pe.wait_ge(*at("gla_kd", l, d))
                            for half in range(2):
                                p = open_("kdT", l, d, half)
                                for j in range(3):
                                    t = 3 * half + j
                                    mm = pe.transpose(p[:, P * j:P * j + P], kd[d][:, t * P:t * P + P], ident)
                                close(mm, "kdT", l, d, half)
                    elif item[:2] == "ds":
                        pe.wait_ge(*at("glav", l, TILES - 1))
                        for d in [int(item[2])]:
                            pe.wait_ge(*at("kdtok", l, d, 1))
                            for par in range(2):
                                p = open_("ds", l, d, par)
                                r = slice(64 * par, 64 * par + 64)
                                for j in range(TILES):
                                    for h in range(GLA_H):
                                        mm = pe.matmul(p[32 * h:32 * h + 32, 64 * j:64 * j + 64],
                                                       kdtok[d][r, j, 32 * h:32 * h + 32],
                                                       glav[r, j, 64 * h:64 * h + 64], start=True, stop=True)
                                close(mm, "ds", l, d, par)

                def gla_a(t):
                    for d in range(2):
                        p = open_("A", l, t, d)
                        pe.wait_ge(*at("qbd", l, t, d))
                        pe.wait_ge(*at("gla_ki", l, d))
                        close(pe.matmul(p[:], ki[d][:, t * P:t * P + P], qbd[d].rearrange("p h t -> p (h t)"),
                                        start=True, stop=True), "A", l, t, d)

                def gla_o(t):
                    p = open_("o", l, t)
                    for d in range(2):
                        pe.wait_ge(*at("Sbd", l, t, d))
                        for c in range(2):
                            pe.matmul(p[64 * c:64 * c + 64, 0:256], qd[d][:, t * P + 64 * c:t * P + 64 * c + 64],
                                      Sbd[d][:, c].rearrange("p h v -> p (h v)"), start=(d == 0), stop=False,
                                      skip_group_check=True)
                    for d in range(2):
                        pe.wait_ge(*at("A_masked", l, t, d))
                        for h in range(GLA_H):
                            mm = pe.matmul(p[:, 64 * h:64 * h + 64], Ab[t % 2][d][:, h, :], glav[:, t, 64 * h:64 * h + 64],
                                           start=False, stop=(d == 1), skip_group_check=True)
                    close(mm, "o", l, t)

                def gla_t(t):
                    p = open_("oT", l, t)
                    pe.wait_ge(*at("o_norm", l, t))
                    for f in range(2):
                        mm = pe.transpose(p[:, P * f:P * f + P], on[:, t % 2, P * f:P * f + P], ident)
                    close(mm, "oT", l, t)

                def project_q(h):
                    if h >= MLA_H:
                        return
                    if h == 0:
                        pe.wait_ge(*at("swap_q", l))
                        pe.wait_ge(*at("lora_norm", l, 1, LAT))
                    for c in chunks_of("q", l):
                        p = open_("qp", l, h, c)
                        for f in range(2):
                            mm = pe.matmul(p[:, 0:c[1]], wuq[:, f, h, :], cqkv[:, f, c[0]:sum(c)], start=(f == 0),
                                           stop=(f == 1))
                        close(mm, "qp", l, h, c)

                def project_k(h):
                    if h >= MLA_H:
                        return
                    for c in (CTX, LAT):
                        p = open_("kp", l, h, c)
                        for f in range(2):
                            mm = pe.matmul(p[0:64, 0:c[1]], wukv[:, f, h, 0:64], cqkv[:, 2 + f, c[0]:sum(c)],
                                           start=(f == 0), stop=(f == 1))
                        close(mm, "kp", l, h, c)

                def max_groups(h):
                    return [(h, q0, t, half, min(nk, 384)) for q0, nq, nk in qbs(l)
                            for t in range(q0 // P, (q0 + nq) // P) for half in range(-(-nk // 384))]

                def maxes(groups):
                    for h, q0, t, half, n in groups:
                        if h < MLA_H:
                            pe.wait_ge(*at("round_q", l, h))
                            pe.wait_ge(*at("round_k", l, h))
                            q, k = qr, kr
                        else:
                            pe.wait_ge(*at("q_high", l, h))
                            pe.wait_ge(*at("k_once", l, (h - MLA_H) // 3))
                            pe.wait_ge(*at("k_twice", l, (h - MLA_H) // 3))
                            pe.wait_ge(*at("q_pad", l, h % 2))
                            q, k = q_high[h % 2][0:96, :], k_twice[(h - MLA_H) // 3][0:96, :]
                        p = open_("mx", l, h, q0, t, half)
                        close(pe.matmul(p[:, 0:n], q[:, t * P:t * P + P], k[:, n * half:n * half + n],
                                        start=True, stop=True), "mx", l, h, q0, t, half)

                def max_rows(h):
                    pe.wait_ge(*at("neg_max", l, h))
                    for q0, nq, nk in qbs(l):
                        p = open_("nm", l, h, q0)
                        for j in range(nq // P):
                            t = q0 // P + j
                            mm = pe.matmul(p[96:97, P * j:P * j + P], nmx[:, h % 2, t:t + 1], ident, start=True,
                                           stop=True)
                        close(mm, "nm", l, h, q0)

                def values(tiles):
                    for t in tiles:
                        p = open_("vp", l, t)
                        for f in range(2):
                            mm = pe.matmul(p[:, 0:384].rearrange("p (h v) -> p h v", h=MLA_H),
                                           cqkv[:, 2 + f, t * P:t * P + P], wukv[:, f, :, 64:128],
                                           start=(f == 0), stop=(f == 1))
                        close(mm, "vp", l, t)

                slot = [0]
                pend = []

                def pv(h, q0, nq, kt, nkt, sl):
                    i = pv_index(l, h, q0)
                    if kt == 0 and i >= 2:
                        lb, hb, qb = pv_owner(i - 2)
                        pe.wait_ge(*at("o_scaled", lb, hb, qb))
                    pe.wait_ge(*at("prob", l, sl))
                    e = h % 2
                    if h < MLA_H:
                        v = vm[:, kt, h // 2, 64 * e:64 * e + P]
                    else:
                        v = vg[:, kt, (h - MLA_H) // 3, 64 * e:64 * e + P]
                    if h == 0 and kt == 0:
                        pe.wait_ge(*at("vm", l, TILES - 1, 1))
                        pe.wait_ge(*at("vg", l, TILES - 1, 1))
                    mm = pe.matmul(pv_banks[i % 2][:, 0:nq], v, prob[sl % 4][:, 0:nq], start=(kt == 0),
                                   stop=(kt == nkt - 1))
                    if kt == nkt - 1:
                        mm.then_inc(*up("pv_filled", l, h, q0))
                    else:
                        mm.then_inc(*up("prob_used", l, sl))

                def flush(keep_n):
                    while len(pend) > keep_n:
                        pv(*pend.pop(0))

                tiles = out_tiles(l)
                project_q(0)
                project_k(0)
                gla_a(tiles[0])
                maxes(max_groups(0))
                for t in tiles:
                    if t + 1 < TILES:
                        gla_a(t + 1)
                    gla_o(t)
                    if t - 1 in tiles:
                        gla_t(t - 1)
                values(range(3))
                gla_t(TILES - 1)
                values(range(3, TILES))
                for h in heads:
                    if h + 1 < len(heads):
                        project_q(h + 1)
                        groups = max_groups(h + 1)
                    else:
                        groups = []
                    flush(1)
                    max_rows(h)
                    if h + 1 < len(heads):
                        project_k(h + 1)
                    flush(0)
                    units = [(q0, nq, kt, nk // P) for q0, nq, nk in qbs(l) for kt in range(nk // P)]
                    for j, (q0, nq, kt, nkt) in enumerate(units):
                        if kt == 0:
                            pe.wait_ge(*at("nm_row", l, h, q0))
                            pe.wait_ge(*at("kh_ones", l, 1))
                            if h >= MLA_H:
                                pe.wait_ge(*at("q_both", l, h))
                                pe.wait_ge(*at("q_low", l, h))
                                pe.wait_ge(*at("k_low", l, (h - MLA_H) // 3))
                                pe.wait_ge(*at("k_pad", l, 1, 1))
                        p = open_("sc", l, h, q0, kt)
                        keys, queries = slice(kt * P, kt * P + P), slice(q0, q0 + nq)
                        if h < MLA_H:
                            mm = pe.matmul(p[:, 0:nq], kh[h % 2][0:97, keys], qh[h % 2][0:97, queries],
                                           start=True, stop=True)
                        else:
                            g = (h - MLA_H) // 3
                            pe.matmul(p[:, 0:nq], k_twice[g][:, keys], q_both[h % 2][:, queries], start=True,
                                      stop=False)
                            mm = pe.matmul(p[:, 0:nq], k_low[g][0:97, keys], q_high[h % 2][0:97, queries],
                                           start=False, stop=True)
                        close(mm, "sc", l, h, q0, kt)
                        pend.append((h, q0, nq, kt, nkt, slot[0]))
                        slot[0] += 1
                        m = mod_of_head(l, h)
                        if m and j == MAX_FROM[l] - 2:
                            mod(*m[1:])
                        if m and j == MAX_FROM[l] + (-1 if m[2] < 4 else 1):
                            mod_turn(*m[1:])
                        flush(2)
                        if j >= MAX_FROM[l]:
                            maxes(groups[:2])
                            groups = groups[2:]
                flush(0)
                for n in range(2):
                    i = W_POS[("out", l, n)]

                    def out_products(p, t, ks):
                        for k in ks:
                            pe.wait_ge(*at("y_lo", l, k))
                            pe.wait_ge(*at("w_lo", l, n, k))
                            hi, lo = y_hi[:, k, t * P:(t + 1) * P], y_lo[:, k, t * P:(t + 1) * P]
                            pe.matmul(p[:], hi, w_hi[n][k], start=(k == 0), stop=False)
                            pe.matmul(p[:], hi, w_lo[:, i % 2, k, :], start=False, stop=False)
                            mm = pe.matmul(p[:], lo, w_hi[n][k], start=False, stop=(k == KD - 1))
                        return mm

                    todo = out_tiles(l)
                    if n == 0:
                        ahead = [(t, open_("out", l, t, n)) for t in todo[:4]]
                        for t, p in ahead:
                            out_products(p, t, range(4))
                        for t, p in ahead:
                            close(out_products(p, t, range(4, KD)), "out", l, t, n)
                        todo = todo[4:]
                    for t in todo:
                        close(out_products(open_("out", l, t, n), t, range(KD)), "out", l, t, n)
                    block_done(i)


NAMES = ["x", "c", "ctx", "c_ctx", "norm_w", "w_mod", "b_mod", "w_in", "gla_w_a_fwd", "gla_b_a_fwd",
         "gla_w_a_bwd", "gla_b_a_bwd", "gla_norm_w", "mla_q_norm_w", "mla_w_uq", "mla_kv_norm_w", "mla_w_ukv",
         "gqa_q_norm_w", "gqa_k_norm_w", "w_out", "final_norm_w"]


def constants():
    c = np.zeros((P, C_END), np.float32)
    i = np.arange(P)
    c[:, C_ID:C_ID + P] = np.eye(P)
    c[:, C_BLK:C_BLK + P] = (i[:, None] // 64 == i[None, :] // 64)
    c[:, C_PERM:C_PERM + P] = (i[:, None] == (i[None, :] ^ 16))
    for s in range(2):
        c[s::32, C_SEL + s * P:C_SEL + (s + 1) * P] = 1.0
    same = i[:, None] // CHUNK == i[None, :] // CHUNK
    c[:, C_MF:C_MF + P] = same & (i[:, None] <= i[None, :])
    c[:, C_MB:C_MB + P] = same & (i[:, None] >= i[None, :])
    c[:, C_BD:C_BD + GLA_H] = i[:, None] // GLA_DK == np.arange(GLA_H)[None, :]
    t = np.arange(NL_TOK)
    pos = np.stack([t // 64, t % 64]).astype(np.float32)

    def table(width):
        quarter = width // 4
        f = (np.float32(10000.0) ** (-np.arange(quarter, dtype=np.float32) / np.float32(quarter))).astype(np.float32)
        cos, sin = np.zeros((2, width, NL_TOK), np.float32)
        for d in range(width):
            ang = (pos[d // (width // 2)] * f[d % quarter]).astype(np.float32)
            cos[d] = np.cos(ang)
            sin[d] = np.sin(ang) * (-1.0 if d % (width // 2) < quarter else 1.0)
        return cos, sin

    cos, sin = table(HD)
    c[:, C_COSG:C_COSG + 512] = np.concatenate([cos, cos])
    c[:, C_SING:C_SING + 512] = np.concatenate([sin, sin])
    cos, sin = table(ROPE)
    c[64:96, C_TABM:C_TABM + 512] = cos
    c[96:128, C_TABM:C_TABM + 512] = sin
    return c


def kernel(**inputs):
    import concourse.bacc as bacc
    from concourse.bass_utils import run_bass_kernel_spmd as run

    arrays = {f"in_{n}": np.ascontiguousarray(inputs[n]) for n in NAMES}
    arrays["in_consts"] = constants()

    def trace(tally):
        nc = bacc.Bacc("TRN2", target_bir_lowering=False, num_devices=1)
        aps = {n[3:]: nc.dram_tensor(n, v.shape, mybir.dt.from_np(v.dtype), kind="ExternalInput").ap()
               for n, v in arrays.items()}
        out = nc.dram_tensor("out_0", (1, NL_TOK, D), F32, kind="ExternalOutput").ap()
        build(nc, tally, aps, out)
        return nc

    counted = Tally()
    trace(counted)
    nc = trace(Tally(counted))
    r = run(nc, [arrays], core_ids=[0])
    return r.results[0]["out_0"]
```
